# Optimizing a Trainium2 kernel written in Bass

```python
import jax, jax.numpy as jnp
from jax import lax
import numpy as np

D_MODEL = 1024
BATCH = 1
SEQ = 256
DEPTH = 2

MEM_LEN = 256
BLK = 128
ROPE_THETA = 10000.0
EPS = 1e-6
NEG_INF = -1e30

A_HEADS = 8
A_KV_HEADS = 2
A_HEAD_DIM = 64
A_WINDOW = 128

B_HEADS = 8
B_Q_RANK = 256
B_KV_RANK = 128
B_NOPE = 64
B_ROPE = 32
B_V = 64

M_HEADS = 4
M_HEAD_DIM = 128

D_FF = 3584
N_EXPERTS = 8
TOP_K = 2

N_BRANCHES = 3
BRANCH_WIDTH = 512

IN_SIZES = (A_HEADS * A_HEAD_DIM,
            A_KV_HEADS * A_HEAD_DIM,
            A_KV_HEADS * A_HEAD_DIM,
            B_Q_RANK,
            B_KV_RANK,
            B_ROPE,
            M_HEADS * M_HEAD_DIM,
            N_BRANCHES * D_MODEL)
IN_WIDTH = 512 + 128 + 128 + 256 + 128 + 32 + 512 + 3 * 1024

kernel_name = "hybrid_gated_swa_mla_mem_moe_encoder"

def rms_norm(x, g):
    xf = x.astype(jnp.float32)
    y = xf * lax.rsqrt(jnp.mean(xf * xf, axis=-1, keepdims=True) + EPS)
    return (y * g.astype(jnp.float32)).astype(x.dtype)

def rotary(x, pos):
    d = x.shape[-1]
    half = d // 2
    inv_freq = jnp.power(jnp.float32(ROPE_THETA), -jnp.arange(half, dtype=jnp.float32) * (2.0 / d))
    ang = pos.astype(jnp.float32)[:, :, None, None] * inv_freq
    cos, sin = jnp.cos(ang), jnp.sin(ang)
    xf = x.astype(jnp.float32)
    x1, x2 = xf[..., :half], xf[..., half:]
    return jnp.concatenate([x1 * cos - x2 * sin, x2 * cos + x1 * sin], axis=-1).astype(x.dtype)

def window_gqa(q, k, v, sink):
    b, s_len = q.shape[0], q.shape[1]
    nb = s_len // BLK
    grp = A_HEADS // A_KV_HEADS
    qb = q.reshape(b, nb, BLK, A_KV_HEADS, grp, A_HEAD_DIM)

    def band(t):
        tp = jnp.pad(t, ((0, 0), (BLK, BLK), (0, 0), (0, 0))).reshape(b, nb + 2, BLK, A_KV_HEADS, A_HEAD_DIM)
        return jnp.concatenate([tp[:, :-2], tp[:, 1:-1], tp[:, 2:]], axis=2)

    kw, vw = band(k), band(v)
    rel = jnp.arange(3 * BLK)[None, :] - BLK - jnp.arange(BLK)[:, None]
    k_abs = (jnp.arange(nb)[:, None] - 1) * BLK + jnp.arange(3 * BLK)[None, :]
    mask = (jnp.abs(rel) <= A_WINDOW)[None] & ((k_abs >= 0) & (k_abs < s_len))[:, None, :]
    sc = jnp.einsum('bnqkgd,bnjkd->bkgnqj', qb, kw, preferred_element_type=jnp.float32) * (A_HEAD_DIM ** -0.5)
    sc = jnp.where(mask, sc, NEG_INF)
    sk = sink.astype(jnp.float32).reshape(1, A_KV_HEADS, grp, 1, 1, 1)
    m = jnp.maximum(sc.max(axis=-1, keepdims=True), sk)
    e = jnp.exp(sc - m)
    p = e / (e.sum(axis=-1, keepdims=True) + jnp.exp(sk - m))
    o = jnp.einsum('bkgnqj,bnjkd->bnqkgd', p.astype(v.dtype), vw)
    return o.reshape(b, s_len, A_HEADS * A_HEAD_DIM)

def latent_attention(c_q, c_kv, k_rope_raw, pos, g_q, w_uq, g_kv, w_ukv):
    b, s_len = c_q.shape[0], c_q.shape[1]
    q = (rms_norm(c_q, g_q) @ w_uq).reshape(b, s_len, B_HEADS, B_NOPE + B_ROPE)
    q_nope, q_rope = q[..., :B_NOPE], rotary(q[..., B_NOPE:], pos)
    kv = (rms_norm(c_kv, g_kv) @ w_ukv).reshape(b, s_len, B_HEADS, B_NOPE + B_V)
    k_nope, v = kv[..., :B_NOPE], kv[..., B_NOPE:]
    k_rope = rotary(k_rope_raw[:, :, None, :], pos)[:, :, 0]
    scale = (B_NOPE + B_ROPE) ** -0.5
    nb = s_len // BLK

    def to_blocks(t):
        return jnp.moveaxis(t.reshape(b, nb, BLK, *t.shape[2:]), 1, 0)

    def attend(blk):
        qn, qr = blk
        sc = (jnp.einsum('bqhd,bkhd->bhqk', qn, k_nope, preferred_element_type=jnp.float32)
              + jnp.einsum('bqhd,bkd->bhqk', qr, k_rope, preferred_element_type=jnp.float32)) * scale
        p = jax.nn.softmax(sc, axis=-1)
        return jnp.einsum('bhqk,bkhd->bqhd', p.astype(v.dtype), v)

    o = lax.map(attend, (to_blocks(q_nope), to_blocks(q_rope)))
    return jnp.moveaxis(o, 0, 1).reshape(b, s_len, B_HEADS * B_V)

def memory_attention(q_flat, mem_n, w_kv):
    b, s_len = q_flat.shape[0], q_flat.shape[1]
    n_mem = mem_n.shape[1]
    kv = (mem_n @ w_kv).reshape(b, n_mem, 2, M_HEADS, M_HEAD_DIM)
    k, v = kv[:, :, 0], kv[:, :, 1]
    q = q_flat.reshape(b, s_len, M_HEADS, M_HEAD_DIM)
    sc = jnp.einsum('bqhd,bkhd->bhqk', q, k, preferred_element_type=jnp.float32) * (M_HEAD_DIM ** -0.5)
    p = jax.nn.softmax(sc, axis=-1)
    o = jnp.einsum('bhqk,bkhd->bqhd', p.astype(v.dtype), v)
    return o.reshape(b, s_len, M_HEADS * M_HEAD_DIM)

def swiglu(h, w_gate, w_up, w_down):
    return (jax.nn.silu(h @ w_gate) * (h @ w_up)) @ w_down

def moe_swiglu(h, w_router, w_gate, w_up, w_down):
    b, s_len, d = h.shape
    n_tok = b * s_len
    n_asg = n_tok * TOP_K
    ht = h.reshape(n_tok, d)
    logits = jnp.matmul(ht, w_router, preferred_element_type=jnp.float32)
    top_v, top_i = lax.top_k(logits, TOP_K)
    top_w = jax.nn.softmax(top_v, axis=-1)
    flat_e = top_i.reshape(n_asg)
    flat_tok = jnp.repeat(jnp.arange(n_tok, dtype=jnp.int32), TOP_K)
    flat_w = top_w.reshape(n_asg)
    order = jnp.argsort(flat_e)
    sorted_e = flat_e[order]
    counts = jnp.bincount(flat_e, length=N_EXPERTS)
    padded = (counts + BLK - 1) // BLK * BLK
    start = jnp.cumsum(counts) - counts
    pad_end = jnp.cumsum(padded)
    pad_start = pad_end - padded
    dest = pad_start[sorted_e] + jnp.arange(n_asg) - start[sorted_e]
    n_slots = n_asg + N_EXPERTS * BLK
    n_blk = n_slots // BLK
    tok_buf = jnp.full((n_slots,), n_tok, jnp.int32).at[dest].set(flat_tok[order])
    w_buf = jnp.zeros((n_slots,), jnp.float32).at[dest].set(flat_w[order])
    blk_e = jnp.minimum(jnp.searchsorted(pad_end, jnp.arange(n_blk) * BLK, side='right'), N_EXPERTS - 1)
    h_pad = jnp.concatenate([ht, jnp.zeros((1, d), ht.dtype)], axis=0)

    def expert_block(args):
        tok, wt, e = args
        xb = h_pad[tok]
        y = (jax.nn.silu(xb @ w_gate[e]) * (xb @ w_up[e])) @ w_down[e]
        return y * wt[:, None].astype(h.dtype)

    y = lax.map(expert_block, (tok_buf.reshape(n_blk, BLK), w_buf.reshape(n_blk, BLK), blk_e))
    out = jnp.zeros((n_tok + 1, d), h.dtype).at[tok_buf].add(y.reshape(n_slots, d))
    return out[:n_tok].reshape(b, s_len, d)

def setup_inputs(seed: int = 0) -> dict:
    key = jax.random.key(seed)
    ks = jax.random.split(key, 24)
    n_dense = (DEPTH + 1) // 2
    n_moe = DEPTH // 2

    def w(k, shape, fan_in):
        return jax.random.normal(k, shape, jnp.float32) * (fan_in ** -0.5)

    def gain(k, shape):
        return 1.0 + 0.02 * jax.random.normal(k, shape, jnp.float32)

    x = jax.random.normal(ks[0], (BATCH, SEQ, D_MODEL), jnp.float32)
    mem = jax.random.normal(ks[1], (BATCH, MEM_LEN, D_MODEL), jnp.float32)
    positions = (jax.random.randint(ks[2], (BATCH, 1), 0, SEQ, dtype=jnp.int32)
                 + jnp.arange(SEQ, dtype=jnp.int32)[None, :])
    return {
        "x": x,
        "mem": mem,
        "positions": positions,
        "g_mix": gain(ks[3], (DEPTH, D_MODEL)),
        "w_in": w(ks[4], (DEPTH, D_MODEL, IN_WIDTH), D_MODEL),
        "g_q_lat": gain(ks[5], (DEPTH, B_Q_RANK)),
        "w_uq": w(ks[6], (DEPTH, B_Q_RANK, B_HEADS * (B_NOPE + B_ROPE)), B_Q_RANK),
        "g_kv_lat": gain(ks[7], (DEPTH, B_KV_RANK)),
        "w_ukv": w(ks[8], (DEPTH, B_KV_RANK, B_HEADS * (B_NOPE + B_V)), B_KV_RANK),
        "sink": 0.5 * jax.random.normal(ks[9], (DEPTH, A_HEADS), jnp.float32),
        "w_mem_kv": w(ks[10], (DEPTH, D_MODEL, 2 * M_HEADS * M_HEAD_DIM), D_MODEL),
        "w_branch": w(ks[11], (DEPTH, N_BRANCHES, BRANCH_WIDTH, D_MODEL), BRANCH_WIDTH),
        "w_out": w(ks[12], (DEPTH, D_MODEL, D_MODEL), D_MODEL),
        "g_ffn": gain(ks[13], (DEPTH, D_MODEL)),
        "w_gate_dense": w(ks[14], (n_dense, D_MODEL, D_FF), D_MODEL),
        "w_up_dense": w(ks[15], (n_dense, D_MODEL, D_FF), D_MODEL),
        "w_down_dense": w(ks[16], (n_dense, D_FF, D_MODEL), D_FF),
        "w_router": w(ks[17], (n_moe, D_MODEL, N_EXPERTS), D_MODEL),
        "w_gate_exp": w(ks[18], (n_moe, N_EXPERTS, D_MODEL, D_FF), D_MODEL),
        "w_up_exp": w(ks[19], (n_moe, N_EXPERTS, D_MODEL, D_FF), D_MODEL),
        "w_down_exp": w(ks[20], (n_moe, N_EXPERTS, D_FF, D_MODEL), D_FF),
        "g_mem": gain(ks[21], (D_MODEL,)),
        "g_final": gain(ks[22], (D_MODEL,)),
    }

def reference(x, mem, positions, g_mix, w_in, g_q_lat, w_uq, g_kv_lat, w_ukv, sink, w_mem_kv,
              w_branch, w_out, g_ffn, w_gate_dense, w_up_dense, w_down_dense, w_router,
              w_gate_exp, w_up_exp, w_down_exp, g_mem, g_final):
    b, s_len, _ = x.shape
    mem_n = rms_norm(mem, g_mem)
    split_points = [int(p) for p in np.cumsum(IN_SIZES)[:-1]]
    for l in range(DEPTH):
        h = rms_norm(x, g_mix[l])
        qa, ka, va, cq, ckv, kr, qm, gates = jnp.split(h @ w_in[l], split_points, axis=-1)
        y_a = window_gqa(rotary(qa.reshape(b, s_len, A_HEADS, A_HEAD_DIM), positions),
                         rotary(ka.reshape(b, s_len, A_KV_HEADS, A_HEAD_DIM), positions),
                         va.reshape(b, s_len, A_KV_HEADS, A_HEAD_DIM), sink[l])
        y_b = latent_attention(cq, ckv, kr, positions, g_q_lat[l], w_uq[l], g_kv_lat[l], w_ukv[l])
        y_m = memory_attention(qm, mem_n, w_mem_kv[l])
        g = jax.nn.sigmoid(gates.astype(jnp.float32)).astype(x.dtype).reshape(b, s_len, N_BRANCHES, D_MODEL)
        mixed = (g[:, :, 0] * (y_a @ w_branch[l, 0])
                 + g[:, :, 1] * (y_b @ w_branch[l, 1])
                 + g[:, :, 2] * (y_m @ w_branch[l, 2]))
        x = x + mixed @ w_out[l]
        h = rms_norm(x, g_ffn[l])
        if l % 2 == 0:
            i = l // 2
            x = x + swiglu(h, w_gate_dense[i], w_up_dense[i], w_down_dense[i])
        else:
            i = l // 2
            x = x + moe_swiglu(h, w_router[i], w_gate_exp[i], w_up_exp[i], w_down_exp[i])
    return rms_norm(x, g_final)


_drawn_inputs = setup_inputs


def setup_inputs(seed=0):
    import zlib

    import numpy as np

    out = dict(_drawn_inputs(seed))
    spreads = {}
    factors = {'g_mix': 8.0,
     'g_q_lat': 8.0,
     'g_kv_lat': 3.746,
     'sink': 8.0,
     'g_mem': 8.0,
     'g_final': 7.991,
     'g_ffn': 3.373}
    for name, (base, spread) in spreads.items():
        noise = np.random.default_rng([zlib.crc32(name.encode()), seed]).standard_normal(out[name].shape)
        drawn = base * np.exp(spread * noise) if base else spread * noise
        out[name] = __import__('jax').numpy.asarray(drawn.astype(out[name].dtype))
    for name, factor in factors.items():
        out[name] = (out[name] * factor).astype(out[name].dtype)
    return out
```

```python
from contextlib import ExitStack

import concourse.bass as bass
from concourse import mybir

F32 = mybir.dt.float32
F32R = mybir.dt.float32r
I32 = mybir.dt.int32
U32 = mybir.dt.uint32
ALU = mybir.AluOpType
ACT = mybir.ActivationFunctionType
AX = mybir.AxisListType

P = 128
TOK = 256
NT = TOK // P
D = 1024
KD = D // P
DEPTH = 2
A_HEADS, A_KV, A_DIM = 8, 2, 64
B_HEADS, B_NOPE, B_ROPE, B_V = 8, 64, 32, 64
B_QK = B_NOPE + B_ROPE
Q_RANK, KV_RANK = 256, 128
M_HEADS, M_DIM = 4, 128
D_FF = 3584
FF_GROUP = 512
GROUPS = D_FF // FF_GROUP
EXPERTS = 8
SLOTS = 128
BRANCHES = 3
EPS = 1e-6
MASKED = -1e30
THETA = 10000.0

COL_QA = 0
COL_KVCQ = A_HEADS * A_DIM
COL_CKVKR = COL_KVCQ + 2 * A_KV * A_DIM + Q_RANK
COL_QM = COL_CKVKR + KV_RANK + B_ROPE
COL_GATES = COL_QM + M_HEADS * M_DIM

CHUNK = 1024
RAW = 6
SPLIT = 4
FFN_CHUNKS = 3 * GROUPS * 4
PAIR_CHUNKS = 24
assert FFN_CHUNKS % RAW == 0 and FFN_CHUNKS % SPLIT == 0
assert PAIR_CHUNKS % RAW == 0 and PAIR_CHUNKS % SPLIT == 0

TWO_PI_HI = 6.28125
TWO_PI_MID = 0.0019350051879882812
TWO_PI_LO = 3.01991598196e-07
ROUND = 12582912.0
PI_BELOW = 3.1415925


class Tally:

    def __init__(self):
        self.count = {}
        self.events = {}
        self.body = None

    def add(self, name, key, n=1):
        self.count[name] = self.count.get(name, 0) + n
        self.events[name, key] = [self.count[name], 0, 1]
        if self.body is not None:
            self.body.append((name, key))

    def enter_loop(self):
        self.body, self.start = [], dict(self.count)

    def leave_loop(self, times):
        per = {n: c - self.start.get(n, 0) for n, c in self.count.items()}
        for name, key in self.body:
            self.events[name, key][1:] = per[name], times
        for n, c in per.items():
            self.count[n] += c * (times - 1)
        self.body = None

    def after(self, name, key, it=0):
        base, per, _ = self.events[name, key]
        return base + it * per

    def last(self, name, key):
        base, per, times = self.events[name, key]
        return base + (times - 1) * per

    def before(self, name, key, it=0):
        return self.after(name, key, it) - 1



def mixer_chunks(l):
    return ([("qa", l, c) for c in range(4)] + [("kvcq", l, c) for c in range(4)]
            + [("ckvkr", l, c) for c in range(2)] + [("qm", l, c) for c in range(4)]
            + [("uq", l, c) for c in range(2)] + [("ukv", l, 0)]
            + [("gate", l, g, c) for g in range(6) for c in range(4)]
            + [("branch", l, h, i, c) for h in range(2) for i in range(BRANCHES) for c in range(2)]
            + [("out", l, n, c) for n in range(2) for c in range(4)])


def group_order():
    steps = [("GU", 0)]
    for g in range(1, GROUPS):
        steps += [("GU", g), ("D", g - 1)]
    return steps + [("D", GROUPS - 1)]


def group_chunks(tag, kind, g):
    if kind == "GU":
        return [(tag, "G", g, c) for c in range(4)] + [(tag, "U", g, c) for c in range(4)]
    return [(tag, "D", g, c) for c in range(4)]


def build_tally():
    tl = Tally()
    areas, full_by, free_by, prior, latest = {}, {}, {}, {}, {}

    def psum(key, area, full=None, free=None):
        areas[key] = area
        if full is None:
            full = (f"psum_full{area}", key)
            tl.add(*full)
        if free is None:
            free = (f"psum_free{area}", key)
            tl.add(*free)
        full_by[key], free_by[key] = full, free
        prior[key], latest[area] = latest.get(area), key

    def split(key, area, full=None):
        psum(key, area, full)
        tl.add("hi_copied", key)

    def chunks(keys):
        for key in keys:
            tl.add("chunk", key)
        return "chunk", keys[-1]

    for a in range(2):
        split(("memT", a), a)
    for l in range(DEPTH):
        psum(("memk", l), 2, full=chunks([("memk", l, c) for c in range(4)]))
        psum(("memv", l), 3, full=chunks([("memv", l, c) for c in range(4)]))
    for l in range(DEPTH):
        keys = mixer_chunks(l)
        chunks(keys)
        last = {key[0]: ("chunk", key) for key in keys}
        for a in range(2):
            split(("hT", 2 * l, a), a)
        tl.add("qa_ready", l)
        tl.add("k_ready", l)
        psum(("qa", l), 2, last["qa"], ("qa_ready", l))
        psum(("kvcq", l), 3, last["kvcq"], ("k_ready", l))
        psum(("ckvkr", l), 0, last["ckvkr"], ("k_ready", l))
        psum(("qm", l), 1, last["qm"])
        psum(("T_qa", l), 2)
        split(("T_lat", l), 1)
        split(("T_kv", l), 2)
        for t in range(NT):
            tl.add("qb_copied", (l, t))
            psum(("uq", l, t), (3, 0)[t], last["uq"], ("qb_copied", (l, t)))
        psum(("ukv_k", l, 0), 1)
        psum(("ukv_k", l, 1), 2)
        psum(("ukv_v", l), 3, last["ukv"])
        psum(("T_qb", l, 0), 0)
        psum(("T_qb", l, 1), 1)
        for step in attention_steps():
            for kind, n in step:
                if kind == "QK":
                    a_unit = attention_units()[n][0] == "A"
                    tl.add("exp_done", (l, n), 5 if a_unit else 4)
                    psum(("S", l, n), 0, free=None if a_unit else ("exp_done", (l, n)))
                elif kind == "T":
                    psum(("pT", l, n), 1)
                elif kind == "PV":
                    split(("oT", l, n), 2)
                elif kind == "gate" and n[1] == 3:
                    psum(("gate", l, n[0]), 3, ("chunk", ("gate", l, *n)))
        for h in range(2):
            for i in range(BRANCHES):
                psum(("branch", l, h, i), (h * BRANCHES + i) % 2, ("chunk", ("branch", l, h, i, 1)))
            tl.add("hi_copied", ("mixed", l, h))
        for n in range(2):
            psum(("out", l, n), 2 + n, ("chunk", ("out", l, n, 3)))
        for a in range(2):
            split(("hT", 2 * l + 1, a), a)
        if l == 0:
            def dense_step(kind, g, tag):
                last_chunk = chunks(group_chunks(tag, kind, g))
                if kind == "GU":
                    for name in ("silu_done", "act_ready", "hi_copied", "act_split"):
                        tl.add(name, (tag, g))
                    psum((tag, "G", g), 0, ("chunk", (tag, "G", g, 3)), ("silu_done", (tag, g)))
                    psum((tag, "U", g), 1, last_chunk, ("act_ready", (tag, g)))
                return last_chunk

            dense_step("GU", 0, "dense")
            tl.enter_loop()
            for tag, kind, g in dense_pair():
                dense_step(kind, g, tag)
            tl.leave_loop((GROUPS - 1) // 2)
            last_chunk = dense_step("D", "last", "dense")
            for t in range(NT):
                psum(("down", t), 2 + t, last_chunk)
        else:
            psum(("router",), 2)
            tl.add("turns_ready", "turns")
            psum(("rank",), 3, free=("turns_ready", "turns"))
            tl.enter_loop()
            for key in ("cur", "onehot", "onehot_w"):
                tl.add("routed", key)
            split(("gather",), 3)
            psum(("T_Pw",), 1)
            for kind, g in group_order():
                last_chunk = chunks(group_chunks("moe", kind, g))
                if kind == "GU":
                    tl.add("silu_done", ("moe", g))
                    tl.add("act_ready", ("moe", g))
                    psum(("moe", "GU", g), 0, last_chunk, ("act_ready", ("moe", g)))
                    if g == 0:
                        split(("moe", "T", 0), 1)
                elif g + 1 < GROUPS:
                    split(("moe", "T", g + 1), 1)
                else:
                    psum(("moe", "D"), 2, last_chunk)
            for t in range(NT):
                tl.add("x_added", ("scatter", t))
                psum(("scatter", t), (3, 0)[t], free=("x_added", ("scatter", t)))
            tl.leave_loop(EXPERTS)
    return tl, areas, full_by, free_by, prior


def dense_pair():
    return [("pair", "GU", 1), ("pair", "D", 0), ("pair", "GU", 2), ("pair", "D", 1)]


def attention_units():
    return [("A", j) for j in range(4)] + [("B", j) for j in range(4)] + [("M", j) for j in range(2)]


def y_place(u):
    kind, j = attention_units()[u]
    return {"A": (j, 1), "B": (4 + j, 1), "M": (8 + 2 * j, 2)}[kind]


def attention_steps():
    gates = [(g, c) for g in range(6) for c in range(4)]
    n = len(attention_units())
    steps = []
    for u in range(n + 2):
        step = []
        if u < n:
            step.append(("QK", u))
        if gates:
            step.append(("gate", gates.pop(0)))
        if u >= 2:
            step.append(("PV", u - 2))
        if 1 <= u <= n:
            step.append(("T", u - 1))
        if gates:
            step.append(("gate", gates.pop(0)))
        steps.append(step)
    assert not gates
    return steps


def trunk_kernel(nc, A, inv_freq, out):
    tl, areas, full_by, free_by, prior = build_tally()
    units = attention_units()

    with ExitStack() as ctx:
        def sem(name):
            return ctx.enter_context(nc.semaphore(name))

        def sb_in(scope):
            return lambda name, shape, dt=F32: scope.enter_context(nc.sbuf_tensor(name, shape, dt))

        sb = sb_in(ctx)

        raw = [sb(f"raw{i}", [P, CHUNK]) for i in range(RAW)]
        whi = [sb(f"whi{i}", [P, CHUNK], F32R) for i in range(SPLIT)]
        wlo = [sb(f"wlo{i}", [P, CHUNK], F32R) for i in range(SPLIT)]
        x = sb("x", [P, NT, D])
        gain = sb("gain", [P, D])
        hT_hi = sb("hT_hi", [P, KD, TOK], F32R)
        hT_lo = sb("hT_lo", [P, KD, TOK], F32R)
        kM = sb("kM", [P, DEPTH, M_HEADS, TOK])
        vM = sb("vM", [P, DEPTH, NT, M_HEADS * M_DIM])
        gates = sb("gates", [P, BRANCHES * KD, TOK])
        normed = gates[:, 0:8, :].rearrange("p (t a) n -> p t (a n)", t=NT)
        junk = gates[:, 8:16, :].rearrange("p (t a) n -> p t (a n)", t=NT)
        ident = sb("ident", [P, P])
        mask = sb("mask", [P, NT, TOK])
        freqs = sb("freqs", [P, 48])
        pos_i = sb("pos_i", [P, NT], I32)
        pos_f = sb("pos_f", [P, NT])
        cosA = sb("cosA", [P, NT, A_DIM])
        sinA = sb("sinA", [P, NT, A_DIM])
        cosB = sb("cosB", [P, NT, B_ROPE])
        sinB = sb("sinB", [P, NT, B_ROPE])
        ang = sb("ang", [P, 5, NT, 48])
        sumsq = sb("sumsq", [P, NT])
        meansq = sb("meansq", [P, NT])
        rstd = sb("rstd", [P, NT])
        power = sb("power", [P, 4])
        g_lat = sb("g_lat", [P, DEPTH, Q_RANK + KV_RANK])
        sink = sb("sink", [P, DEPTH, A_HEADS])
        lat_sumsq = sb("lat_sumsq", [P, 2, NT])
        lat_meansq = sb("lat_meansq", [P, 2, NT])
        lat_rstd = sb("lat_rstd", [P, 2, NT])
        row_max = sb("row_max", [P, 4])
        neg_max = sb("neg_max", [P, 4])
        sink_arg = sb("sink_arg", [P, 4])
        sink_exp = sb("sink_exp", [P, 4])
        row_sum = sb("row_sum", [P, 4])
        inv_sum = sb("inv_sum", [P, 4])
        y_hi = sb("y_hi", [P, 12, TOK], F32R)
        y_lo = sb("y_lo", [P, 12, TOK], F32R)

        attn = ExitStack()
        sb = sb_in(attn)
        qaT = sb("qaT", [P, 4, TOK])
        kaT = sb("kaT", [P, A_KV, TOK])
        vA = sb("vA", [P, NT, A_KV * A_DIM])
        cqT_hi = sb("cqT_hi", [P, 2, TOK], F32R)
        cqT_lo = sb("cqT_lo", [P, 2, TOK], F32R)
        ckvT_hi = sb("ckvT_hi", [P, TOK], F32R)
        ckvT_lo = sb("ckvT_lo", [P, TOK], F32R)
        qBT = sb("qBT", [B_QK, B_HEADS, TOK])
        kBT = sb("kBT", [B_QK, B_HEADS, TOK])
        vB = sb("vB", [P, NT, B_HEADS * B_V])
        qMT = sb("qMT", [P, M_HEADS, TOK])
        rows = ExitStack()
        sb = sb_in(rows)
        qa_rot = sb("qa_rot", [P, NT, A_HEADS * A_DIM])
        cq_n = sb("cq_n", [P, NT, Q_RANK])
        kr_pad = sb("kr_pad", [P, NT, B_QK])
        qB = sb("qB", [P, NT, B_HEADS, B_QK])
        rows.close()
        sb = sb_in(attn)
        probs = sb("probs", [P, 2, 2, NT, TOK])
        pT = sb("pT", [P, 2, NT, TOK])
        rot1 = gates[:, 16:18, :].rearrange("p a n -> p (a n)")
        rot2 = gates[:, 18:20, :].rearrange("p a n -> p (a n)")
        k_dup = gates[:, 20:22, :].rearrange("p t (k a n) -> p t k a n", k=A_KV, a=2)
        ckv_n = gates[:, 22, :].rearrange("p (t n) -> p t n", t=NT)
        attn.close()

        mixing = ExitStack()
        sb = sb_in(mixing)
        mixed = sb("mixed", [P, 4, TOK])
        gated = sb("gated", [P, 4, TOK])
        mixT_hi = sb("mixT_hi", [P, KD, TOK], F32R)
        mixT_lo = sb("mixT_lo", [P, KD, TOK], F32R)
        mixing.close()

        ffn = ExitStack()
        sb = sb_in(ffn)
        silu = sb("silu", [P, 4, TOK])
        act = sb("act", [P, 4, TOK])
        actT_hi = [sb(f"actT_hi{i}", [P, 4, TOK], F32R) for i in range(2)]
        actT_lo = [sb(f"actT_lo{i}", [P, 4, TOK], F32R) for i in range(2)]
        zeros = sb("zeros", [1, FF_GROUP])
        ffn.close()

        moe = ExitStack()
        sb = sb_in(moe)
        wr = sb("wr", [P, KD, EXPERTS])
        wr_hi = sb("wr_hi", [P, KD, EXPERTS], F32R)
        wr_lo = sb("wr_lo", [P, KD, EXPERTS], F32R)
        logits = sb("logits", [P, NT, EXPERTS])
        top8 = sb("top8", [P, NT, 8])
        top_i = sb("top_i", [P, NT, 8], U32)
        top_f = sb("top_f", [P, NT, 8])
        pair_e = sb("pair_e", [P, NT])
        pair_d = sb("pair_d", [P, NT])
        pair_w = sb("pair_w", [P, 2, NT])
        hot = sb("hot", [P, 2, NT, EXPERTS])
        routed = sb("routed", [P, NT, EXPERTS])
        route_w = sb("route_w", [P, NT, EXPERTS])
        earlier = sb("earlier", [P, P])
        ones = sb("ones", [P, P])
        iota8 = sb("iota8", [P, EXPERTS])
        iotaS = sb("iotaS", [P, SLOTS])
        route = sb("route", [P, 2 * EXPERTS, 4])
        cur = sb("cur", [P, 4])
        most = sb("most", [P, 1])
        turns_f = sb("turns_f", [P, 1])
        turns_i = sb("turns_i", [P, 1], I32)
        onehot = sb("onehot", [P, NT, SLOTS])
        onehot_w = sb("onehot_w", [P, NT, SLOTS])
        back = sb("back", [P, TOK])
        xg_hi = sb("xg_hi", [P, KD, SLOTS], F32R)
        xg_lo = sb("xg_lo", [P, KD, SLOTS], F32R)
        silu_m = sb("silu_m", [P, FF_GROUP])
        act_m = sb("act_m", [P, FF_GROUP])
        actm_hi = [sb(f"actm_hi{i}", [P, 4, SLOTS], F32R) for i in range(2)]
        actm_lo = [sb(f"actm_lo{i}", [P, 4, SLOTS], F32R) for i in range(2)]
        y_sb = sb("y_sb", [P, D])
        moe.close()

        ps = [ctx.enter_context(nc.psum_tensor(f"ps{a}", [P, CHUNK], F32)) for a in range(4)]

        chunk_loaded = [sem(f"chunk_loaded{i}") for i in range(RAW)]
        chunk_hi = sem("chunk_hi")
        chunk_split = sem("chunk_split")
        chunk_used = sem("chunk_used")
        psum_full = [sem(f"psum_full{a}") for a in range(4)]
        psum_free = [sem(f"psum_free{a}") for a in range(4)]
        hi_copied = sem("hi_copied")
        inputs_loaded = sem("inputs_loaded")
        small_loaded = sem("small_loaded")
        router_loaded = sem("router_loaded")
        gain_loaded = sem("gain_loaded")
        constants = sem("constants")
        routing_constants = sem("routing_constants")
        sumsq_ready = sem("sumsq_ready")
        meansq_ready = sem("meansq_ready")
        rstd_ready = sem("rstd_ready")
        norm_done = sem("norm_done")
        lat_sumsq_ready = sem("lat_sumsq_ready")
        lat_meansq_ready = sem("lat_meansq_ready")
        lat_rstd_ready = sem("lat_rstd_ready")
        angles_ready = sem("angles_ready")
        trig_ready = sem("trig_ready")
        dve_step = sem("dve_step")
        v_copied = sem("v_copied")
        qa_ready = sem("qa_ready")
        k_ready = sem("k_ready")
        qb_copied = sem("qb_copied")
        qb_ready = sem("qb_ready")
        kr_copied = sem("kr_copied")
        max_ready = sem("max_ready")
        exp_done = sem("exp_done")
        probs_ready = sem("probs_ready")
        gates_ready = sem("gates_ready")
        mixed_ready = sem("mixed_ready")
        mixed_split = sem("mixed_split")
        x_added = sem("x_added")
        silu_done = sem("silu_done")
        act_ready = sem("act_ready")
        act_split = sem("act_split")
        zeros_ready = sem("zeros_ready")
        wr_hi_ready = sem("wr_hi_ready")
        wr_split = sem("wr_split")
        diff_ready = sem("diff_ready")
        ratio_ready = sem("ratio_ready")
        masks_ready = sem("masks_ready")
        turns_ready = sem("turns_ready")
        routed_sem = sem("routed_step")
        stored = sem("stored")

        counters = {"chunk": chunk_used, "qa_ready": qa_ready, "k_ready": k_ready, "qb_copied": qb_copied,
                    "exp_done": exp_done, "silu_done": silu_done, "act_ready": act_ready,
                    "turns_ready": turns_ready, "x_added": x_added}
        for a in range(4):
            counters[f"psum_full{a}"], counters[f"psum_free{a}"] = psum_full[a], psum_free[a]

        def wait_full(eng, key, it=0):
            name, event = full_by[key]
            eng.wait_ge(counters[name], tl.after(name, event, it))

        def wait_free(eng, key):
            if prior[key] is not None:
                name, event = free_by[prior[key]]
                eng.wait_ge(counters[name], tl.last(name, event))

        def wait_free_in_loop(eng, key, it):
            a = areas[key]
            eng.wait_ge(psum_free[a], tl.before(f"psum_free{a}", key, it))

        def wait_read(eng, key, it=0):
            name, event = free_by[key]
            eng.wait_ge(counters[name], tl.after(name, event, it))

        def area(key):
            return ps[areas[key]]

        def chunk_no(key, it=0):
            return tl.before("chunk", key, it)

        def slot(key):
            return tl.before("chunk", key)

        w_in = A["w_in"].rearrange("l (k p) n -> l p k n", p=P)
        w_mem = A["w_mem_kv"].rearrange("l (k p) n -> l p k n", p=P)
        w_uq = A["w_uq"].rearrange("l (k p) n -> l p k n", p=P)
        w_branch = A["w_branch"].rearrange("l b (k p) n -> l b p k n", p=P)
        w_out = A["w_out"].rearrange("l (k p) n -> l p k n", p=P)
        dense_w = {"G": A["w_gate_dense"].rearrange("l (k p) n -> l p k n", p=P),
                   "U": A["w_up_dense"].rearrange("l (k p) n -> l p k n", p=P),
                   "D": A["w_down_dense"].rearrange("l (k p) n -> l k p n", p=P)}
        expert_w = {"G": A["w_gate_exp"].rearrange("l e (k p) n -> (l e) p k n", p=P),
                    "U": A["w_up_exp"].rearrange("l e (k p) n -> (l e) p k n", p=P),
                    "D": A["w_down_exp"].rearrange("l e (k p) n -> (l e) k p n", p=P)}

        def chunk_source(key, it=0):
            kind = key[0]
            if kind in ("memk", "memv"):
                _, l, c = key
                n0 = 0 if kind == "memk" else M_HEADS * M_DIM
                return w_mem[l, :, 2 * c:2 * c + 2, n0:n0 + 512]
            if kind in ("qa", "kvcq", "qm"):
                _, l, c = key
                n0 = {"qa": COL_QA, "kvcq": COL_KVCQ, "qm": COL_QM}[kind]
                return w_in[l, :, 2 * c:2 * c + 2, n0:n0 + 512]
            if kind == "ckvkr":
                _, l, c = key
                return w_in[l, :, 4 * c:4 * c + 4, COL_CKVKR:COL_QM]
            if kind == "uq":
                _, l, c = key
                return w_uq[l, :, c, :]
            if kind == "ukv":
                return A["w_ukv"][key[1]]
            if kind == "gate":
                _, l, g, c = key
                n0 = COL_GATES + 512 * g
                return w_in[l, :, 2 * c:2 * c + 2, n0:n0 + 512]
            if kind == "branch":
                _, l, h, i, c = key
                return w_branch[l, i, :, 2 * c:2 * c + 2, 512 * h:512 * h + 512]
            if kind == "out":
                _, l, n, c = key
                return w_out[l, :, 2 * c:2 * c + 2, 512 * n:512 * n + 512]
            _, which, g, c = key
            if kind == "moe":
                w = expert_w[which][it]
                if which == "D":
                    return w[4 * g + c]
                return w[:, 2 * c:2 * c + 2, FF_GROUP * g:FF_GROUP * (g + 1)]
            w = dense_w[which][0]
            if kind == "dense":
                g = GROUPS - 1 if g == "last" else g
                if which == "D":
                    return w[4 * g + c]
                return w[:, 2 * c:2 * c + 2, FF_GROUP * g:FF_GROUP * (g + 1)]
            if which == "D":
                return w[it * 8 + (4 * g + c)]
            return w[:, 2 * c:2 * c + 2, bass.ds(it * (2 * FF_GROUP) + g * FF_GROUP, FF_GROUP)]

        def chunk_view(key, tile):
            kind = key[0]
            if kind == "ckvkr":
                return tile[:, 0:4 * (KV_RANK + B_ROPE)].rearrange("p (k n) -> p k n", k=4)
            if kind == "uq":
                return tile[:, 0:B_HEADS * B_QK]
            if kind == "ukv" or key[1] == "D":
                return tile[:, :]
            return tile[:, :].rearrange("p (k n) -> p k n", k=2)

        def chunk_width(key):
            return {"ckvkr": 4 * (KV_RANK + B_ROPE), "uq": B_HEADS * B_QK}.get(key[0], CHUNK)

        opening = [(k, l, c) for l in range(DEPTH) for k in ("memk", "memv") for c in range(4)]
        dense_first = group_chunks("dense", "GU", 0)
        dense_loop = [c for tag, kind, g in dense_pair() for c in group_chunks(tag, kind, g)]
        dense_last = group_chunks("dense", "D", "last")
        moe_loop = [c for kind, g in group_order() for c in group_chunks("moe", kind, g)]
        DENSE_TURNS = (GROUPS - 1) // 2
        assert len(dense_loop) == PAIR_CHUNKS and len(moe_loop) == FFN_CHUNKS

        block = ctx.enter_context(nc.Block())

        @block.sync
        def _(sp):
            def load(key, it=0, weights_of=None):
                n = slot(key)
                if not isinstance(it, int) or n >= RAW:
                    sp.wait_ge(chunk_split, chunk_no(key, it) - RAW + 1)
                src = chunk_source(key, it if weights_of is None else weights_of)
                sp.dma_start(chunk_view(key, raw[n % RAW]), src).then_inc(chunk_loaded[n % RAW], 16)

            sp.dma_start(normed, A["mem"][0].rearrange("(t p) d -> p t d", p=P)).then_inc(inputs_loaded, 16)
            sp.dma_start(x[:, :, :], A["x"][0].rearrange("(t p) d -> p t d", p=P)).then_inc(inputs_loaded, 16)
            for key in opening + mixer_chunks(0) + dense_first:
                load(key)
            with nc.sync.Fori(0, DENSE_TURNS) as it:
                for key in dense_loop:
                    load(key, it)
            for key in dense_last + mixer_chunks(1):
                load(key)
            with nc.sync.Fori(0, EXPERTS) as e:
                for key in moe_loop:
                    load(key, e)
            sp.wait_ge(turns_ready, 1)
            turns = nc.sync.value_load(turns_i[0:1, 0:1], min_val=EXPERTS, max_val=2 * EXPERTS)
            with nc.sync.If(turns > EXPERTS):
                with nc.sync.Fori(EXPERTS, 2 * EXPERTS) as e:
                    for key in moe_loop:
                        load(key, e, weights_of=e - EXPERTS)
            sp.wait_ge(norm_done, 2 * 6)
            sp.dma_start(out[0].rearrange("(t p) d -> p t d", p=P), normed).then_inc(stored, 16)
            sp.wait_ge(stored, 16)

        @block.gpsimd
        def _(pool):
            def load_gain(n, row):
                if n:
                    pool.wait_ge(norm_done, 2 * n)
                pool.dma_start(gain[:, :], row.partition_broadcast(P)).then_inc(gain_loaded, 16)

            load_gain(0, A["g_mem"])
            for t in range(NT):
                pool.dma_start(pos_i[:, t:t + 1],
                               A["positions"][0, P * t:P * (t + 1)].unsqueeze(1)).then_inc(small_loaded, 16)
            pool.dma_start(freqs[:, :], inv_freq.partition_broadcast(P)).then_inc(small_loaded, 16)
            for l in range(DEPTH):
                pool.dma_start(g_lat[:, l, 0:Q_RANK], A["g_q_lat"][l].partition_broadcast(P)).then_inc(small_loaded, 16)
                pool.dma_start(g_lat[:, l, Q_RANK:], A["g_kv_lat"][l].partition_broadcast(P)).then_inc(small_loaded, 16)
                pool.dma_start(sink[:, l, :], A["sink"][l].partition_broadcast(P)).then_inc(small_loaded, 16)
            nc.gpsimd.memset(ident[:, :], 0.0).then_inc(constants, 1)
            nc.gpsimd.memset(mask[:, :, :], 0.0).then_inc(constants, 1)
            nc.gpsimd.memset(power[:, :], -0.5).then_inc(constants, 1)
            pool.wait_ge(constants, 3)
            nc.gpsimd.affine_select(out=ident[:, :], in_=ident[:, :], compare_op=ALU.not_equal, fill=1.0, base=0,
                                    pattern=[[-1, P]], channel_multiplier=1).then_inc(constants, 1)
            nc.gpsimd.affine_select(out=mask[:, 0, P:], in_=mask[:, 0, P:], compare_op=ALU.is_ge, fill=MASKED,
                                    base=0, pattern=[[-1, P]], channel_multiplier=1).then_inc(constants, 1)
            nc.gpsimd.affine_select(out=mask[:, 1, 0:P], in_=mask[:, 1, 0:P], compare_op=ALU.is_ge, fill=MASKED,
                                    base=0, pattern=[[1, P]], channel_multiplier=-1).then_inc(constants, 1)

            def rstd_of(n):
                pool.wait_ge(meansq_ready, n + 1)
                nc.gpsimd.tensor_tensor(rstd[:, :], meansq[:, :], power[:, 0:NT], ALU.pow).then_inc(rstd_ready, 1)

            rstd_of(0)
            load_gain(1, A["g_mix"][0])
            for l in range(DEPTH):
                rstd_of(2 * l + 1)
                load_gain(2 * l + 2, A["g_ffn"][l])
                pool.wait_ge(chunk_used, tl.after("chunk", ("qa", l, 3)))
                nc.gpsimd.memset(kr_pad[:, :, 0:B_NOPE], 0.0).then_inc(constants, 1)
                pool.wait_ge(lat_meansq_ready, l + 1)
                nc.gpsimd.tensor_tensor(lat_rstd[:, :, :], lat_meansq[:, :, :],
                                        power[:, :].rearrange("p (a t) -> p a t", a=2),
                                        ALU.pow).then_inc(lat_rstd_ready, 1)
                rstd_of(2 * l + 2)
                load_gain(2 * l + 3, A["g_mix"][1] if l == 0 else A["g_final"])
                if l == 0:
                    nc.gpsimd.memset(zeros[:, :], 0.0).then_inc(zeros_ready, 1)
                else:
                    pool.dma_start(wr[:, :, :], A["w_router"][0].rearrange("(k p) e -> p k e", p=P)).then_inc(router_loaded, 16)
                    nc.gpsimd.memset(ones[:, :], 1.0).then_inc(routing_constants, 1)
                    nc.gpsimd.iota(iota8[:, :], pattern=[[1, EXPERTS]], base=0, channel_multiplier=0,
                                   allow_small_or_imprecise_dtypes=True).then_inc(routing_constants, 1)
                    nc.gpsimd.iota(iotaS[:, :], pattern=[[1, SLOTS]], base=0, channel_multiplier=0,
                                   allow_small_or_imprecise_dtypes=True).then_inc(routing_constants, 1)
                    pool.wait_ge(routing_constants, 1)
                    nc.gpsimd.affine_select(out=earlier[:, :], in_=ones[:, :], compare_op=ALU.is_gt, fill=0.0, base=0,
                                            pattern=[[1, P]], channel_multiplier=-1).then_inc(routing_constants, 1)
            rstd_of(5)

        @block.scalar
        def _(eng):
            s = nc.scalar

            def hi_of(key, it=0):
                n = slot(key)
                w = chunk_width(key)
                loaded = 16 * (n // RAW + 1) + it * (16 * (tl.events["chunk", key][1] // RAW))
                eng.wait_ge(chunk_loaded[n % RAW], loaded)
                if not isinstance(it, int) or n >= SPLIT:
                    eng.wait_ge(chunk_used, chunk_no(key, it) - SPLIT + 1)
                s.activation(whi[n % SPLIT][:, 0:w], raw[n % RAW][:, 0:w], ACT.Copy).then_inc(chunk_hi, 1)

            def copy_hi(key, dst, src, it=0):
                wait_full(eng, key, it)
                s.activation(dst, src, ACT.Copy).then_inc(hi_copied, 1)

            def copy_out(key, dst, src, it=0):
                wait_full(eng, key, it)
                a = areas[key]
                s.activation(dst, src, ACT.Copy).then_inc(psum_free[a], 1)

            def squares(n, src):
                for t in range(NT):
                    s.activation(junk[:, t, :], src[:, t, :], ACT.Square, accum_out=sumsq[:, t:t + 1]).then_inc(sumsq_ready, 1)

            def transposed(name):
                for a in range(2):
                    key = name + (a,)
                    copy_hi(key, hT_hi[:, 4 * a:4 * a + 4, :].rearrange("p k n -> p (k n)"), area(key)[:, :])

            eng.wait_ge(inputs_loaded, 32)
            squares(0, normed)
            eng.wait_ge(angles_ready, 2)
            s.activation(ang[:, 3, :, :], ang[:, 0, :, :], ACT.Sin).then_inc(trig_ready, 1)
            s.activation(ang[:, 4, :, :], ang[:, 1, :, :], ACT.Sin).then_inc(trig_ready, 1)
            for key in opening[0:SPLIT]:
                hi_of(key)
            transposed(("memT",))
            pending = opening[SPLIT:] + mixer_chunks(0)[0:2]
            for l in range(DEPTH):
                for key in pending[0:2]:
                    hi_of(key)
                pending = pending[2:]
                copy_out(("memk", l), kM[:, l, :, :].rearrange("p h n -> p (h n)"), area(("memk", l))[:, :])
                for key in pending[0:6]:
                    hi_of(key)
                pending = pending[6:]
            eng.wait_ge(norm_done, 2)
            eng.wait_ge(meansq_ready, 1)
            for l in range(DEPTH):
                todo = mixer_chunks(l)
                done = [2 if l == 0 else 0]

                def ahead(key, more=3):
                    upto = min(len(todo), todo.index(key) + 1 + more)
                    for k in todo[done[0]:upto]:
                        hi_of(k)
                    done[0] = max(done[0], upto)

                ahead(("qa", l, 0))
                if l:
                    for t in range(NT):
                        wait_read(eng, ("down", t))
                squares(2 * l + 1, x)
                transposed(("hT", 2 * l))
                ahead(("kvcq", l, 3))
                key = ("kvcq", l)
                wait_full(eng, key)
                kv = area(key)[:, :].rearrange("p (t n) -> p t n", t=NT)
                s.activation(vA[:, :, :], kv[:, :, 128:256], ACT.Copy).then_inc(v_copied, 1)
                for t in range(NT):
                    s.activation(junk[:, t, 0:Q_RANK], kv[:, t, 256:512], ACT.Square,
                                 accum_out=lat_sumsq[:, 0, t:t + 1]).then_inc(lat_sumsq_ready, 1)
                ahead(("ckvkr", l, 1))
                key = ("ckvkr", l)
                wait_full(eng, key)
                kv = area(key)[:, :].rearrange("p (t n) -> p t n", t=NT)
                for t in range(NT):
                    s.activation(junk[:, t, 512:512 + KV_RANK], kv[:, t, 0:KV_RANK], ACT.Square,
                                 accum_out=lat_sumsq[:, 1, t:t + 1]).then_inc(lat_sumsq_ready, 1)
                ahead(("qm", l, 3))
                copy_out(("qm", l), qMT[:, :, :].rearrange("p h n -> p (h n)"), area(("qm", l))[:, :])
                copy_out(("T_qa", l), qaT[:, :, :].rearrange("p h n -> p (h n)"), area(("T_qa", l))[:, :])
                key = ("T_lat", l)
                copy_hi(key, cqT_hi[:, :, :].rearrange("p k n -> p (k n)"), area(key)[:, 512:1024])
                key = ("T_kv", l)
                copy_hi(key, ckvT_hi[:, :], area(key)[:, 0:TOK])
                s.activation(kBT[B_NOPE:B_QK, :, :],
                             area(key)[B_NOPE:B_QK, 512:512 + TOK].unsqueeze(1).to_broadcast([B_ROPE, B_HEADS, TOK]),
                             ACT.Copy).then_inc(kr_copied, 1)
                ahead(("uq", l, 1))
                for t in range(NT):
                    key = ("uq", l, t)
                    wait_full(eng, key)
                    s.activation(qB[:, t, :, :].rearrange("p (a h) n -> p a (h n)", a=2),
                                 area(key)[:, :].rearrange("p (a n) -> p a n", a=2)[:, :, 0:4 * B_QK],
                                 ACT.Copy).then_inc(qb_copied, 1)
                ahead(("ukv", l, 0))
                for a in range(2):
                    key = ("ukv_k", l, a)
                    copy_out(key, kBT[0:B_NOPE, 4 * a:4 * a + 4, :].rearrange("p h n -> p (h n)"), area(key)[0:B_NOPE, :])
                copy_out(("T_qb", l, 0), qBT[:, 0:4, :].rearrange("p h n -> p (h n)"), area(("T_qb", l, 0))[0:B_QK, :])

                def exps(u):
                    kind, j = units[u]
                    eng.wait_ge(max_ready, l * len(units) + u + 1)
                    if kind == "A":
                        for q in range(4):
                            tile = probs[:, u % 2, q // 2, q % 2, :]
                            s.activation(tile, tile, ACT.Exp, bias=neg_max[:, q:q + 1],
                                         accum_out=row_sum[:, q:q + 1]).then_inc(exp_done, 1)
                        s.activation(sink_exp[:, :], sink_arg[:, :], ACT.Exp).then_inc(exp_done, 1)
                    else:
                        wait_full(eng, ("pT", l, u - 2))
                        scale = (B_QK if kind == "B" else M_DIM) ** -0.5
                        for q in range(4):
                            s.activation(probs[:, u % 2, q // 2, q % 2, :],
                                         area(("S", l, u))[:, TOK * q:TOK * (q + 1)], ACT.Exp,
                                         bias=neg_max[:, q:q + 1], scale=scale,
                                         accum_out=row_sum[:, q:q + 1]).then_inc(exp_done, 1)

                for step in attention_steps():
                    first_gate = True
                    for kind, n in step:
                        if kind == "gate":
                            ahead(("gate", l, *n))
                            if n[1] == 3:
                                g = n[0]
                                copy_out(("gate", l, g), gates[:, 4 * g:4 * g + 4, :].rearrange("p a n -> p (a n)"),
                                         area(("gate", l, g))[:, :])
                            if first_gate and step[0][0] == "QK":
                                exps(step[0][1])
                            first_gate = False
                        elif kind == "T":
                            key = ("pT", l, n)
                            if n >= 1:
                                wait_full(eng, ("oT", l, n - 1))
                            copy_out(key, pT[:, :, :, :].rearrange("p h k n -> p (h k n)"), area(key)[:, :])
                        elif kind == "PV":
                            key = ("oT", l, n)
                            blk, wide = y_place(n)
                            copy_hi(key, y_hi[:, blk:blk + wide, :].rearrange("p b n -> p (b n)"),
                                    area(key)[:, 0:wide * TOK])
                for g in range(6):
                    eng.wait_ge(psum_free[3], tl.after("psum_free3", ("gate", l, g)))
                    part = gates[:, 4 * g:4 * g + 4, :]
                    s.activation(part, part, ACT.Sigmoid).then_inc(gates_ready, 1)
                    ahead(("branch", l, 0, 0, 0), min(g, 3))
                for h in range(2):
                    ahead(("branch", l, h, 2, 1))
                    if l:
                        wait_full(eng, ("branch", l, h, 2))
                    eng.wait_ge(mixed_ready, 2 * l + h + 1)
                    s.activation(mixT_hi[:, 4 * h:4 * h + 4, :], mixed[:, :, :], ACT.Copy).then_inc(hi_copied, 1)
                ahead(("out", l, 1, 3))
                if l == 0:
                    for key in dense_first[0:SPLIT]:
                        hi_of(key)
                wait_read(eng, ("out", l, 1))
                squares(2 * l + 2, x)
                transposed(("hT", 2 * l + 1))

                if l == 0:
                    def dense_silu(tag, g, it=0):
                        wait_full(eng, (tag, "G", g), it)
                        if tag == "pair":
                            eng.wait_ge(act_ready, tl.before("act_ready", (tag, g), it))
                        s.activation(silu[:, :, :], ps[0][:, :].rearrange("p (a n) -> p a n", a=4),
                                     ACT.Silu).then_inc(silu_done, 1)

                    def dense_hi(tag, g, pair, it=0):
                        eng.wait_ge(act_ready, tl.after("act_ready", (tag, g), it))
                        s.activation(actT_hi[pair][:, :, :], act[:, :, :], ACT.Copy).then_inc(hi_copied, 1)

                    for key in dense_first[SPLIT:7]:
                        hi_of(key)
                    dense_silu("dense", 0)
                    hi_of(dense_first[7])
                    dense_hi("dense", 0, 0)
                    with s.Fori(0, DENSE_TURNS) as it:
                        for tag, kind, g in dense_pair():
                            keys = group_chunks(tag, kind, g)
                            if kind == "GU":
                                for key in keys[0:7]:
                                    hi_of(key, it)
                                dense_silu(tag, g, it)
                                hi_of(keys[7], it)
                            else:
                                for key in keys[0:3]:
                                    hi_of(key, it)
                                dense_hi(tag, g + 1, (g + 1) % 2, it)
                                hi_of(keys[3], it)
                    for key in dense_last:
                        hi_of(key)

            eng.wait_ge(router_loaded, 16)
            s.activation(wr_hi[:, :, :], wr[:, :, :], ACT.Copy).then_inc(wr_hi_ready, 1)
            eng.wait_ge(diff_ready, 1)
            s.activation(pair_e[:, :], pair_d[:, :], ACT.Exp).then_inc(ratio_ready, 1)
            eng.wait_ge(turns_ready, 1)
            turns = s.value_load(turns_i[0:1, 0:1], min_val=EXPERTS, max_val=2 * EXPERTS)
            with s.Fori(0, turns) as e:
                for key in moe_loop[0:3]:
                    hi_of(key, e)
                copy_hi(("gather",), xg_hi[:, :, :].rearrange("p k n -> p (k n)"), ps[3][:, :], e)
                todo_m = moe_loop[3:]

                def more(n):
                    for key in todo_m[0:n]:
                        hi_of(key, e)
                    del todo_m[0:n]

                def moe_silu(g):
                    wait_full(eng, ("moe", "GU", g), e)
                    if g:
                        eng.wait_ge(act_ready, tl.after("act_ready", ("moe", g - 1), e))
                    s.activation(silu_m[:, :], ps[0][:, 0:FF_GROUP], ACT.Silu).then_inc(silu_done, 1)

                def moe_hi(g):
                    key = ("moe", "T", g)
                    wait_full(eng, key, e)
                    s.activation(actm_hi[g % 2][:, :, :], ps[1][:, 0:FF_GROUP].rearrange("p (a n) -> p a n", a=4),
                                 ACT.Copy).then_inc(hi_copied, 1)

                more(7)
                moe_silu(0)
                moe_hi(0)
                for g in range(1, GROUPS):
                    more(8)
                    moe_silu(g)
                    more(4)
                    moe_hi(g)
                more(len(todo_m))
                wait_full(eng, ("moe", "D"), e)
                s.activation(y_sb[:, :], ps[2][:, :], ACT.Copy).then_inc(psum_free[2], 1)
            eng.wait_ge(x_added, turns * NT)
            squares(5, x)

        @block.vector
        def _(eng):
            v = nc.vector
            steps = [0]

            def step(ins):
                steps[0] += 1
                ins.then_inc(dve_step, 1)
                eng.wait_ge(dve_step, steps[0])

            def lo_of(key, it=0):
                n = slot(key)
                w = chunk_width(key)
                eng.wait_ge(chunk_hi, chunk_no(key, it) + 1)
                v.tensor_tensor(wlo[n % SPLIT][:, 0:w], raw[n % RAW][:, 0:w], whi[n % SPLIT][:, 0:w].bitcast(F32),
                                ALU.subtract).then_inc(chunk_split, 1)

            def rest(key, lo, src, hi, it=0):
                eng.wait_ge(hi_copied, tl.after("hi_copied", key, it))
                v.tensor_tensor(lo, src, hi.bitcast(F32), ALU.subtract).then_inc(psum_free[areas[key]], 1)

            def norm(n, src, dst):
                eng.wait_ge(sumsq_ready, 2 * (n + 1))
                v.tensor_scalar(meansq[:, :], sumsq[:, :], 1.0 / D, EPS, ALU.mult, ALU.add).then_inc(meansq_ready, 1)
                eng.wait_ge(rstd_ready, n + 1)
                eng.wait_ge(gain_loaded, 16 * (n + 1))
                for t in range(NT):
                    v.scalar_tensor_tensor(dst[:, t, :], src[:, t, :], rstd[:, t:t + 1], gain[:, :],
                                           ALU.mult, ALU.mult).then_inc(norm_done, 1)

            def transposed(name):
                for a in range(2):
                    key = name + (a,)
                    sl = slice(4 * a, 4 * a + 4)
                    rest(key, hT_lo[:, sl, :].rearrange("p k n -> p (k n)"), area(key)[:, :],
                         hT_hi[:, sl, :].rearrange("p k n -> p (k n)"))

            def rotate(src, heads, half, cos, sin, dsts, done=None):
                n = heads * 2 * half
                r1 = rot1[:, 0:n].rearrange("p (h a d) -> p h a d", h=heads, a=2)
                r2 = rot2[:, 0:n].rearrange("p (h a d) -> p h a d", h=heads, a=2)
                c = cos.rearrange("p (a d) -> p a d", a=2)
                sn = sin.rearrange("p (a d) -> p a d", a=2)
                v.tensor_tensor(rot1[:, 0:n].rearrange("p (h n) -> p h n", h=heads),
                                src, cos.unsqueeze(1).to_broadcast([P, heads, 2 * half]), ALU.mult)
                v.tensor_tensor(r2[:, :, 0, :], src[:, :, half:2 * half],
                                sn[:, 0, :].unsqueeze(1).to_broadcast([P, heads, half]), ALU.mult)
                step(v.tensor_tensor(r2[:, :, 1, :], src[:, :, 0:half],
                                     sn[:, 1, :].unsqueeze(1).to_broadcast([P, heads, half]), ALU.mult))
                for dst in dsts:
                    ins = v.tensor_tensor(dst, rot1[:, 0:n].rearrange("p (h n) -> p h n", h=heads),
                                          rot2[:, 0:n].rearrange("p (h n) -> p h n", h=heads), ALU.add)
                    if done is None:
                        step(ins)
                    else:
                        ins.then_inc(*done[0:2])
                        eng.wait_ge(done[0], done[2])

            eng.wait_ge(small_loaded, 16 * (NT + 1 + 3 * DEPTH))
            step(v.tensor_copy(pos_f[:, :], pos_i[:, :]))
            for t in range(NT):
                step(v.tensor_scalar(ang[:, 2, t, :], freqs[:, :], pos_f[:, t:t + 1], None, ALU.mult))
            for out_i, quarter in ((0, 0.0), (1, 0.25)):
                r, k = ang[:, out_i, :, :], ang[:, 3 + out_i, :, :]
                step(v.tensor_scalar(k, ang[:, 2, :, :], 0.15915494309189535, quarter, ALU.mult, ALU.add))
                step(v.tensor_scalar(k, k, ROUND, None, ALU.add))
                step(v.tensor_scalar(k, k, ROUND, None, ALU.subtract))
                step(v.scalar_tensor_tensor(r, k, -TWO_PI_HI, ang[:, 2, :, :], ALU.mult, ALU.add))
                step(v.scalar_tensor_tensor(r, k, -TWO_PI_MID, r, ALU.mult, ALU.add))
                step(v.scalar_tensor_tensor(r, k, -TWO_PI_LO, r, ALU.mult, ALU.add))
                if quarter:
                    step(v.tensor_scalar(r, r, 1.5707963267948966, None, ALU.add))
                step(v.tensor_scalar(k, r, PI_BELOW, -6.283185307179586, ALU.is_gt, ALU.mult))
                step(v.tensor_tensor(r, r, k, ALU.add))
                step(v.tensor_scalar(k, r, -PI_BELOW, 6.283185307179586, ALU.is_lt, ALU.mult))
                step(v.tensor_tensor(r, r, k, ALU.add))
                v.tensor_scalar(r, r, PI_BELOW, -PI_BELOW, ALU.min, ALU.max).then_inc(angles_ready, 1)

            norm(0, normed, normed)
            eng.wait_ge(trig_ready, 2)
            for cos, sin, f0, half in ((cosA, sinA, 0, A_DIM // 2), (cosB, sinB, A_DIM // 2, B_ROPE // 2)):
                v.tensor_copy(cos[:, :, 0:half], ang[:, 4, :, f0:f0 + half])
                v.tensor_copy(cos[:, :, half:], ang[:, 4, :, f0:f0 + half])
                v.tensor_scalar(sin[:, :, 0:half], ang[:, 3, :, f0:f0 + half], -1.0, None, ALU.mult)
                step(v.tensor_copy(sin[:, :, half:], ang[:, 3, :, f0:f0 + half]))
            transposed(("memT",))
            seq = opening + mixer_chunks(0)[0:2]
            for key in seq[0:SPLIT]:
                lo_of(key)
            seq = seq[SPLIT:]
            for l in range(DEPTH):
                for key in seq[0:6]:
                    lo_of(key)
                seq = seq[6:]
                key = ("memv", l)
                wait_full(eng, key)
                v.tensor_copy(vM[:, l, :, :].rearrange("p t n -> p (t n)"), area(key)[:, :]).then_inc(psum_free[3], 1)
                for key in seq[0:2]:
                    lo_of(key)
                seq = seq[2:]
            for l in range(DEPTH):
                todo = mixer_chunks(l)
                done = [2 if l == 0 else 0]

                def ahead(key, more=3):
                    upto = min(len(todo), todo.index(key) + 1 + more)
                    for k in todo[done[0]:upto]:
                        lo_of(k)
                    done[0] = max(done[0], upto)

                if l == 0:
                    wait_full(eng, ("memT", 1))
                ahead(("qa", l, 0))
                norm(2 * l + 1, x, normed)
                transposed(("hT", 2 * l))
                ahead(("qa", l, 3))
                key = ("qa", l)
                wait_full(eng, key)
                for t in range(NT):
                    rotate(area(key)[:, 512 * t:512 * t + 512].rearrange("p (h n) -> p h n", h=A_HEADS), A_HEADS,
                           A_DIM // 2, cosA[:, t, :], sinA[:, t, :],
                           [qa_rot[:, t, :].rearrange("p (h n) -> p h n", h=A_HEADS)],
                           (qa_ready, 1, l + 1) if t == NT - 1 else None)
                ahead(("kvcq", l, 3))
                key = ("kvcq", l)
                eng.wait_ge(lat_sumsq_ready, 4 * l + 2)
                for t in range(NT):
                    rotate(area(key)[:, 512 * t:512 * t + 128].rearrange("p (h n) -> p h n", h=A_KV), A_KV,
                           A_DIM // 2, cosA[:, t, :], sinA[:, t, :],
                           [k_dup[:, t, :, i, :] for i in range(2)])
                ahead(("ckvkr", l, 1))
                wait_full(eng, ("ckvkr", l))
                eng.wait_ge(lat_sumsq_ready, 4 * (l + 1))
                step(v.tensor_scalar(lat_meansq[:, 0, :], lat_sumsq[:, 0, :], 1.0 / Q_RANK, EPS, ALU.mult, ALU.add))
                v.tensor_scalar(lat_meansq[:, 1, :], lat_sumsq[:, 1, :], 1.0 / KV_RANK, EPS, ALU.mult,
                                ALU.add).then_inc(lat_meansq_ready, 1)
                for t in range(NT):
                    rotate(area(("ckvkr", l))[:, 512 * t + KV_RANK:512 * t + KV_RANK + B_ROPE].unsqueeze(1), 1,
                           B_ROPE // 2, cosB[:, t, :], sinB[:, t, :], [kr_pad[:, t, B_NOPE:].unsqueeze(1)])
                eng.wait_ge(lat_rstd_ready, l + 1)
                eng.wait_ge(v_copied, l + 1)
                for t in range(NT):
                    v.scalar_tensor_tensor(cq_n[:, t, :], area(("kvcq", l))[:, 512 * t + 256:512 * t + 512],
                                           lat_rstd[:, 0, t:t + 1], g_lat[:, l, 0:Q_RANK], ALU.mult, ALU.mult)
                v.scalar_tensor_tensor(ckv_n[:, 0, :], area(("ckvkr", l))[:, 0:KV_RANK],
                                       lat_rstd[:, 1, 0:1], g_lat[:, l, Q_RANK:], ALU.mult, ALU.mult)
                v.scalar_tensor_tensor(ckv_n[:, 1, :], area(("ckvkr", l))[:, 512:512 + KV_RANK],
                                       lat_rstd[:, 1, 1:2], g_lat[:, l, Q_RANK:], ALU.mult, ALU.mult).then_inc(k_ready, 1)
                ahead(("qm", l, 3))
                key = ("T_lat", l)
                eng.wait_ge(hi_copied, tl.after("hi_copied", key))
                step(v.tensor_copy(kaT[:, :, :].rearrange("p h n -> p (h n)"), area(key)[:, 0:512]))
                rest(key, cqT_lo[:, :, :].rearrange("p k n -> p (k n)"), area(key)[:, 512:1024],
                     cqT_hi[:, :, :].rearrange("p k n -> p (k n)"))
                key = ("T_kv", l)
                eng.wait_ge(kr_copied, l + 1)
                rest(key, ckvT_lo[:, :], area(key)[:, 0:TOK], ckvT_hi[:, :])
                ahead(("uq", l, 1))
                for t in range(NT):
                    eng.wait_ge(qb_copied, NT * l + t + 1)
                    rotate(qB[:, t, :, B_NOPE:], B_HEADS, B_ROPE // 2, cosB[:, t, :], sinB[:, t, :],
                           [qB[:, t, :, B_NOPE:]], (qb_ready, 1, NT * l + t + 1))
                ahead(("ukv", l, 0))
                key = ("ukv_v", l)
                wait_full(eng, key)
                v.tensor_copy(vB[:, :, :].rearrange("p t n -> p (t n)"), area(key)[:, :]).then_inc(psum_free[3], 1)
                key = ("T_qb", l, 1)
                wait_full(eng, key)
                v.tensor_copy(qBT[:, 4:8, :].rearrange("p h n -> p (h n)"), area(key)[0:B_QK, :]).then_inc(psum_free[1], 1)

                def maxima(u):
                    kind, j = units[u]
                    key = ("S", l, u)
                    wait_full(eng, key)
                    if kind == "A":
                        if u >= 2:
                            wait_full(eng, ("pT", l, u - 2))
                        v.scalar_tensor_tensor(probs[:, u % 2, :, :, :].rearrange("p h t n -> p h (t n)"),
                                               area(key)[:, :].rearrange("p (h n) -> p h n", h=2), A_DIM ** -0.5,
                                               mask[:, :, :].rearrange("p t n -> p (t n)").unsqueeze(1).to_broadcast([P, 2, NT * TOK]),
                                               ALU.mult, ALU.add).then_inc(psum_free[0], 1)
                        wait_read(eng, key)
                        step(v.tensor_reduce(row_max[:, :], probs[:, u % 2, :, :, :].rearrange("p h t n -> p (h t) n"),
                                             AX.X, ALU.max))
                        both = sink[:, l, 2 * j:2 * j + 2].unsqueeze(2).to_broadcast([P, 2, NT])
                        m22 = row_max[:, :].rearrange("p (h t) -> p h t", h=2)
                        step(v.tensor_tensor(m22, m22, both, ALU.max))
                        step(v.tensor_scalar(neg_max[:, :], row_max[:, :], -1.0, None, ALU.mult))
                        v.tensor_tensor(sink_arg[:, :].rearrange("p (h t) -> p h t", h=2),
                                        neg_max[:, :].rearrange("p (h t) -> p h t", h=2), both,
                                        ALU.add).then_inc(max_ready, 1)
                    else:
                        scale = (B_QK if kind == "B" else M_DIM) ** -0.5
                        step(v.tensor_reduce(row_max[:, :], area(key)[:, :].rearrange("p (q n) -> p q n", q=4),
                                             AX.X, ALU.max))
                        v.tensor_scalar(neg_max[:, :], row_max[:, :], -scale, None, ALU.mult).then_inc(max_ready, 1)

                def normalise(u):
                    kind, j = units[u]
                    eng.wait_ge(exp_done, tl.after("exp_done", (l, u)))
                    if kind == "A":
                        step(v.tensor_tensor(row_sum[:, :], row_sum[:, :], sink_exp[:, :], ALU.add))
                    step(v.reciprocal(inv_sum[:, :], row_sum[:, :]))
                    tile = probs[:, u % 2, :, :, :].rearrange("p h t n -> p (h t) n")
                    v.tensor_tensor(tile, tile, inv_sum[:, :].unsqueeze(2).to_broadcast([P, 4, TOK]),
                                    ALU.mult).then_inc(probs_ready, 1)

                for n_step, st in enumerate(attention_steps()):
                    if 1 <= n_step <= len(units):
                        normalise(n_step - 1)
                    for kind, n in st:
                        if kind == "QK":
                            maxima(n)
                        elif kind == "gate":
                            ahead(("gate", l, *n))
                        elif kind == "PV":
                            key = ("oT", l, n)
                            blk, wide = y_place(n)
                            rest(key, y_lo[:, blk:blk + wide, :].rearrange("p b n -> p (b n)"),
                                 area(key)[:, 0:wide * TOK], y_hi[:, blk:blk + wide, :].rearrange("p b n -> p (b n)"))
                for h in range(2):
                    for i in range(BRANCHES):
                        ahead(("branch", l, h, i, 1))
                        key = ("branch", l, h, i)
                        g = 2 * i + h
                        wait_full(eng, key)
                        eng.wait_ge(gates_ready, 6 * l + g + 1)
                        if i == 0 and h:
                            eng.wait_ge(hi_copied, tl.after("hi_copied", ("mixed", l, 0)))
                        dst = mixed if i == 0 else gated
                        v.tensor_tensor(dst[:, :, :], area(key)[:, :].rearrange("p (a n) -> p a n", a=4),
                                        gates[:, 4 * g:4 * g + 4, :], ALU.mult).then_inc(psum_free[areas[key]], 1)
                        wait_read(eng, key)
                        if i == 1:
                            step(v.tensor_tensor(mixed[:, :, :], mixed[:, :, :], gated[:, :, :], ALU.add))
                        if i == 2:
                            v.tensor_tensor(mixed[:, :, :], mixed[:, :, :], gated[:, :, :], ALU.add).then_inc(mixed_ready, 1)
                    eng.wait_ge(hi_copied, tl.after("hi_copied", ("mixed", l, h)))
                    v.tensor_tensor(mixT_lo[:, 4 * h:4 * h + 4, :], mixed[:, :, :],
                                    mixT_hi[:, 4 * h:4 * h + 4, :].bitcast(F32), ALU.subtract).then_inc(mixed_split, 1)
                    if h == 0:
                        eng.wait_ge(mixed_split, 2 * l + 1)
                for n in range(2):
                    ahead(("out", l, n, 3))
                    key = ("out", l, n)
                    wait_full(eng, key)
                    cols = x[:, :, 512 * n:512 * n + 512]
                    v.tensor_tensor(cols, area(key)[:, :].rearrange("p (t n) -> p t n", t=NT), cols,
                                    ALU.add).then_inc(psum_free[areas[key]], 1)
                    wait_read(eng, key)
                if l == 0:
                    for key in dense_first[0:SPLIT]:
                        lo_of(key)
                norm(2 * l + 2, x, normed)
                transposed(("hT", 2 * l + 1))

                if l == 0:
                    def product(tag, g, it=0):
                        wait_full(eng, (tag, "U", g), it)
                        eng.wait_ge(silu_done, tl.after("silu_done", (tag, g), it))
                        v.tensor_tensor(act[:, :, :], ps[1][:, :].rearrange("p (a n) -> p a n", a=4), silu[:, :, :],
                                        ALU.mult).then_inc(act_ready, 1)

                    def act_rest(tag, g, pair, it=0):
                        eng.wait_ge(hi_copied, tl.after("hi_copied", (tag, g), it))
                        v.tensor_tensor(actT_lo[pair][:, :, :], act[:, :, :], actT_hi[pair][:, :, :].bitcast(F32),
                                        ALU.subtract).then_inc(act_split, 1)

                    for key in dense_first[SPLIT:]:
                        lo_of(key)
                    product("dense", 0)
                    act_rest("dense", 0, 0)
                    with v.Fori(0, DENSE_TURNS) as it:
                        for tag, kind, g in dense_pair():
                            keys = group_chunks(tag, kind, g)
                            if kind == "GU":
                                for key in keys:
                                    lo_of(key, it)
                            else:
                                for key in keys[0:3]:
                                    lo_of(key, it)
                                eng.wait_ge(act_split, tl.before("act_split", (tag, g + 1), it))
                                product(tag, g + 1, it)
                                act_rest(tag, g + 1, (g + 1) % 2, it)
                                lo_of(keys[3], it)
                    for key in dense_last:
                        lo_of(key)
                    for t in range(NT):
                        wait_full(eng, ("down", t))
                        v.tensor_tensor(x[:, t, :], ps[2 + t][:, :], x[:, t, :], ALU.add).then_inc(psum_free[2 + t], 1)
                        wait_read(eng, ("down", t))

            eng.wait_ge(wr_hi_ready, 1)
            v.tensor_tensor(wr_lo[:, :, :], wr[:, :, :], wr_hi[:, :, :].bitcast(F32), ALU.subtract).then_inc(wr_split, 1)
            wait_full(eng, ("router",))
            eng.wait_ge(routing_constants, 4)
            v.tensor_copy(logits[:, :, :], ps[2][:, :].rearrange("p (t n) -> p t n", t=NT)[:, :, 0:EXPERTS]).then_inc(psum_free[2], 1)
            wait_read(eng, ("router",))
            for t in range(NT):
                step(v.max(top8[:, t, :], logits[:, t, :]))
                step(v.max_index(top_i[:, t, :], top8[:, t, :], logits[:, t, :]))
            step(v.tensor_copy(top_f[:, :, :], top_i[:, :, :]))
            v.tensor_tensor(pair_d[:, :], top8[:, :, 1], top8[:, :, 0], ALU.subtract).then_inc(diff_ready, 1)
            for r in range(2):
                for t in range(NT):
                    step(v.tensor_scalar(hot[:, r, t, :], iota8[:, :], top_f[:, t, r:r + 1], None, ALU.is_equal))
            v.tensor_tensor(routed[:, :, :], hot[:, 0, :, :], hot[:, 1, :, :], ALU.add).then_inc(masks_ready, 1)
            eng.wait_ge(ratio_ready, 1)
            step(v.tensor_scalar(pair_d[:, :], pair_e[:, :], 1.0, None, ALU.add))
            step(v.reciprocal(pair_w[:, 0, :], pair_d[:, :]))
            step(v.tensor_tensor(pair_w[:, 1, :], pair_w[:, 0, :], pair_e[:, :], ALU.mult))
            for t in range(NT):
                step(v.tensor_scalar(route_w[:, t, :], hot[:, 0, t, :], pair_w[:, 0, t:t + 1], None, ALU.mult))
                step(v.scalar_tensor_tensor(route_w[:, t, :], hot[:, 1, t, :], pair_w[:, 1, t:t + 1], route_w[:, t, :],
                                            ALU.mult, ALU.add))
            wait_full(eng, ("rank",))
            for t in range(NT):
                step(v.tensor_scalar(logits[:, t, :], ps[3][:, EXPERTS * t:EXPERTS * (t + 1)], 1.0, None, ALU.add))
                step(v.tensor_tensor(logits[:, t, :], logits[:, t, :], routed[:, t, :], ALU.mult))
                for turn in range(2):
                    part = route[:, EXPERTS * turn:EXPERTS * (turn + 1), :]
                    step(v.tensor_scalar(part[:, :, t], logits[:, t, :], float(1 + SLOTS * turn), None, ALU.subtract))
                    step(v.tensor_copy(part[:, :, 2 + t], route_w[:, t, :]))
            step(v.tensor_reduce(most[:, :], ps[3][:, NT * EXPERTS:(NT + 1) * EXPERTS], AX.X, ALU.max))
            step(v.tensor_scalar(turns_f[:, :], most[:, :], SLOTS + 0.5, float(EXPERTS), ALU.is_gt, ALU.mult))
            step(v.tensor_scalar(turns_f[:, :], turns_f[:, :], float(EXPERTS), None, ALU.add))
            v.tensor_copy(turns_i[:, :], turns_f[:, :]).then_inc(turns_ready, 1)
            eng.wait_ge(turns_ready, 1)
            turns = v.value_load(turns_i[0:1, 0:1], min_val=EXPERTS, max_val=2 * EXPERTS)

            with v.Fori(0, turns) as e:
                def routed_wait(key):
                    eng.wait_ge(routed_sem, tl.after("routed", key, e))

                v.tensor_copy(cur[:, :], route[:, bass.ds(e, 1), :].rearrange("p a b -> p (a b)")).then_inc(routed_sem, 1)
                routed_wait("cur")
                for t in range(NT):
                    ins = v.tensor_scalar(onehot[:, t, :], iotaS[:, :], cur[:, t:t + 1], None, ALU.is_equal)
                ins.then_inc(routed_sem, 1)
                for t in range(NT):
                    ins = v.tensor_scalar(onehot_w[:, t, :], iotaS[:, :], cur[:, t:t + 1], cur[:, 2 + t:3 + t],
                                          ALU.is_equal, ALU.mult)
                ins.then_inc(routed_sem, 1)
                for key in moe_loop[0:2]:
                    lo_of(key, e)
                rest(("gather",), xg_lo[:, :, :].rearrange("p k n -> p (k n)"), ps[3][:, :],
                     xg_hi[:, :, :].rearrange("p k n -> p (k n)"), e)
                wait_full(eng, ("T_Pw",), e)
                v.tensor_copy(back[:, :], ps[1][:, 0:TOK]).then_inc(psum_free[1], 1)
                todo_m = moe_loop[2:]

                def more(n):
                    for key in todo_m[0:n]:
                        lo_of(key, e)
                    del todo_m[0:n]

                def moe_product(g):
                    eng.wait_ge(silu_done, tl.after("silu_done", ("moe", g), e))
                    if g:
                        wait_full(eng, ("moe", "T", g - 1), e)
                    v.tensor_tensor(act_m[:, :], ps[0][:, FF_GROUP:], silu_m[:, :], ALU.mult).then_inc(act_ready, 1)

                def moe_rest(g):
                    rest(("moe", "T", g), actm_lo[g % 2][:, :, :],
                         ps[1][:, 0:FF_GROUP].rearrange("p (a n) -> p a n", a=4), actm_hi[g % 2][:, :, :], e)

                more(8)
                moe_product(0)
                moe_rest(0)
                for g in range(1, GROUPS):
                    more(8)
                    moe_product(g)
                    more(4)
                    moe_rest(g)
                more(len(todo_m))
                for t in range(NT):
                    key = ("scatter", t)
                    wait_full(eng, key, e)
                    v.tensor_tensor(x[:, t, :], area(key)[:, :], x[:, t, :], ALU.add).then_inc(x_added, 1)

            norm(5, x, normed)

        @block.tensor
        def _(pe):
            mm = nc.tensor.matmul

            def three(o, w_hi, w_lo, a_hi, a_lo, start, stop, stationary):
                for i, (w, a) in enumerate(((w_hi, a_hi), (w_hi, a_lo), (w_lo, a_hi))):
                    lhsT, rhs = (w, a) if stationary else (a, w)
                    ins = mm(o, lhsT, rhs, start=start and i == 0, stop=stop and i == 2, skip_group_check=True)
                return ins

            def wait_chunk(key, it=0):
                pe.wait_ge(chunk_split, chunk_no(key, it) + 1)
                n = slot(key) % SPLIT
                return whi[n], wlo[n]

            def stationary_chunk(key, a_hi, a_lo, out, first, last, it=0):
                hi, lo = wait_chunk(key, it)
                for kk in range(2):
                    for j in range(4):
                        w = slice(512 * kk + P * j, 512 * kk + P * (j + 1))
                        ins = three(out[:, TOK * j:TOK * (j + 1)], hi[:, w], lo[:, w], a_hi(kk), a_lo(kk),
                                    first and kk == 0 and j % 2 == 0, last and kk == 1, True)
                return ins

            def moving_chunk(key, a_hi, a_lo, outs, blocks, width, first, last, it=0):
                hi, lo = wait_chunk(key, it)
                for kk in range(blocks):
                    w = slice(width * kk, width * (kk + 1))
                    for t, o in enumerate(outs):
                        ins = three(o, hi[:, w], lo[:, w], a_hi(kk, t), a_lo(kk, t),
                                    first and kk == 0, last and kk == blocks - 1, False)
                return ins

            def used(ins):
                ins.then_inc(chunk_used, 1)

            def h_at(k):
                return lambda kk: hT_hi[:, k + kk, :], lambda kk: hT_lo[:, k + kk, :]

            def h_tile(k):
                return (lambda kk, t: hT_hi[:, k + kk, P * t:P * (t + 1)],
                        lambda kk, t: hT_lo[:, k + kk, P * t:P * (t + 1)])

            def banks(key, width):
                return [area(key)[:, 512 * t:512 * t + width] for t in range(NT)]

            def transposes(name):
                for a in range(2):
                    key = name + (a,)
                    wait_free(pe, key)
                    for k in range(4):
                        for t in range(NT):
                            c = TOK * k + P * t
                            ins = nc.tensor.transpose(area(key)[:, c:c + P], normed[:, t, P * (4 * a + k):P * (4 * a + k + 1)], ident[:, :])
                    ins.then_inc(psum_full[areas[key]], 1)

            def stationary_section(keys, full_key, act_of):
                wait_free(pe, full_key)
                for i, key in enumerate(keys):
                    used(stationary_chunk(key, *act_of(i), area(full_key), i == 0, i == len(keys) - 1))

            def moving_section(keys, full_key, width, blocks, act_of):
                wait_free(pe, full_key)
                for i, key in enumerate(keys):
                    used(moving_chunk(key, *act_of(i), banks(full_key, width), blocks, width, i == 0, i == len(keys) - 1))

            pe.wait_ge(constants, 6)
            pe.wait_ge(norm_done, 2)
            transposes(("memT",))
            wait_read(pe, ("memT", 1))
            for l in range(DEPTH):
                stationary_section([("memk", l, c) for c in range(4)], ("memk", l), lambda i: h_at(2 * i))
                moving_section([("memv", l, c) for c in range(4)], ("memv", l), 512, 2, lambda i: h_tile(2 * i))

            for l in range(DEPTH):
                pe.wait_ge(norm_done, 2 * (2 * l + 2))
                transposes(("hT", 2 * l))
                wait_read(pe, ("hT", 2 * l, 1))
                moving_section([("qa", l, c) for c in range(4)], ("qa", l), 512, 2, lambda i: h_tile(2 * i))
                moving_section([("kvcq", l, c) for c in range(4)], ("kvcq", l), 512, 2, lambda i: h_tile(2 * i))
                moving_section([("ckvkr", l, c) for c in range(2)], ("ckvkr", l), KV_RANK + B_ROPE, 4, lambda i: h_tile(4 * i))
                stationary_section([("qm", l, c) for c in range(4)], ("qm", l), lambda i: h_at(2 * i))
                key = ("T_qa", l)
                wait_free(pe, key)
                for j in range(4):
                    for t in range(NT):
                        ins = nc.tensor.transpose(area(key)[:, TOK * j + P * t:TOK * j + P * (t + 1)],
                                                  qa_rot[:, t, P * j:P * (j + 1)], ident[:, :])
                ins.then_inc(psum_full[areas[key]], 1)
                wait_read(pe, ("kvcq", l))
                wait_read(pe, ("ckvkr", l))
                key = ("T_lat", l)
                wait_free(pe, key)
                for kv in range(A_KV):
                    for t in range(NT):
                        nc.tensor.transpose(area(key)[:, TOK * kv + P * t:TOK * kv + P * (t + 1)],
                                            k_dup[:, t, kv, :, :].rearrange("p a n -> p (a n)"), ident[:, :])
                for k in range(2):
                    for t in range(NT):
                        c = 512 + TOK * k + P * t
                        ins = nc.tensor.transpose(area(key)[:, c:c + P], cq_n[:, t, P * k:P * (k + 1)], ident[:, :])
                ins.then_inc(psum_full[areas[key]], 1)
                key = ("T_kv", l)
                wait_free(pe, key)
                pe.wait_ge(constants, 6 + l + 1)
                for t in range(NT):
                    nc.tensor.transpose(area(key)[:, P * t:P * (t + 1)], ckv_n[:, t, :], ident[:, :])
                for t in range(NT):
                    ins = nc.tensor.transpose(area(key)[0:B_QK, 512 + P * t:512 + P * (t + 1)], kr_pad[:, t, :], ident[:, :])
                ins.then_inc(psum_full[areas[key]], 1)
                wait_read(pe, ("T_lat", l))
                for t in range(NT):
                    wait_free(pe, ("uq", l, t))
                for k in range(2):
                    hi, lo = wait_chunk(("uq", l, k))
                    for t in range(NT):
                        for half in range(2):
                            w = slice(4 * B_QK * half, 4 * B_QK * (half + 1))
                            ins = three(area(("uq", l, t))[:, 512 * half:512 * half + 4 * B_QK], hi[:, w], lo[:, w],
                                        cqT_hi[:, k, P * t:P * (t + 1)], cqT_lo[:, k, P * t:P * (t + 1)], k == 0, k == 1, False)
                    used(ins)
                hi, lo = wait_chunk(("ukv", l, 0))
                wait_read(pe, ("T_kv", l))
                for a in range(2):
                    key = ("ukv_k", l, a)
                    wait_free(pe, key)
                    for j in range(4):
                        w = slice(P * (4 * a + j), P * (4 * a + j + 1))
                        ins = three(area(key)[:, TOK * j:TOK * (j + 1)], hi[:, w], lo[:, w], ckvT_hi[:, :], ckvT_lo[:, :],
                                    True, True, True)
                    ins.then_inc(psum_full[areas[key]], 1)
                key = ("ukv_v", l)
                wait_free(pe, key)
                values = [w[:, :].rearrange("p (h n) -> p h n", h=B_HEADS)[:, :, B_NOPE:] for w in (hi, lo)]
                for t in range(NT):
                    ins = three(area(key)[:, 512 * t:512 * (t + 1)].rearrange("p (h n) -> p h n", h=B_HEADS), *values,
                                ckvT_hi[:, P * t:P * (t + 1)], ckvT_lo[:, P * t:P * (t + 1)], True, True, False)
                used(ins)
                for a in range(2):
                    key = ("T_qb", l, a)
                    wait_free(pe, key)
                    pe.wait_ge(qb_ready, NT * (l + 1))
                    for j in range(4):
                        for t in range(NT):
                            c = TOK * j + P * t
                            ins = nc.tensor.transpose(area(key)[0:B_QK, c:c + P], qB[:, t, 4 * a + j, :], ident[:, :])
                    ins.then_inc(psum_full[areas[key]], 1)

                def scores(u):
                    kind, j = units[u]
                    key = ("S", l, u)
                    wait_free(pe, key)
                    if u == 0:
                        for k in (("T_qa", l), ("T_lat", l), ("T_qb", l, 0), ("T_qb", l, 1), ("ukv_k", l, 0),
                                  ("ukv_k", l, 1), ("ukv_v", l), ("qm", l)):
                            wait_read(pe, k)
                    for h in range(2):
                        head = 2 * j + h
                        for t in range(NT):
                            o = area(key)[:, TOK * (NT * h + t):TOK * (NT * h + t + 1)]
                            tt = slice(P * t, P * (t + 1))
                            if kind == "A":
                                r = slice(A_DIM * h, A_DIM * (h + 1))
                                ins = mm(o, qaT[r, j, tt], kaT[r, j // 2, :], start=True, stop=True)
                            elif kind == "B":
                                ins = mm(o, qBT[:, head, tt], kBT[:, head, :], start=True, stop=True)
                            else:
                                ins = mm(o, qMT[:, head, tt], kM[:, l, head, :], start=True, stop=True)
                    ins.then_inc(psum_full[0], 1)

                def turn(u):
                    key = ("pT", l, u)
                    pe.wait_ge(probs_ready, l * len(units) + u + 1)
                    wait_free(pe, key)
                    for h in range(2):
                        for kt in range(NT):
                            for t in range(NT):
                                c = TOK * (NT * h + kt) + P * t
                                ins = nc.tensor.transpose(area(key)[:, c:c + P], probs[:, u % 2, h, t, P * kt:P * (kt + 1)], ident[:, :])
                    ins.then_inc(psum_full[1], 1)

                def values_of(u):
                    kind, j = units[u]
                    key = ("oT", l, u)
                    wait_free(pe, key)
                    wait_read(pe, ("pT", l, u))
                    for h in range(2):
                        head = 2 * j + h
                        for kt in range(NT):
                            if kind == "M":
                                o, lhsT = area(key)[:, TOK * h:TOK * (h + 1)], vM[:, l, kt, M_DIM * head:M_DIM * (head + 1)]
                            else:
                                o = area(key)[64 * h:64 * (h + 1), 0:TOK]
                                c = A_DIM * (j // 2) if kind == "A" else B_V * head
                                lhsT = (vA if kind == "A" else vB)[:, kt, c:c + 64]
                            ins = mm(o, lhsT, pT[:, h, kt, :], start=kt == 0, stop=kt == NT - 1)
                    ins.then_inc(psum_full[2], 1)

                for step in attention_steps():
                    for kind, n in step:
                        if kind == "QK":
                            scores(n)
                        elif kind == "PV":
                            values_of(n)
                        elif kind == "T":
                            turn(n)
                        else:
                            g, c = n
                            key = ("gate", l, g)
                            if c == 0:
                                wait_free(pe, key)
                            used(stationary_chunk(("gate", l, g, c), *h_at(2 * c), area(key), c == 0, c == 3))

                for h in range(2):
                    for i in range(BRANCHES):
                        wait_read(pe, ("oT", l, len(units) - 1))
                        stationary_section([("branch", l, h, i, c) for c in range(2)], ("branch", l, h, i),
                                           lambda c: (lambda kk: y_hi[:, 4 * i + 2 * c + kk, :],
                                                      lambda kk: y_lo[:, 4 * i + 2 * c + kk, :]))
                pe.wait_ge(mixed_split, 2 * (l + 1))
                for n in range(2):
                    moving_section([("out", l, n, c) for c in range(4)], ("out", l, n), 512, 2,
                                   lambda i: (lambda kk, t: mixT_hi[:, 2 * i + kk, P * t:P * (t + 1)],
                                              lambda kk, t: mixT_lo[:, 2 * i + kk, P * t:P * (t + 1)]))
                pe.wait_ge(norm_done, 2 * (2 * l + 3))
                transposes(("hT", 2 * l + 1))
                wait_read(pe, ("hT", 2 * l + 1, 1))

                if l == 0:
                    pe.wait_ge(zeros_ready, 1)
                    for t in range(NT):
                        wait_free(pe, ("down", t))
                        for half in range(2):
                            mm(ps[2 + t][:, 512 * half:512 * (half + 1)], zeros[0:1, 0:P], zeros[0:1, :], start=True,
                               stop=False, skip_group_check=True)

                    def up(tag, g, it=0):
                        for which, a, freed, name in (("G", 0, silu_done, "silu_done"), ("U", 1, act_ready, "act_ready")):
                            if tag == "dense":
                                wait_free(pe, (tag, which, g))
                            else:
                                pe.wait_ge(freed, tl.before(name, (tag, g), it))
                            for c in range(4):
                                used(stationary_chunk((tag, which, g, c), *h_at(2 * c), ps[a], c == 0, c == 3, it))

                    def down(tag, g, pair, splits, it=0):
                        pe.wait_ge(act_split, splits)
                        for j in range(4):
                            hi, lo = wait_chunk((tag, "D", g, j), it)
                            for t in range(NT):
                                for half in range(2):
                                    w = slice(512 * half, 512 * (half + 1))
                                    ins = three(ps[2 + t][:, w], hi[:, w], lo[:, w],
                                                actT_hi[pair][:, j, P * t:P * (t + 1)], actT_lo[pair][:, j, P * t:P * (t + 1)],
                                                False, g == "last" and j == 3, False)
                            used(ins)

                    up("dense", 0)
                    with nc.tensor.Fori(0, DENSE_TURNS) as it:
                        for tag, kind, g in dense_pair():
                            if kind == "GU":
                                up(tag, g, it)
                            else:
                                down(tag, g, g % 2, it * 2 + (g + 1), it)
                    down("dense", "last", (GROUPS - 1) % 2, GROUPS)

            pe.wait_ge(wr_split, 1)
            wait_free(pe, ("router",))
            for t in range(NT):
                for k in range(KD):
                    ins = three(ps[2][:, 512 * t:512 * t + EXPERTS], wr_hi[:, k, :], wr_lo[:, k, :],
                                hT_hi[:, k, P * t:P * (t + 1)], hT_lo[:, k, P * t:P * (t + 1)], k == 0, k == KD - 1, False)
            ins.then_inc(psum_full[2], 1)
            pe.wait_ge(masks_ready, 1)
            wait_free(pe, ("rank",))
            mm(ps[3][:, 0:8], earlier[:, :], routed[:, 0, :], start=True, stop=True)
            mm(ps[3][:, 8:16], ones[:, :], routed[:, 0, :], start=True, stop=False)
            mm(ps[3][:, 8:16], earlier[:, :], routed[:, 1, :], start=False, stop=True)
            mm(ps[3][:, 16:24], ones[:, :], routed[:, 0, :], start=True, stop=False)
            mm(ps[3][:, 16:24], ones[:, :], routed[:, 1, :], start=False, stop=True).then_inc(psum_full[3], 1)
            pe.wait_ge(turns_ready, 1)
            turns = nc.tensor.value_load(turns_i[0:1, 0:1], min_val=EXPERTS, max_val=2 * EXPERTS)

            with nc.tensor.Fori(0, turns) as e:
                pe.wait_ge(routed_sem, tl.after("routed", "onehot_w", e))
                for k in range(KD):
                    for t in range(NT):
                        ins = mm(ps[3][:, SLOTS * k:SLOTS * (k + 1)], normed[:, t, P * k:P * (k + 1)], onehot[:, t, :],
                                 start=t == 0, stop=t == NT - 1)
                ins.then_inc(psum_full[3], 1)
                wait_free_in_loop(pe, ("T_Pw",), e)
                for t in range(NT):
                    ins = nc.tensor.transpose(ps[1][:, P * t:P * (t + 1)], onehot_w[:, t, :], ident[:, :])
                ins.then_inc(psum_full[1], 1)
                wait_read(pe, ("gather",), e)

                def transposed_act(g):
                    key = ("moe", "T", g)
                    pe.wait_ge(act_ready, tl.after("act_ready", ("moe", g), e))
                    wait_free_in_loop(pe, key, e)
                    for j in range(4):
                        ins = nc.tensor.transpose(ps[1][:, P * j:P * (j + 1)], act_m[:, P * j:P * (j + 1)], ident[:, :])
                    ins.then_inc(psum_full[1], 1)

                for kind, g in group_order():
                    if kind == "GU":
                        if g:
                            pe.wait_ge(act_ready, tl.after("act_ready", ("moe", g - 1), e))
                        for which in "GU":
                            o = ps[0][:, 0:FF_GROUP] if which == "G" else ps[0][:, FF_GROUP:]
                            for c in range(4):
                                ins = moving_chunk(("moe", which, g, c), lambda kk, t: xg_hi[:, 2 * c + kk, :],
                                                   lambda kk, t: xg_lo[:, 2 * c + kk, :], [o], 2, 512, c == 0, c == 3, e)
                                used(ins)
                    else:
                        wait_read(pe, ("moe", "T", g), e)
                        if g == 0:
                            wait_free_in_loop(pe, ("moe", "D"), e)
                        for j in range(4):
                            hi, lo = wait_chunk(("moe", "D", g, j), e)
                            for half in range(2):
                                w = slice(512 * half, 512 * (half + 1))
                                ins = three(ps[2][:, w], hi[:, w], lo[:, w], actm_hi[g % 2][:, j, :],
                                            actm_lo[g % 2][:, j, :], g == 0 and j == 0, g == GROUPS - 1 and j == 3, False)
                            used(ins)
                    if (kind, g) == ("GU", 0):
                        transposed_act(0)
                    elif kind == "D" and g + 1 < GROUPS:
                        transposed_act(g + 1)
                wait_read(pe, ("moe", "D"), e)
                for t in range(NT):
                    for half in range(2):
                        w = slice(512 * half, 512 * (half + 1))
                        ins = mm(area(("scatter", t))[:, w], back[:, P * t:P * (t + 1)], y_sb[:, w], start=True, stop=True)
                    ins.then_inc(psum_full[areas["scatter", t]], 1)


INPUTS = ["x", "mem", "positions", "g_mix", "w_in", "g_q_lat", "w_uq", "g_kv_lat", "w_ukv", "sink", "w_mem_kv",
          "w_branch", "w_out", "g_ffn", "w_gate_dense", "w_up_dense", "w_down_dense", "w_router", "w_gate_exp",
          "w_up_exp", "w_down_exp", "g_mem", "g_final"]


def kernel(**inputs):
    import numpy as np
    import concourse.bacc as bacc
    from concourse.bass_utils import run_bass_kernel_spmd

    nc = bacc.Bacc("TRN2", target_bir_lowering=False, num_devices=1)
    arrays, args = {}, {}
    freqs = []
    for dim in (A_DIM, B_ROPE):
        exponent = -np.arange(dim // 2, dtype=np.float32) * np.float32(2.0 / dim)
        freqs.append(np.power(np.float64(THETA), exponent.astype(np.float64)).astype(np.float32))
    arrays["inv_freq"] = np.concatenate(freqs)
    for name in INPUTS:
        arrays["in_" + name] = np.ascontiguousarray(inputs[name])
    for name, a in arrays.items():
        args[name] = nc.dram_tensor(name, a.shape, mybir.dt.from_np(a.dtype), kind="ExternalInput").ap()
    out = nc.dram_tensor("out", (1, TOK, D), F32, kind="ExternalOutput").ap()
    trunk_kernel(nc, {n: args["in_" + n] for n in INPUTS}, args["inv_freq"], out)
    r = run_bass_kernel_spmd(nc, [arrays], core_ids=[0])
    return r.results[0]["out"]
```

```python
from contextlib import ExitStack

import concourse.bass as bass
from concourse import mybir

F32 = mybir.dt.float32
F32R = mybir.dt.float32r
I32 = mybir.dt.int32
U32 = mybir.dt.uint32
ALU = mybir.AluOpType
ACT = mybir.ActivationFunctionType
AX = mybir.AxisListType

P = 128
TOK = 256
NT = TOK // P
D = 1024
KD = D // P
DEPTH = 2
A_HEADS, A_KV, A_DIM = 8, 2, 64
B_HEADS, B_NOPE, B_ROPE, B_V = 8, 64, 32, 64
B_QK = B_NOPE + B_ROPE
Q_RANK, KV_RANK = 256, 128
M_HEADS, M_DIM = 4, 128
D_FF = 3584
FF_GROUP = 512
GROUPS = D_FF // FF_GROUP
EXPERTS = 8
SLOTS = 128
BRANCHES = 3
EPS = 1e-6
MASKED = -1e30
THETA = 10000.0

COL_QA = 0
COL_KVCQ = A_HEADS * A_DIM
COL_CKVKR = COL_KVCQ + 2 * A_KV * A_DIM + Q_RANK
COL_QM = COL_CKVKR + KV_RANK + B_ROPE
COL_GATES = COL_QM + M_HEADS * M_DIM

CHUNK = 1024
RAW = 6
DEEP = 21
SPLIT = 4
FFN_CHUNKS = 3 * GROUPS * 4
PAIR_CHUNKS = 24
assert FFN_CHUNKS % DEEP == 0 and FFN_CHUNKS % SPLIT == 0
assert PAIR_CHUNKS % RAW == 0 and PAIR_CHUNKS % SPLIT == 0

TWO_PI_HI = 6.28125
TWO_PI_MID = 0.0019350051879882812
TWO_PI_LO = 3.01991598196e-07
ROUND = 12582912.0
PI_BELOW = 3.1415925


class Tally:

    def __init__(self):
        self.count = {}
        self.events = {}
        self.body = None

    def add(self, name, key, n=1):
        self.count[name] = self.count.get(name, 0) + n
        self.events[name, key] = [self.count[name], 0, 1]
        if self.body is not None:
            self.body.append((name, key))

    def enter_loop(self):
        self.body, self.start = [], dict(self.count)

    def leave_loop(self, times):
        per = {n: c - self.start.get(n, 0) for n, c in self.count.items()}
        for name, key in self.body:
            self.events[name, key][1:] = per[name], times
        for n, c in per.items():
            self.count[n] += c * (times - 1)
        self.body = None

    def after(self, name, key, it=0):
        base, per, _ = self.events[name, key]
        return base + it * per

    def last(self, name, key):
        base, per, times = self.events[name, key]
        return base + (times - 1) * per

    def before(self, name, key, it=0):
        return self.after(name, key, it) - 1



def mixer_chunks(l):
    return ([("qa", l, c) for c in range(4)] + [("kvcq", l, c) for c in range(4)]
            + [("ckvkr", l, c) for c in range(2)] + [("qm", l, c) for c in range(4)]
            + [("uq", l, c) for c in range(2)] + [("ukv", l, 0)]
            + [("gate", l, g, c) for g in range(6) for c in range(4)]
            + [("branch", l, h, i, c) for h in range(2) for i in range(BRANCHES) for c in range(2)]
            + [("out", l, n, c) for part in range(2) for n in range(2) for c in (2 * part, 2 * part + 1)])


def group_order():
    steps = [("GU", 0)]
    for g in range(1, GROUPS):
        steps += [("GU", g), ("D", g - 1)]
    return steps + [("D", GROUPS - 1)]


def group_chunks(tag, kind, g):
    if kind == "GU":
        return [(tag, "G", g, c) for c in range(4)] + [(tag, "U", g, c) for c in range(4)]
    return [(tag, "D", g, c) for c in range(4)]


def build_tally():
    tl = Tally()
    areas, full_by, free_by, prior, latest = {}, {}, {}, {}, {}

    def psum(key, area, full=None, free=None):
        areas[key] = area
        if full is None:
            full = (f"psum_full{area}", key)
            tl.add(*full)
        if free is None:
            free = (f"psum_free{area}", key)
            tl.add(*free)
        full_by[key], free_by[key] = full, free
        prior[key], latest[area] = latest.get(area), key

    def split(key, area, full=None):
        psum(key, area, full)
        tl.add("hi_copied", key)

    tiles, experts_from = {}, [0]

    def chunks(keys):
        for key in keys:
            n = tl.count.get("chunk", 0)
            if key[0] == "moe":
                n -= experts_from[0]
                tiles[key] = (RAW + n % DEEP if n % DEEP < DEEP - RAW
                              else (experts_from[0] + n % DEEP - (DEEP - RAW)) % RAW)
            else:
                tiles[key] = n % RAW
            tl.add("chunk", key)
            tl.add(f"loaded{tiles[key]}", key)
        return "chunk", keys[-1]

    def transposed(name):
        for a in range(2):
            for half in range(2):
                tl.add("hi_copied", (*name, 2 * a + half))
                tl.add("hT_split", (*name, 2 * a + half))
            psum((*name, a, "area"), a, free=("hT_split", (*name, 2 * a + 1)))

    transposed(("memT",))
    for l in range(DEPTH):
        psum(("memk", l), 2, full=chunks([("memk", l, c) for c in range(4)]))
        psum(("memv", l), 3, full=chunks([("memv", l, c) for c in range(4)]))
    for l in range(DEPTH):
        keys = mixer_chunks(l)
        chunks(keys)
        last = {key[0]: ("chunk", key) for key in keys}
        transposed(("hT", 2 * l))
        tl.add("qa_ready", l)
        tl.add("k_ready", l)
        psum(("qa", l), 2, last["qa"], ("qa_ready", l))
        psum(("kvcq", l), 3, last["kvcq"], ("k_ready", l))
        psum(("ckvkr", l), 0, last["ckvkr"], ("k_ready", l))
        psum(("qm", l), 1, last["qm"])
        psum(("T_qa", l), 2)
        split(("T_lat", l), 1)
        split(("T_kv", l), 2)
        for t in range(NT):
            tl.add("qb_copied", (l, t))
            psum(("uq", l, t), (3, 0)[t], last["uq"], ("qb_copied", (l, t)))
        psum(("ukv_k", l, 0), 1)
        psum(("ukv_k", l, 1), 2)
        psum(("ukv_v", l), 3, last["ukv"])
        psum(("T_qb", l, 0), 0)
        psum(("T_qb", l, 1), 1)
        for step in attention_steps():
            for kind, n in step:
                if kind == "QK":
                    a_unit = attention_units()[n][0] == "A"
                    tl.add("exp_done", (l, n), 5 if a_unit else 4)
                    psum(("S", l, n), 0, free=None if a_unit else ("exp_done", (l, n)))
                elif kind == "T":
                    psum(("pT", l, n), 1)
                elif kind == "PV":
                    split(("oT", l, n), 2)
                elif kind == "gate" and n[1] == 3:
                    psum(("gate", l, n[0]), 3, ("chunk", ("gate", l, *n)))
        for h in range(2):
            for i in range(BRANCHES):
                psum(("branch", l, h, i), (h * BRANCHES + i) % 2, ("chunk", ("branch", l, h, i, 1)))
            tl.add("hi_copied", ("mixed", l, h))
        for n in range(2):
            for t in range(NT):
                tl.add("x_added", ("out", l, n, t))
            psum(("out", l, n), 2 + n, ("chunk", ("out", l, n, 3)), ("x_added", ("out", l, n, NT - 1)))
        transposed(("hT", 2 * l + 1))
        if l == 0:
            def dense_step(kind, g, tag):
                last_chunk = chunks(group_chunks(tag, kind, g))
                if kind == "GU":
                    for name in ("silu_done", "act_ready", "hi_copied", "act_split"):
                        tl.add(name, (tag, g))
                    psum((tag, "G", g), 0, ("chunk", (tag, "G", g, 3)), ("silu_done", (tag, g)))
                    psum((tag, "U", g), 1, last_chunk, ("act_ready", (tag, g)))
                return last_chunk

            dense_step("GU", 0, "dense")
            tl.enter_loop()
            for tag, kind, g in dense_pair():
                dense_step(kind, g, tag)
            tl.leave_loop((GROUPS - 1) // 2)
            last_chunk = dense_step("D", "last", "dense")
            for t in range(NT):
                tl.add("x_added", ("down", t))
                psum(("down", t), 2 + t, last_chunk, ("x_added", ("down", t)))
        else:
            psum(("router",), 2)
            psum(("router_T",), 2)
            tl.add("turns_ready", "turns")
            psum(("rank",), 3, free=("turns_ready", "turns"))
            psum(("zero",), 2)
            tl.add("routed", "first")
            tl.add("psum_full3", ("gathered", "first"))
            experts_from[0] = tl.count["chunk"]
            tl.enter_loop()
            areas["gather",] = 3
            tl.add("hi_copied", ("gather",))
            tl.add("psum_free3", ("gather",))
            tl.add("routed", "onehot_w")
            tl.add("routed", "onehot")
            for kind, g in group_order():
                last_chunk = chunks(group_chunks("moe", kind, g))
                if kind == "GU":
                    tl.add("silu_done", ("moe", g))
                    tl.add("act_ready", ("moe", g))
                    psum(("moe", "GU", g), 0, last_chunk, ("act_ready", ("moe", g)))
                    if g == 0:
                        for t in range(NT):
                            tl.add("x_added", ("scatter", t))
                            psum(("scatter", t), (3, 2)[t], free=("x_added", ("scatter", t)))
                        split(("moe", "T", 0), 1)
                    if g == 1:
                        psum(("T_back",), 1)
                elif g + 1 < GROUPS:
                    split(("moe", "T", g + 1), 1)
            tl.add("psum_full3", ("gathered", "next"))
            tl.leave_loop(EXPERTS)
    return tl, areas, full_by, free_by, prior, tiles


def dense_pair():
    return [("pair", "GU", 1), ("pair", "D", 0), ("pair", "GU", 2), ("pair", "D", 1)]


def before_silu(g):
    return order_index("GU", g) + 8 + SPLIT - 1


def before_split(g):
    return order_index("GU", 0) + 8 + SPLIT if g == 0 else order_index("D", g - 1) + 4 + SPLIT - 1


def order_index(kind, g):
    steps = group_order()
    return sum(8 if k == "GU" else 4 for k, _ in steps[:steps.index((kind, g))])


def attention_units():
    return [("A", j) for j in range(4)] + [("B", j) for j in range(4)] + [("M", j) for j in range(2)]


def y_place(u):
    kind, j = attention_units()[u]
    return {"A": (j, 1), "B": (4 + j, 1), "M": (8 + 2 * j, 2)}[kind]


def attention_steps():
    gates = [(g, c) for g in range(6) for c in range(4)]
    n = len(attention_units())
    steps = []
    for u in range(n + 2):
        step = []
        if u < n:
            step.append(("QK", u))
        if gates:
            step.append(("gate", gates.pop(0)))
        if u >= 2:
            step.append(("PV", u - 2))
        if 1 <= u <= n:
            step.append(("T", u - 1))
        if gates:
            step.append(("gate", gates.pop(0)))
        steps.append(step)
    assert not gates
    return steps


def trunk_kernel(nc, A, inv_freq, out):
    tl, areas, full_by, free_by, prior, tiles = build_tally()
    units = attention_units()

    with ExitStack() as ctx:
        def sem(name):
            return ctx.enter_context(nc.semaphore(name))

        def sb_in(scope):
            return lambda name, shape, dt=F32: scope.enter_context(nc.sbuf_tensor(name, shape, dt))

        sb = sb_in(ctx)

        raw = [sb(f"raw{i}", [P, CHUNK]) for i in range(RAW)]
        whi = [sb(f"whi{i}", [P, CHUNK], F32R) for i in range(SPLIT)]
        wlo = [sb(f"wlo{i}", [P, CHUNK], F32R) for i in range(SPLIT)]
        x = sb("x", [P, NT, D])
        gain = sb("gain", [P, D])
        kM = sb("kM", [P, DEPTH, M_HEADS, TOK])
        vM = sb("vM", [P, DEPTH, NT, M_HEADS * M_DIM])
        gates = sb("gates", [P, BRANCHES * KD, TOK])
        normed = gates[:, 0:8, :].rearrange("p (t a) n -> p t (a n)", t=NT)
        junk = gates[:, 8:16, :].rearrange("p (t a) n -> p t (a n)", t=NT)
        wr = gates[:, BRANCHES * KD - 1, 0:KD * EXPERTS].rearrange("p (k e) -> p k e", k=KD)
        wr_hi = sb("wr_hi", [P, KD, EXPERTS], F32R)
        wr_lo = sb("wr_lo", [P, KD, EXPERTS], F32R)
        ident = sb("ident", [P, P])
        mask = sb("mask", [P, NT, TOK])
        freqs = sb("freqs", [P, 48])
        pos_i = sb("pos_i", [P, NT], I32)
        pos_f = sb("pos_f", [P, NT])
        cosA = sb("cosA", [P, NT, A_DIM])
        sinA = sb("sinA", [P, NT, A_DIM])
        cosB = sb("cosB", [P, NT, B_ROPE])
        sinB = sb("sinB", [P, NT, B_ROPE])
        ang = sb("ang", [P, 5, NT, 48])
        meansq = sb("meansq", [P, NT])
        rstd = sb("rstd", [P, NT])
        power = sb("power", [P, 4])
        g_lat = sb("g_lat", [P, DEPTH, Q_RANK + KV_RANK])
        sink = sb("sink", [P, DEPTH, A_HEADS])
        lat_sumsq = sb("lat_sumsq", [P, 2, NT])
        lat_meansq = sb("lat_meansq", [P, 2, NT])
        lat_rstd = sb("lat_rstd", [P, 2, NT])
        row_max = sb("row_max", [P, 4])
        neg_max = sb("neg_max", [P, 4])
        sink_arg = sb("sink_arg", [P, 4])
        sink_exp = sb("sink_exp", [P, 4])
        row_sum = sb("row_sum", [P, 4])
        inv_sum = sb("inv_sum", [P, 4])
        sumsq = sb("sumsq", [P, 2, NT])

        trunk = ExitStack()
        sb = sb_in(trunk)
        hT_hi = sb("hT_hi", [P, KD, TOK], F32R)
        hT_lo = sb("hT_lo", [P, KD, TOK], F32R)
        mixer = ExitStack()
        sb = sb_in(mixer)
        y_hi = sb("y_hi", [P, 12, TOK], F32R)
        y_lo = sb("y_lo", [P, 12, TOK], F32R)

        attn = ExitStack()
        sb = sb_in(attn)
        qaT = sb("qaT", [P, 4, TOK])
        kaT = sb("kaT", [P, A_KV, TOK])
        vA = sb("vA", [P, NT, A_KV * A_DIM])
        cqT_hi = sb("cqT_hi", [P, 2, TOK], F32R)
        cqT_lo = sb("cqT_lo", [P, 2, TOK], F32R)
        ckvT_hi = sb("ckvT_hi", [P, TOK], F32R)
        ckvT_lo = sb("ckvT_lo", [P, TOK], F32R)
        qBT = sb("qBT", [B_QK, B_HEADS, TOK])
        kBT = sb("kBT", [B_QK, B_HEADS, TOK])
        vB = sb("vB", [P, NT, B_HEADS * B_V])
        qMT = sb("qMT", [P, M_HEADS, TOK])
        rows = ExitStack()
        sb = sb_in(rows)
        qa_rot = sb("qa_rot", [P, NT, A_HEADS * A_DIM])
        cq_n = sb("cq_n", [P, NT, Q_RANK])
        kr_pad = sb("kr_pad", [P, NT, B_QK])
        qB = sb("qB", [P, NT, B_HEADS, B_QK])
        rows.close()
        sb = sb_in(attn)
        probs = sb("probs", [P, 2, 2, NT, TOK])
        pT = sb("pT", [P, 2, NT, TOK])
        rot1 = gates[:, 16:18, :].rearrange("p a n -> p (a n)")
        rot2 = gates[:, 18:20, :].rearrange("p a n -> p (a n)")
        k_dup = gates[:, 20:22, :].rearrange("p t (k a n) -> p t k a n", k=A_KV, a=2)
        ckv_n = gates[:, 22, :].rearrange("p (t n) -> p t n", t=NT)
        attn.close()

        mixing = ExitStack()
        sb = sb_in(mixing)
        mixed = sb("mixed", [P, 4, TOK])
        gated = sb("gated", [P, 4, TOK])
        mixT_hi = sb("mixT_hi", [P, KD, TOK], F32R)
        mixT_lo = sb("mixT_lo", [P, KD, TOK], F32R)
        mixing.close()

        ffn = ExitStack()
        sb = sb_in(ffn)
        silu = sb("silu", [P, 4, TOK])
        act = sb("act", [P, 4, TOK])
        actT_hi = [sb(f"actT_hi{i}", [P, 4, TOK], F32R) for i in range(2)]
        actT_lo = [sb(f"actT_lo{i}", [P, 4, TOK], F32R) for i in range(2)]
        zeros = sb("zeros", [1, FF_GROUP])
        ffn.close()
        mixer.close()
        trunk.close()

        moe = ExitStack()
        sb = sb_in(moe)
        in_rows = [sb(f"raw{i}", [P, CHUNK]) for i in range(DEEP - 3, DEEP)]
        y_sb = sb("y_sb", [P, D])
        raw += [sb(f"raw{i}", [P, CHUNK]) for i in range(RAW, RAW + 6)]
        raw += [kM[:, l, :, :].rearrange("p h n -> p (h n)") for l in range(DEPTH)]
        raw += [vM[:, l, :, :].rearrange("p t n -> p (t n)") for l in range(DEPTH)]
        raw += [gates[:, a:a + 4, :].rearrange("p a n -> p (a n)") for a in (16, 20)]
        raw += in_rows
        assert len(raw) == DEEP
        logitsT = sb("logitsT", [EXPERTS, TOK])
        logits = sb("logits", [P, NT, EXPERTS])
        top8 = sb("top8", [P, NT, 8])
        top_i = sb("top_i", [P, NT, 8], U32)
        top_f = sb("top_f", [P, NT, 8])
        pair_e = sb("pair_e", [P, NT])
        pair_d = sb("pair_d", [P, NT])
        pair_w = sb("pair_w", [P, 2, NT])
        hot = sb("hot", [P, 2, NT, EXPERTS])
        routed = sb("routed", [P, NT, EXPERTS])
        route_w = sb("route_w", [P, NT, EXPERTS])
        earlier = sb("earlier", [P, P])
        ones = sb("ones", [P, P])
        iota8 = sb("iota8", [P, EXPERTS])
        iotaS = sb("iotaS", [P, SLOTS])
        route = sb("route", [P, 2 * EXPERTS + 1, 4])
        cur = sb("cur", [P, 4])
        cur_next = sb("cur_next", [P, 4])
        zeros_m = sb("zeros_m", [1, FF_GROUP])
        most = sb("most", [P, 1])
        turns_f = sb("turns_f", [P, 1])
        turns_i = sb("turns_i", [P, 1], I32)
        onehot = sb("onehot", [P, NT, SLOTS])
        onehot_w = sb("onehot_w", [P, NT, SLOTS])
        back = sb("back", [P, TOK])
        xg_hi = sb("xg_hi", [P, KD, SLOTS], F32R)
        xg_lo = sb("xg_lo", [P, KD, SLOTS], F32R)
        silu_m = sb("silu_m", [P, FF_GROUP])
        act_m = sb("act_m", [P, FF_GROUP])
        actm_hi = [sb(f"actm_hi{i}", [P, 4, SLOTS], F32R) for i in range(2)]
        actm_lo = [sb(f"actm_lo{i}", [P, 4, SLOTS], F32R) for i in range(2)]
        moe.close()

        ps = [ctx.enter_context(nc.psum_tensor(f"ps{a}", [P, CHUNK], F32)) for a in range(4)]

        chunk_loaded = [sem(f"chunk_loaded{i}") for i in range(DEEP)]
        chunk_hi = sem("chunk_hi")
        chunk_split = sem("chunk_split")
        chunk_used = sem("chunk_used")
        hT_split = sem("hT_split")
        psum_full = [sem(f"psum_full{a}") for a in range(4)]
        psum_free = [sem(f"psum_free{a}") for a in range(4)]
        hi_copied = sem("hi_copied")
        mem_loaded = sem("mem_loaded")
        x_loaded = sem("x_loaded")
        small_loaded = sem("small_loaded")
        router_loaded = sem("router_loaded")
        gain_loaded = sem("gain_loaded")
        constants = sem("constants")
        routing_constants = sem("routing_constants")
        sumsq_ready = sem("sumsq_ready")
        meansq_ready = sem("meansq_ready")
        rstd_ready = sem("rstd_ready")
        norm_done = sem("norm_done")
        lat_sumsq_ready = sem("lat_sumsq_ready")
        lat_meansq_ready = sem("lat_meansq_ready")
        lat_rstd_ready = sem("lat_rstd_ready")
        angles_ready = sem("angles_ready")
        trig_ready = sem("trig_ready")
        dve_step = sem("dve_step")
        v_copied = sem("v_copied")
        qa_ready = sem("qa_ready")
        k_ready = sem("k_ready")
        qb_copied = sem("qb_copied")
        qb_ready = sem("qb_ready")
        kr_copied = sem("kr_copied")
        max_ready = sem("max_ready")
        exp_done = sem("exp_done")
        probs_ready = sem("probs_ready")
        gates_ready = sem("gates_ready")
        mixed_ready = sem("mixed_ready")
        mixed_split = sem("mixed_split")
        x_added = sem("x_added")
        silu_done = sem("silu_done")
        act_ready = sem("act_ready")
        act_split = sem("act_split")
        y_copied = sem("y_copied")
        zeros_ready = sem("zeros_ready")
        wr_hi_ready = sem("wr_hi_ready")
        wr_split = sem("wr_split")
        diff_ready = sem("diff_ready")
        ratio_ready = sem("ratio_ready")
        masks_ready = sem("masks_ready")
        turns_ready = sem("turns_ready")
        picked = sem("picked")
        routed_sem = sem("routed")
        stored = sem("stored")

        counters = {"chunk": chunk_used, "qa_ready": qa_ready, "k_ready": k_ready, "qb_copied": qb_copied,
                    "exp_done": exp_done, "silu_done": silu_done, "act_ready": act_ready,
                    "turns_ready": turns_ready, "x_added": x_added, "hT_split": hT_split}
        for a in range(4):
            counters[f"psum_full{a}"], counters[f"psum_free{a}"] = psum_full[a], psum_free[a]

        def wait_full(eng, key, it=0):
            name, event = full_by[key]
            eng.wait_ge(counters[name], tl.after(name, event, it))

        def wait_free(eng, key):
            if prior[key] is not None:
                name, event = free_by[prior[key]]
                eng.wait_ge(counters[name], tl.last(name, event))

        def wait_free_in_loop(eng, key, it):
            a = areas[key]
            eng.wait_ge(psum_free[a], tl.before(f"psum_free{a}", key, it))

        def wait_read(eng, key, it=0):
            name, event = free_by[key]
            eng.wait_ge(counters[name], tl.after(name, event, it))

        def gathered_by(turn):
            per_turn = tl.events["psum_full3", ("gathered", "next")][1]
            return turn * per_turn + tl.after("psum_full3", ("gathered", "first"))

        def area(key):
            return ps[areas[key]]

        def chunk_no(key, it=0):
            return tl.before("chunk", key, it)

        def slot(key):
            return tl.before("chunk", key)

        def tile(key):
            return tiles[key]

        w_in = A["w_in"].rearrange("l (k p) n -> l p k n", p=P)
        w_mem = A["w_mem_kv"].rearrange("l (k p) n -> l p k n", p=P)
        w_uq = A["w_uq"].rearrange("l (k p) n -> l p k n", p=P)
        w_branch = A["w_branch"].rearrange("l b (k p) n -> l b p k n", p=P)
        w_out = A["w_out"].rearrange("l (k p) n -> l p k n", p=P)
        dense_w = {"G": A["w_gate_dense"].rearrange("l (k p) n -> l p k n", p=P),
                   "U": A["w_up_dense"].rearrange("l (k p) n -> l p k n", p=P),
                   "D": A["w_down_dense"].rearrange("l (k p) n -> l k p n", p=P)}
        expert_w = {"G": A["w_gate_exp"].rearrange("l e (k p) n -> (l e) p k n", p=P),
                    "U": A["w_up_exp"].rearrange("l e (k p) n -> (l e) p k n", p=P),
                    "D": A["w_down_exp"].rearrange("l e (k p) n -> (l e) k p n", p=P)}

        def chunk_source(key, it=0):
            kind = key[0]
            if kind in ("memk", "memv"):
                _, l, c = key
                n0 = 0 if kind == "memk" else M_HEADS * M_DIM
                return w_mem[l, :, 2 * c:2 * c + 2, n0:n0 + 512]
            if kind in ("qa", "kvcq", "qm"):
                _, l, c = key
                n0 = {"qa": COL_QA, "kvcq": COL_KVCQ, "qm": COL_QM}[kind]
                return w_in[l, :, 2 * c:2 * c + 2, n0:n0 + 512]
            if kind == "ckvkr":
                _, l, c = key
                return w_in[l, :, 4 * c:4 * c + 4, COL_CKVKR:COL_QM]
            if kind == "uq":
                _, l, c = key
                return w_uq[l, :, c, :]
            if kind == "ukv":
                return A["w_ukv"][key[1]]
            if kind == "gate":
                _, l, g, c = key
                n0 = COL_GATES + 512 * g
                return w_in[l, :, 2 * c:2 * c + 2, n0:n0 + 512]
            if kind == "branch":
                _, l, h, i, c = key
                return w_branch[l, i, :, 2 * c:2 * c + 2, 512 * h:512 * h + 512]
            if kind == "out":
                _, l, n, c = key
                return w_out[l, :, 2 * c:2 * c + 2, 512 * n:512 * n + 512]
            _, which, g, c = key
            if kind == "moe":
                w = expert_w[which][it]
                if which == "D":
                    return w[4 * g + c]
                return w[:, 2 * c:2 * c + 2, FF_GROUP * g:FF_GROUP * (g + 1)]
            w = dense_w[which][0]
            if kind == "dense":
                g = GROUPS - 1 if g == "last" else g
                if which == "D":
                    return w[4 * g + c]
                return w[:, 2 * c:2 * c + 2, FF_GROUP * g:FF_GROUP * (g + 1)]
            if which == "D":
                return w[it * 8 + (4 * g + c)]
            return w[:, 2 * c:2 * c + 2, bass.ds(it * (2 * FF_GROUP) + g * FF_GROUP, FF_GROUP)]

        def chunk_view(key, tile):
            kind = key[0]
            if kind == "ckvkr":
                return tile[:, 0:4 * (KV_RANK + B_ROPE)].rearrange("p (k n) -> p k n", k=4)
            if kind == "uq":
                return tile[:, 0:B_HEADS * B_QK]
            if kind == "ukv" or key[1] == "D":
                return tile[:, :]
            return tile[:, :].rearrange("p (k n) -> p k n", k=2)

        def chunk_width(key):
            return {"ckvkr": 4 * (KV_RANK + B_ROPE), "uq": B_HEADS * B_QK}.get(key[0], CHUNK)

        opening = [(k, l, c) for l in range(DEPTH) for k in ("memk", "memv") for c in range(4)]
        dense_first = group_chunks("dense", "GU", 0)
        dense_loop = [c for tag, kind, g in dense_pair() for c in group_chunks(tag, kind, g)]
        dense_last = group_chunks("dense", "D", "last")
        moe_loop = [c for kind, g in group_order() for c in group_chunks("moe", kind, g)]
        first_in_rows = next(key for key in moe_loop if tile(key) == DEEP - 3)
        DENSE_TURNS = (GROUPS - 1) // 2
        assert len(dense_loop) == PAIR_CHUNKS and len(moe_loop) == FFN_CHUNKS

        block = ctx.enter_context(nc.Block())

        @block.sync
        def _(sp):
            def load(key, it=0, weights_of=None):
                depth = DEEP if key[0] == "moe" else RAW
                if not isinstance(it, int) or slot(key) >= RAW:
                    sp.wait_ge(chunk_split, chunk_no(key, it) - depth + 1)
                src = chunk_source(key, it if weights_of is None else weights_of)
                sp.dma_start(chunk_view(key, raw[tile(key)]), src).then_inc(chunk_loaded[tile(key)], 16)

            sp.dma_start(normed, A["mem"][0].rearrange("(t p) d -> p t d", p=P)).then_inc(mem_loaded, 16)
            sp.dma_start(x[:, :, :], A["x"][0].rearrange("(t p) d -> p t d", p=P)).then_inc(x_loaded, 16)
            for key in opening + mixer_chunks(0) + dense_first:
                load(key)
            with nc.sync.Fori(0, DENSE_TURNS) as it:
                for key in dense_loop:
                    load(key, it)
            for key in dense_last + mixer_chunks(1):
                load(key)
            sp.wait_ge(chunk_used, tl.after("chunk", ("branch", DEPTH - 1, 1, BRANCHES - 1, 1)))
            sp.wait_ge(mixed_ready, 2 * DEPTH)
            with nc.sync.Fori(0, EXPERTS) as e:
                for key in moe_loop:
                    if key == first_in_rows:
                        wait_full(sp, ("router",))
                    load(key, e)
            sp.wait_ge(turns_ready, 1)
            turns = nc.sync.value_load(turns_i[0:1, 0:1], min_val=EXPERTS, max_val=2 * EXPERTS)
            with nc.sync.If(turns > EXPERTS):
                with nc.sync.Fori(EXPERTS, 2 * EXPERTS) as e:
                    for key in moe_loop:
                        load(key, e, weights_of=e - EXPERTS)
            sp.wait_ge(norm_done, 2 * 6)
            sp.dma_start(out[0].rearrange("(t p) d -> p t d", p=P), normed).then_inc(stored, 16)
            sp.wait_ge(stored, 16)

        @block.gpsimd
        def _(pool):
            def load_gain(n, row):
                if n:
                    pool.wait_ge(norm_done, 2 * n)
                pool.dma_start(gain[:, :], row.partition_broadcast(P)).then_inc(gain_loaded, 16)

            load_gain(0, A["g_mem"])
            for t in range(NT):
                pool.dma_start(pos_i[:, t:t + 1],
                               A["positions"][0, P * t:P * (t + 1)].unsqueeze(1)).then_inc(small_loaded, 16)
            pool.dma_start(freqs[:, :], inv_freq.partition_broadcast(P)).then_inc(small_loaded, 16)
            for l in range(DEPTH):
                pool.dma_start(g_lat[:, l, 0:Q_RANK], A["g_q_lat"][l].partition_broadcast(P)).then_inc(small_loaded, 16)
                pool.dma_start(g_lat[:, l, Q_RANK:], A["g_kv_lat"][l].partition_broadcast(P)).then_inc(small_loaded, 16)
                pool.dma_start(sink[:, l, :], A["sink"][l].partition_broadcast(P)).then_inc(small_loaded, 16)
            pool.dma_start(wr[:, :, :], A["w_router"][0].rearrange("(k p) e -> p k e", p=P)).then_inc(router_loaded, 16)
            nc.gpsimd.memset(ident[:, :], 0.0).then_inc(constants, 1)
            nc.gpsimd.memset(mask[:, :, :], 0.0).then_inc(constants, 1)
            nc.gpsimd.memset(power[:, :], -0.5).then_inc(constants, 1)
            pool.wait_ge(constants, 3)
            nc.gpsimd.affine_select(out=ident[:, :], in_=ident[:, :], compare_op=ALU.not_equal, fill=1.0, base=0,
                                    pattern=[[-1, P]], channel_multiplier=1).then_inc(constants, 1)
            nc.gpsimd.affine_select(out=mask[:, 0, P:], in_=mask[:, 0, P:], compare_op=ALU.is_ge, fill=MASKED,
                                    base=0, pattern=[[-1, P]], channel_multiplier=1).then_inc(constants, 1)
            nc.gpsimd.affine_select(out=mask[:, 1, 0:P], in_=mask[:, 1, 0:P], compare_op=ALU.is_ge, fill=MASKED,
                                    base=0, pattern=[[1, P]], channel_multiplier=-1).then_inc(constants, 1)

            def rstd_of(n):
                pool.wait_ge(meansq_ready, n + 1)
                nc.gpsimd.tensor_tensor(rstd[:, :], meansq[:, :], power[:, 0:NT], ALU.pow).then_inc(rstd_ready, 1)

            rstd_of(0)
            load_gain(1, A["g_mix"][0])
            for l in range(DEPTH):
                rstd_of(2 * l + 1)
                load_gain(2 * l + 2, A["g_ffn"][l])
                pool.wait_ge(chunk_used, tl.after("chunk", ("qa", l, 3)))
                nc.gpsimd.memset(kr_pad[:, :, 0:B_NOPE], 0.0).then_inc(constants, 1)
                pool.wait_ge(lat_meansq_ready, l + 1)
                nc.gpsimd.tensor_tensor(lat_rstd[:, :, :], lat_meansq[:, :, :],
                                        power[:, :].rearrange("p (a t) -> p a t", a=2),
                                        ALU.pow).then_inc(lat_rstd_ready, 1)
                rstd_of(2 * l + 2)
                load_gain(2 * l + 3, A["g_mix"][1] if l == 0 else A["g_final"])
                if l == 0:
                    nc.gpsimd.memset(zeros[:, :], 0.0).then_inc(zeros_ready, 1)
                else:
                    nc.gpsimd.memset(ones[:, :], 1.0).then_inc(routing_constants, 1)
                    nc.gpsimd.memset(zeros_m[:, :], 0.0).then_inc(routing_constants, 1)
                    nc.gpsimd.memset(back[:, :], 0.0).then_inc(routing_constants, 1)
                    nc.gpsimd.memset(route[:, 2 * EXPERTS, :], -1.0).then_inc(routing_constants, 1)
                    nc.gpsimd.iota(iota8[:, :], pattern=[[1, EXPERTS]], base=0, channel_multiplier=0,
                                   allow_small_or_imprecise_dtypes=True).then_inc(routing_constants, 1)
                    nc.gpsimd.iota(iotaS[:, :], pattern=[[1, SLOTS]], base=0, channel_multiplier=0,
                                   allow_small_or_imprecise_dtypes=True).then_inc(routing_constants, 1)
                    pool.wait_ge(routing_constants, 1)
                    nc.gpsimd.affine_select(out=earlier[:, :], in_=ones[:, :], compare_op=ALU.is_gt, fill=0.0, base=0,
                                            pattern=[[1, P]], channel_multiplier=-1).then_inc(routing_constants, 1)
            rstd_of(5)

        @block.scalar
        def _(eng):
            s = nc.scalar

            def hi_of(key, it=0):
                n = slot(key)
                w = chunk_width(key)
                loads, loads_per_turn, _ = tl.events[f"loaded{tile(key)}", key]
                eng.wait_ge(chunk_loaded[tile(key)], 16 * loads + it * (16 * loads_per_turn))
                if not isinstance(it, int) or n >= SPLIT:
                    eng.wait_ge(chunk_used, chunk_no(key, it) - SPLIT + 1)
                s.activation(whi[n % SPLIT][:, 0:w], raw[tile(key)][:, 0:w], ACT.Copy).then_inc(chunk_hi, 1)

            def copy_hi(key, dst, src, it=0):
                wait_full(eng, key, it)
                s.activation(dst, src, ACT.Copy).then_inc(hi_copied, 1)

            def copy_out(key, dst, src, it=0):
                wait_full(eng, key, it)
                a = areas[key]
                s.activation(dst, src, ACT.Copy).then_inc(psum_free[a], 1)

            def squares(src, added=None):
                for half in range(2):
                    for t in range(NT):
                        if added is not None:
                            eng.wait_ge(x_added, tl.after("x_added", added(half, t)))
                        cols = slice(512 * half, 512 * (half + 1))
                        s.activation(junk[:, t, cols], src[:, t, cols], ACT.Square,
                                     accum_out=sumsq[:, half, t:t + 1]).then_inc(sumsq_ready, 1)

            def transposed(name):
                for a in range(2):
                    wait_full(eng, (*name, a, "area"))
                    for half in range(2):
                        k = 4 * a + 2 * half
                        s.activation(hT_hi[:, k:k + 2, :].rearrange("p k n -> p (k n)"),
                                     ps[a][:, 512 * half:512 * (half + 1)], ACT.Copy).then_inc(hi_copied, 1)

            eng.wait_ge(mem_loaded, 16)
            squares(normed)
            for key in opening[0:SPLIT]:
                hi_of(key)
            transposed(("memT",))
            pending = opening[SPLIT:] + mixer_chunks(0)[0:2]
            for l in range(DEPTH):
                for key in pending[0:2]:
                    hi_of(key)
                pending = pending[2:]
                copy_out(("memk", l), kM[:, l, :, :].rearrange("p h n -> p (h n)"), area(("memk", l))[:, :])
                if l == 0:
                    eng.wait_ge(angles_ready, 2)
                    s.activation(ang[:, 3, :, :], ang[:, 0, :, :], ACT.Sin).then_inc(trig_ready, 1)
                    s.activation(ang[:, 4, :, :], ang[:, 1, :, :], ACT.Sin).then_inc(trig_ready, 1)
                    eng.wait_ge(router_loaded, 16)
                    s.activation(wr_hi[:, :, :], wr[:, :, :], ACT.Copy).then_inc(wr_hi_ready, 1)
                for key in pending[0:3]:
                    hi_of(key)
                if l == 0:
                    eng.wait_ge(x_loaded, 16)
                    squares(x)
                for key in pending[3:6]:
                    hi_of(key)
                pending = pending[6:]
            for l in range(DEPTH):
                todo = mixer_chunks(l)
                done = [2 if l == 0 else 0]

                def ahead(key, more=3):
                    upto = min(len(todo), todo.index(key) + 1 + more)
                    for k in todo[done[0]:upto]:
                        hi_of(k)
                    done[0] = max(done[0], upto)

                ahead(("qa", l, 0))
                if l:
                    squares(x, lambda half, t: ("down", t))
                transposed(("hT", 2 * l))
                ahead(("kvcq", l, 3))
                key = ("kvcq", l)
                wait_full(eng, key)
                kv = area(key)[:, :].rearrange("p (t n) -> p t n", t=NT)
                s.activation(vA[:, :, :], kv[:, :, 128:256], ACT.Copy).then_inc(v_copied, 1)
                for t in range(NT):
                    s.activation(junk[:, t, 0:Q_RANK], kv[:, t, 256:512], ACT.Square,
                                 accum_out=lat_sumsq[:, 0, t:t + 1]).then_inc(lat_sumsq_ready, 1)
                ahead(("ckvkr", l, 1))
                key = ("ckvkr", l)
                wait_full(eng, key)
                kv = area(key)[:, :].rearrange("p (t n) -> p t n", t=NT)
                for t in range(NT):
                    s.activation(junk[:, t, 512:512 + KV_RANK], kv[:, t, 0:KV_RANK], ACT.Square,
                                 accum_out=lat_sumsq[:, 1, t:t + 1]).then_inc(lat_sumsq_ready, 1)
                ahead(("qm", l, 3))
                copy_out(("qm", l), qMT[:, :, :].rearrange("p h n -> p (h n)"), area(("qm", l))[:, :])
                copy_out(("T_qa", l), qaT[:, :, :].rearrange("p h n -> p (h n)"), area(("T_qa", l))[:, :])
                key = ("T_lat", l)
                copy_hi(key, cqT_hi[:, :, :].rearrange("p k n -> p (k n)"), area(key)[:, 512:1024])
                key = ("T_kv", l)
                copy_hi(key, ckvT_hi[:, :], area(key)[:, 0:TOK])
                s.activation(kBT[B_NOPE:B_QK, :, :],
                             area(key)[B_NOPE:B_QK, 512:512 + TOK].unsqueeze(1).to_broadcast([B_ROPE, B_HEADS, TOK]),
                             ACT.Copy).then_inc(kr_copied, 1)
                ahead(("uq", l, 1))
                for t in range(NT):
                    key = ("uq", l, t)
                    wait_full(eng, key)
                    s.activation(qB[:, t, :, :].rearrange("p (a h) n -> p a (h n)", a=2),
                                 area(key)[:, :].rearrange("p (a n) -> p a n", a=2)[:, :, 0:4 * B_QK],
                                 ACT.Copy).then_inc(qb_copied, 1)
                ahead(("ukv", l, 0))
                for a in range(2):
                    key = ("ukv_k", l, a)
                    copy_out(key, kBT[0:B_NOPE, 4 * a:4 * a + 4, :].rearrange("p h n -> p (h n)"), area(key)[0:B_NOPE, :])
                copy_out(("T_qb", l, 0), qBT[:, 0:4, :].rearrange("p h n -> p (h n)"), area(("T_qb", l, 0))[0:B_QK, :])

                def exps(u):
                    kind, j = units[u]
                    eng.wait_ge(max_ready, l * len(units) + u + 1)
                    if kind == "A":
                        for q in range(4):
                            tile = probs[:, u % 2, q // 2, q % 2, :]
                            s.activation(tile, tile, ACT.Exp, bias=neg_max[:, q:q + 1],
                                         accum_out=row_sum[:, q:q + 1]).then_inc(exp_done, 1)
                        s.activation(sink_exp[:, :], sink_arg[:, :], ACT.Exp).then_inc(exp_done, 1)
                    else:
                        wait_full(eng, ("pT", l, u - 2))
                        scale = (B_QK if kind == "B" else M_DIM) ** -0.5
                        for q in range(4):
                            s.activation(probs[:, u % 2, q // 2, q % 2, :],
                                         area(("S", l, u))[:, TOK * q:TOK * (q + 1)], ACT.Exp,
                                         bias=neg_max[:, q:q + 1], scale=scale,
                                         accum_out=row_sum[:, q:q + 1]).then_inc(exp_done, 1)

                for step in attention_steps():
                    first_gate = True
                    for kind, n in step:
                        if kind == "gate":
                            if n[1] != 3:
                                ahead(("gate", l, *n))
                            else:
                                g = n[0]
                                copy_out(("gate", l, g), gates[:, 4 * g:4 * g + 4, :].rearrange("p a n -> p (a n)"),
                                         area(("gate", l, g))[:, :])
                                ahead(("gate", l, *n))
                            if first_gate and step[0][0] == "QK":
                                exps(step[0][1])
                            first_gate = False
                        elif kind == "T":
                            key = ("pT", l, n)
                            if n >= 1:
                                wait_full(eng, ("oT", l, n - 1))
                            copy_out(key, pT[:, :, :, :].rearrange("p h k n -> p (h k n)"), area(key)[:, :])
                        elif kind == "PV":
                            key = ("oT", l, n)
                            blk, wide = y_place(n)
                            copy_hi(key, y_hi[:, blk:blk + wide, :].rearrange("p b n -> p (b n)"),
                                    area(key)[:, 0:wide * TOK])
                for g in range(6):
                    eng.wait_ge(psum_free[3], tl.after("psum_free3", ("gate", l, g)))
                    part = gates[:, 4 * g:4 * g + 4, :]
                    s.activation(part, part, ACT.Sigmoid).then_inc(gates_ready, 1)
                    ahead(("branch", l, 0, 0, 0), min(g, 3))
                for h in range(2):
                    ahead(("branch", l, h, 2, 1))
                    if l:
                        wait_full(eng, ("branch", l, h, 2))
                    eng.wait_ge(mixed_ready, 2 * l + h + 1)
                    s.activation(mixT_hi[:, 4 * h:4 * h + 4, :], mixed[:, :, :], ACT.Copy).then_inc(hi_copied, 1)
                ahead(("out", l, 1, 1))
                ahead(("out", l, 0, 3), 2)
                if l == 0:
                    for key in dense_first[0:2]:
                        hi_of(key)
                squares(x, lambda half, t: ("out", l, half, t))
                if l == 0:
                    for key in dense_first[2:SPLIT]:
                        hi_of(key)
                transposed(("hT", 2 * l + 1))

                if l == 0:
                    def dense_silu(tag, g, it=0):
                        wait_full(eng, (tag, "G", g), it)
                        if tag == "pair":
                            eng.wait_ge(act_ready, tl.before("act_ready", (tag, g), it))
                        s.activation(silu[:, :, :], ps[0][:, :].rearrange("p (a n) -> p a n", a=4),
                                     ACT.Silu).then_inc(silu_done, 1)

                    def dense_hi(n, pair):
                        eng.wait_ge(act_ready, n + 1)
                        s.activation(actT_hi[pair][:, :, :], act[:, :, :], ACT.Copy).then_inc(hi_copied, 1)

                    for key in dense_first[SPLIT:7]:
                        hi_of(key)
                    dense_silu("dense", 0)
                    hi_of(dense_first[7])
                    with s.Fori(0, DENSE_TURNS) as it:
                        for tag, kind, g in dense_pair():
                            keys = group_chunks(tag, kind, g)
                            if kind == "GU":
                                for key in keys[0:3]:
                                    hi_of(key, it)
                                dense_hi(it * 2 + (g - 1), (g - 1) % 2)
                                for key in keys[3:7]:
                                    hi_of(key, it)
                                dense_silu(tag, g, it)
                                hi_of(keys[7], it)
                            else:
                                for key in keys:
                                    hi_of(key, it)
                    dense_hi(GROUPS - 1, (GROUPS - 1) % 2)
                    for key in dense_last:
                        hi_of(key)

            eng.wait_ge(diff_ready, 1)
            s.activation(pair_e[:, :], pair_d[:, :], ACT.Exp).then_inc(ratio_ready, 1)
            wait_full(eng, ("zero",))
            eng.wait_ge(turns_ready, 1)
            turns = s.value_load(turns_i[0:1, 0:1], min_val=EXPERTS, max_val=2 * EXPERTS)
            with s.Fori(0, turns) as e:
                done_m = [0]

                def upto(n):
                    for key in moe_loop[done_m[0]:n]:
                        hi_of(key, e)
                    done_m[0] = max(done_m[0], n)

                def moe_silu(g):
                    wait_full(eng, ("moe", "GU", g), e)
                    if g:
                        eng.wait_ge(act_ready, tl.after("act_ready", ("moe", g - 1), e))
                    s.activation(silu_m[:, :], ps[0][:, 0:FF_GROUP], ACT.Silu).then_inc(silu_done, 1)

                def moe_hi(g):
                    key = ("moe", "T", g)
                    wait_full(eng, key, e)
                    s.activation(actm_hi[g % 2][:, :, :], ps[1][:, 0:FF_GROUP].rearrange("p (a n) -> p a n", a=4),
                                 ACT.Copy).then_inc(hi_copied, 1)

                upto(2)
                eng.wait_ge(psum_full[3], gathered_by(e))
                s.activation(xg_hi[:, :, :].rearrange("p k n -> p (k n)"), ps[3][:, :], ACT.Copy).then_inc(hi_copied, 1)
                upto(4)
                eng.wait_ge(chunk_used, chunk_no(moe_loop[0], e))
                s.activation(y_sb[:, :], ps[2][:, :], ACT.Copy).then_inc(y_copied, 1)
                upto(before_silu(0))
                moe_silu(0)
                upto(before_split(0))
                moe_hi(0)
                for g in range(1, GROUPS):
                    upto(before_silu(g))
                    moe_silu(g)
                    upto(before_split(g))
                    moe_hi(g)
                upto(FFN_CHUNKS)
            eng.wait_ge(chunk_used, chunk_no(moe_loop[0], turns))
            s.activation(y_sb[:, :], ps[2][:, :], ACT.Copy).then_inc(y_copied, 1)
            for half in range(2):
                for t in range(NT):
                    eng.wait_ge(x_added, tl.after("x_added", ("scatter", t), turns))
                    cols = slice(512 * half, 512 * (half + 1))
                    s.activation(junk[:, t, cols], x[:, t, cols], ACT.Square,
                                 accum_out=sumsq[:, half, t:t + 1]).then_inc(sumsq_ready, 1)

        @block.vector
        def _(eng):
            v = nc.vector
            steps = [0]

            def step(ins):
                steps[0] += 1
                ins.then_inc(dve_step, 1)
                eng.wait_ge(dve_step, steps[0])

            def lo_of(key, it=0):
                n = slot(key)
                w = chunk_width(key)
                eng.wait_ge(chunk_hi, chunk_no(key, it) + 1)
                v.tensor_tensor(wlo[n % SPLIT][:, 0:w], raw[tile(key)][:, 0:w], whi[n % SPLIT][:, 0:w].bitcast(F32),
                                ALU.subtract).then_inc(chunk_split, 1)

            def rest(key, lo, src, hi, it=0):
                eng.wait_ge(hi_copied, tl.after("hi_copied", key, it))
                v.tensor_tensor(lo, src, hi.bitcast(F32), ALU.subtract).then_inc(psum_free[areas[key]], 1)

            def norm(n, src, dst):
                eng.wait_ge(sumsq_ready, 2 * NT * (n + 1))
                step(v.tensor_tensor(meansq[:, :], sumsq[:, 0, :], sumsq[:, 1, :], ALU.add))
                v.tensor_scalar(meansq[:, :], meansq[:, :], 1.0 / D, EPS, ALU.mult, ALU.add).then_inc(meansq_ready, 1)
                eng.wait_ge(rstd_ready, n + 1)
                eng.wait_ge(gain_loaded, 16 * (n + 1))
                for t in range(NT):
                    v.scalar_tensor_tensor(dst[:, t, :], src[:, t, :], rstd[:, t:t + 1], gain[:, :],
                                           ALU.mult, ALU.mult).then_inc(norm_done, 1)

            def transposed(name):
                for i in range(4):
                    eng.wait_ge(hi_copied, tl.after("hi_copied", (*name, i)))
                    flat = lambda w: w[:, 2 * i:2 * i + 2, :].rearrange("p k n -> p (k n)")
                    v.tensor_tensor(flat(hT_lo), ps[i // 2][:, 512 * (i % 2):512 * (i % 2 + 1)],
                                    flat(hT_hi).bitcast(F32), ALU.subtract).then_inc(hT_split, 1)

            def rotate(src, heads, half, cos, sin, dsts, done=None):
                n = heads * 2 * half
                r1 = rot1[:, 0:n].rearrange("p (h a d) -> p h a d", h=heads, a=2)
                r2 = rot2[:, 0:n].rearrange("p (h a d) -> p h a d", h=heads, a=2)
                c = cos.rearrange("p (a d) -> p a d", a=2)
                sn = sin.rearrange("p (a d) -> p a d", a=2)
                v.tensor_tensor(rot1[:, 0:n].rearrange("p (h n) -> p h n", h=heads),
                                src, cos.unsqueeze(1).to_broadcast([P, heads, 2 * half]), ALU.mult)
                v.tensor_tensor(r2[:, :, 0, :], src[:, :, half:2 * half],
                                sn[:, 0, :].unsqueeze(1).to_broadcast([P, heads, half]), ALU.mult)
                step(v.tensor_tensor(r2[:, :, 1, :], src[:, :, 0:half],
                                     sn[:, 1, :].unsqueeze(1).to_broadcast([P, heads, half]), ALU.mult))
                for dst in dsts:
                    ins = v.tensor_tensor(dst, rot1[:, 0:n].rearrange("p (h n) -> p h n", h=heads),
                                          rot2[:, 0:n].rearrange("p (h n) -> p h n", h=heads), ALU.add)
                    if done is None:
                        step(ins)
                    else:
                        ins.then_inc(*done[0:2])
                        eng.wait_ge(done[0], done[2])

            norm(0, normed, normed)
            transposed(("memT",))
            seq = opening + mixer_chunks(0)[0:2]
            for key in seq[0:SPLIT]:
                lo_of(key)
            seq = seq[SPLIT:]
            eng.wait_ge(small_loaded, 16 * (NT + 1 + 3 * DEPTH))
            step(v.tensor_copy(pos_f[:, :], pos_i[:, :]))
            for t in range(NT):
                step(v.tensor_scalar(ang[:, 2, t, :], freqs[:, :], pos_f[:, t:t + 1], None, ALU.mult))
            for out_i, quarter in ((0, 0.0), (1, 0.25)):
                r, k = ang[:, out_i, :, :], ang[:, 3 + out_i, :, :]
                step(v.tensor_scalar(k, ang[:, 2, :, :], 0.15915494309189535, quarter, ALU.mult, ALU.add))
                step(v.tensor_scalar(k, k, ROUND, None, ALU.add))
                step(v.tensor_scalar(k, k, ROUND, None, ALU.subtract))
                step(v.scalar_tensor_tensor(r, k, -TWO_PI_HI, ang[:, 2, :, :], ALU.mult, ALU.add))
                step(v.scalar_tensor_tensor(r, k, -TWO_PI_MID, r, ALU.mult, ALU.add))
                step(v.scalar_tensor_tensor(r, k, -TWO_PI_LO, r, ALU.mult, ALU.add))
                if quarter:
                    step(v.tensor_scalar(r, r, 1.5707963267948966, None, ALU.add))
                step(v.tensor_scalar(k, r, PI_BELOW, -6.283185307179586, ALU.is_gt, ALU.mult))
                step(v.tensor_tensor(r, r, k, ALU.add))
                step(v.tensor_scalar(k, r, -PI_BELOW, 6.283185307179586, ALU.is_lt, ALU.mult))
                step(v.tensor_tensor(r, r, k, ALU.add))
                v.tensor_scalar(r, r, PI_BELOW, -PI_BELOW, ALU.min, ALU.max).then_inc(angles_ready, 1)

            for l in range(DEPTH):
                for key in seq[0:5]:
                    lo_of(key)
                if l == 0:
                    wait_full(eng, ("memT", 1, "area"))
                    norm(1, x, normed)
                lo_of(seq[5])
                seq = seq[6:]
                key = ("memv", l)
                wait_full(eng, key)
                v.tensor_copy(vM[:, l, :, :].rearrange("p t n -> p (t n)"), area(key)[:, :]).then_inc(psum_free[3], 1)
                for key in seq[0:2]:
                    lo_of(key)
                seq = seq[2:]
            eng.wait_ge(wr_hi_ready, 1)
            v.tensor_tensor(wr_lo[:, :, :], wr[:, :, :], wr_hi[:, :, :].bitcast(F32), ALU.subtract).then_inc(wr_split, 1)
            eng.wait_ge(trig_ready, 2)
            for cos, sin, f0, half in ((cosA, sinA, 0, A_DIM // 2), (cosB, sinB, A_DIM // 2, B_ROPE // 2)):
                v.tensor_copy(cos[:, :, 0:half], ang[:, 4, :, f0:f0 + half])
                v.tensor_copy(cos[:, :, half:], ang[:, 4, :, f0:f0 + half])
                v.tensor_scalar(sin[:, :, 0:half], ang[:, 3, :, f0:f0 + half], -1.0, None, ALU.mult)
                step(v.tensor_copy(sin[:, :, half:], ang[:, 3, :, f0:f0 + half]))
            for l in range(DEPTH):
                todo = mixer_chunks(l)
                done = [2 if l == 0 else 0]

                def ahead(key, more=3):
                    upto = min(len(todo), todo.index(key) + 1 + more)
                    for k in todo[done[0]:upto]:
                        lo_of(k)
                    done[0] = max(done[0], upto)

                ahead(("qa", l, 0))
                if l:
                    norm(2 * l + 1, x, normed)
                transposed(("hT", 2 * l))
                ahead(("qa", l, 3))
                key = ("qa", l)
                wait_full(eng, key)
                for t in range(NT):
                    rotate(area(key)[:, 512 * t:512 * t + 512].rearrange("p (h n) -> p h n", h=A_HEADS), A_HEADS,
                           A_DIM // 2, cosA[:, t, :], sinA[:, t, :],
                           [qa_rot[:, t, :].rearrange("p (h n) -> p h n", h=A_HEADS)],
                           (qa_ready, 1, l + 1) if t == NT - 1 else None)
                ahead(("kvcq", l, 3))
                key = ("kvcq", l)
                eng.wait_ge(lat_sumsq_ready, 4 * l + 2)
                for t in range(NT):
                    rotate(area(key)[:, 512 * t:512 * t + 128].rearrange("p (h n) -> p h n", h=A_KV), A_KV,
                           A_DIM // 2, cosA[:, t, :], sinA[:, t, :],
                           [k_dup[:, t, :, i, :] for i in range(2)])
                ahead(("ckvkr", l, 1))
                wait_full(eng, ("ckvkr", l))
                eng.wait_ge(lat_sumsq_ready, 4 * (l + 1))
                step(v.tensor_scalar(lat_meansq[:, 0, :], lat_sumsq[:, 0, :], 1.0 / Q_RANK, EPS, ALU.mult, ALU.add))
                v.tensor_scalar(lat_meansq[:, 1, :], lat_sumsq[:, 1, :], 1.0 / KV_RANK, EPS, ALU.mult,
                                ALU.add).then_inc(lat_meansq_ready, 1)
                for t in range(NT):
                    rotate(area(("ckvkr", l))[:, 512 * t + KV_RANK:512 * t + KV_RANK + B_ROPE].unsqueeze(1), 1,
                           B_ROPE // 2, cosB[:, t, :], sinB[:, t, :], [kr_pad[:, t, B_NOPE:].unsqueeze(1)])
                eng.wait_ge(lat_rstd_ready, l + 1)
                eng.wait_ge(v_copied, l + 1)
                for t in range(NT):
                    v.scalar_tensor_tensor(cq_n[:, t, :], area(("kvcq", l))[:, 512 * t + 256:512 * t + 512],
                                           lat_rstd[:, 0, t:t + 1], g_lat[:, l, 0:Q_RANK], ALU.mult, ALU.mult)
                v.scalar_tensor_tensor(ckv_n[:, 0, :], area(("ckvkr", l))[:, 0:KV_RANK],
                                       lat_rstd[:, 1, 0:1], g_lat[:, l, Q_RANK:], ALU.mult, ALU.mult)
                v.scalar_tensor_tensor(ckv_n[:, 1, :], area(("ckvkr", l))[:, 512:512 + KV_RANK],
                                       lat_rstd[:, 1, 1:2], g_lat[:, l, Q_RANK:], ALU.mult, ALU.mult).then_inc(k_ready, 1)
                ahead(("qm", l, 3))
                key = ("T_lat", l)
                eng.wait_ge(hi_copied, tl.after("hi_copied", key))
                step(v.tensor_copy(kaT[:, :, :].rearrange("p h n -> p (h n)"), area(key)[:, 0:512]))
                rest(key, cqT_lo[:, :, :].rearrange("p k n -> p (k n)"), area(key)[:, 512:1024],
                     cqT_hi[:, :, :].rearrange("p k n -> p (k n)"))
                key = ("T_kv", l)
                eng.wait_ge(kr_copied, l + 1)
                rest(key, ckvT_lo[:, :], area(key)[:, 0:TOK], ckvT_hi[:, :])
                ahead(("uq", l, 1))
                for t in range(NT):
                    eng.wait_ge(qb_copied, NT * l + t + 1)
                    rotate(qB[:, t, :, B_NOPE:], B_HEADS, B_ROPE // 2, cosB[:, t, :], sinB[:, t, :],
                           [qB[:, t, :, B_NOPE:]], (qb_ready, 1, NT * l + t + 1))
                ahead(("ukv", l, 0))
                key = ("ukv_v", l)
                wait_full(eng, key)
                v.tensor_copy(vB[:, :, :].rearrange("p t n -> p (t n)"), area(key)[:, :]).then_inc(psum_free[3], 1)
                key = ("T_qb", l, 1)
                wait_full(eng, key)
                v.tensor_copy(qBT[:, 4:8, :].rearrange("p h n -> p (h n)"), area(key)[0:B_QK, :]).then_inc(psum_free[1], 1)

                def maxima(u):
                    kind, j = units[u]
                    key = ("S", l, u)
                    wait_full(eng, key)
                    if kind == "A":
                        if u >= 2:
                            wait_full(eng, ("pT", l, u - 2))
                        v.scalar_tensor_tensor(probs[:, u % 2, :, :, :].rearrange("p h t n -> p h (t n)"),
                                               area(key)[:, :].rearrange("p (h n) -> p h n", h=2), A_DIM ** -0.5,
                                               mask[:, :, :].rearrange("p t n -> p (t n)").unsqueeze(1).to_broadcast([P, 2, NT * TOK]),
                                               ALU.mult, ALU.add).then_inc(psum_free[0], 1)
                        wait_read(eng, key)
                        step(v.tensor_reduce(row_max[:, :], probs[:, u % 2, :, :, :].rearrange("p h t n -> p (h t) n"),
                                             AX.X, ALU.max))
                        both = sink[:, l, 2 * j:2 * j + 2].unsqueeze(2).to_broadcast([P, 2, NT])
                        m22 = row_max[:, :].rearrange("p (h t) -> p h t", h=2)
                        step(v.tensor_tensor(m22, m22, both, ALU.max))
                        step(v.tensor_scalar(neg_max[:, :], row_max[:, :], -1.0, None, ALU.mult))
                        v.tensor_tensor(sink_arg[:, :].rearrange("p (h t) -> p h t", h=2),
                                        neg_max[:, :].rearrange("p (h t) -> p h t", h=2), both,
                                        ALU.add).then_inc(max_ready, 1)
                    else:
                        scale = (B_QK if kind == "B" else M_DIM) ** -0.5
                        step(v.tensor_reduce(row_max[:, :], area(key)[:, :].rearrange("p (q n) -> p q n", q=4),
                                             AX.X, ALU.max))
                        v.tensor_scalar(neg_max[:, :], row_max[:, :], -scale, None, ALU.mult).then_inc(max_ready, 1)

                def normalise(u):
                    kind, j = units[u]
                    eng.wait_ge(exp_done, tl.after("exp_done", (l, u)))
                    if kind == "A":
                        step(v.tensor_tensor(row_sum[:, :], row_sum[:, :], sink_exp[:, :], ALU.add))
                    step(v.reciprocal(inv_sum[:, :], row_sum[:, :]))
                    tile = probs[:, u % 2, :, :, :].rearrange("p h t n -> p (h t) n")
                    v.tensor_tensor(tile, tile, inv_sum[:, :].unsqueeze(2).to_broadcast([P, 4, TOK]),
                                    ALU.mult).then_inc(probs_ready, 1)

                for n_step, st in enumerate(attention_steps()):
                    if 1 <= n_step <= len(units):
                        normalise(n_step - 1)
                    for kind, n in st:
                        if kind == "QK":
                            maxima(n)
                        elif kind == "gate":
                            ahead(("gate", l, *n))
                        elif kind == "PV":
                            key = ("oT", l, n)
                            blk, wide = y_place(n)
                            rest(key, y_lo[:, blk:blk + wide, :].rearrange("p b n -> p (b n)"),
                                 area(key)[:, 0:wide * TOK], y_hi[:, blk:blk + wide, :].rearrange("p b n -> p (b n)"))
                for h in range(2):
                    for i in range(BRANCHES):
                        ahead(("branch", l, h, i, 1))
                        key = ("branch", l, h, i)
                        g = 2 * i + h
                        wait_full(eng, key)
                        eng.wait_ge(gates_ready, 6 * l + g + 1)
                        if i == 0 and h:
                            eng.wait_ge(hi_copied, tl.after("hi_copied", ("mixed", l, 0)))
                        dst = mixed if i == 0 else gated
                        v.tensor_tensor(dst[:, :, :], area(key)[:, :].rearrange("p (a n) -> p a n", a=4),
                                        gates[:, 4 * g:4 * g + 4, :], ALU.mult).then_inc(psum_free[areas[key]], 1)
                        wait_read(eng, key)
                        if i == 1:
                            step(v.tensor_tensor(mixed[:, :, :], mixed[:, :, :], gated[:, :, :], ALU.add))
                        if i == 2:
                            v.tensor_tensor(mixed[:, :, :], mixed[:, :, :], gated[:, :, :], ALU.add).then_inc(mixed_ready, 1)
                    eng.wait_ge(hi_copied, tl.after("hi_copied", ("mixed", l, h)))
                    v.tensor_tensor(mixT_lo[:, 4 * h:4 * h + 4, :], mixed[:, :, :],
                                    mixT_hi[:, 4 * h:4 * h + 4, :].bitcast(F32), ALU.subtract).then_inc(mixed_split, 1)
                    if h == 0:
                        eng.wait_ge(mixed_split, 2 * l + 1)
                for n in range(2):
                    ahead(("out", l, n, 3), 2)
                    if n and l == 0:
                        for key in dense_first[0:2]:
                            lo_of(key)
                    wait_full(eng, ("out", l, n))
                    for t in range(NT):
                        cols = x[:, t, 512 * n:512 * n + 512]
                        v.tensor_tensor(cols, area(("out", l, n))[:, 512 * t:512 * (t + 1)], cols,
                                        ALU.add).then_inc(x_added, 1)
                norm(2 * l + 2, x, normed)
                if l == 0:
                    for key in dense_first[2:SPLIT]:
                        lo_of(key)
                transposed(("hT", 2 * l + 1))

                if l == 0:
                    def product(tag, g, it=0):
                        wait_full(eng, (tag, "U", g), it)
                        eng.wait_ge(silu_done, tl.after("silu_done", (tag, g), it))
                        v.tensor_tensor(act[:, :, :], ps[1][:, :].rearrange("p (a n) -> p a n", a=4), silu[:, :, :],
                                        ALU.mult).then_inc(act_ready, 1)

                    def act_rest(n, pair):
                        eng.wait_ge(hi_copied, n + tl.after("hi_copied", ("dense", 0)))
                        v.tensor_tensor(actT_lo[pair][:, :, :], act[:, :, :], actT_hi[pair][:, :, :].bitcast(F32),
                                        ALU.subtract).then_inc(act_split, 1)

                    for key in dense_first[SPLIT:]:
                        lo_of(key)
                    product("dense", 0)
                    with v.Fori(0, DENSE_TURNS) as it:
                        for tag, kind, g in dense_pair():
                            keys = group_chunks(tag, kind, g)
                            if kind == "GU":
                                for key in keys[0:3]:
                                    lo_of(key, it)
                                act_rest(it * 2 + (g - 1), (g - 1) % 2)
                                for key in keys[3:]:
                                    lo_of(key, it)
                            else:
                                for key in keys[0:3]:
                                    lo_of(key, it)
                                eng.wait_ge(act_split, tl.before("act_split", (tag, g + 1), it))
                                product(tag, g + 1, it)
                                lo_of(keys[3], it)
                    act_rest(GROUPS - 1, (GROUPS - 1) % 2)
                    for key in dense_last:
                        lo_of(key)
                    for t in range(NT):
                        wait_full(eng, ("down", t))
                        v.tensor_tensor(x[:, t, :], ps[2 + t][:, :], x[:, t, :], ALU.add).then_inc(x_added, 1)

            wait_full(eng, ("router",))
            v.tensor_copy(logitsT[:, :], ps[2][0:EXPERTS, 0:TOK]).then_inc(psum_free[2], 1)
            wait_full(eng, ("router_T",))
            eng.wait_ge(routing_constants, 7)
            v.tensor_copy(logits[:, :, :], ps[2][:, 0:NT * EXPERTS].rearrange("p (t n) -> p t n", t=NT)).then_inc(psum_free[2], 1)
            wait_read(eng, ("router_T",))
            for t in range(NT):
                step(v.max(top8[:, t, :], logits[:, t, :]))
                step(v.max_index(top_i[:, t, :], top8[:, t, :], logits[:, t, :]))
            step(v.tensor_copy(top_f[:, :, :], top_i[:, :, :]))
            v.tensor_tensor(pair_d[:, :], top8[:, :, 1], top8[:, :, 0], ALU.subtract).then_inc(diff_ready, 1)
            for r in range(2):
                for t in range(NT):
                    step(v.tensor_scalar(hot[:, r, t, :], iota8[:, :], top_f[:, t, r:r + 1], None, ALU.is_equal))
            v.tensor_tensor(routed[:, :, :], hot[:, 0, :, :], hot[:, 1, :, :], ALU.add).then_inc(masks_ready, 1)
            eng.wait_ge(ratio_ready, 1)
            step(v.tensor_scalar(pair_d[:, :], pair_e[:, :], 1.0, None, ALU.add))
            step(v.reciprocal(pair_w[:, 0, :], pair_d[:, :]))
            step(v.tensor_tensor(pair_w[:, 1, :], pair_w[:, 0, :], pair_e[:, :], ALU.mult))
            for t in range(NT):
                step(v.tensor_scalar(route_w[:, t, :], hot[:, 0, t, :], pair_w[:, 0, t:t + 1], None, ALU.mult))
                step(v.scalar_tensor_tensor(route_w[:, t, :], hot[:, 1, t, :], pair_w[:, 1, t:t + 1], route_w[:, t, :],
                                            ALU.mult, ALU.add))
            wait_full(eng, ("rank",))
            for t in range(NT):
                step(v.tensor_scalar(logits[:, t, :], ps[3][:, EXPERTS * t:EXPERTS * (t + 1)], 1.0, None, ALU.add))
                step(v.tensor_tensor(logits[:, t, :], logits[:, t, :], routed[:, t, :], ALU.mult))
                for turn in range(2):
                    part = route[:, EXPERTS * turn:EXPERTS * (turn + 1), :]
                    step(v.tensor_scalar(part[:, :, t], logits[:, t, :], float(1 + SLOTS * turn), None, ALU.subtract))
                    step(v.tensor_copy(part[:, :, 2 + t], route_w[:, t, :]))
            step(v.tensor_reduce(most[:, :], ps[3][:, NT * EXPERTS:(NT + 1) * EXPERTS], AX.X, ALU.max))
            step(v.tensor_scalar(turns_f[:, :], most[:, :], SLOTS + 0.5, float(EXPERTS), ALU.is_gt, ALU.mult))
            step(v.tensor_scalar(turns_f[:, :], turns_f[:, :], float(EXPERTS), None, ALU.add))
            v.tensor_copy(turns_i[:, :], turns_f[:, :]).then_inc(turns_ready, 1)
            eng.wait_ge(turns_ready, 1)
            turns = v.value_load(turns_i[0:1, 0:1], min_val=EXPERTS, max_val=2 * EXPERTS)

            def slots_of(e, tile_, name, dst, weights):
                v.tensor_copy(tile_[:, :], route[:, bass.ds(e, 1), :].rearrange("p a b -> p (a b)")).then_inc(picked, 1)
                eng.wait_ge(picked, name)
                for t in range(NT):
                    if weights:
                        ins = v.tensor_scalar(dst[:, t, :], iotaS[:, :], tile_[:, t:t + 1], tile_[:, 2 + t:3 + t],
                                              ALU.is_equal, ALU.mult)
                    else:
                        ins = v.tensor_scalar(dst[:, t, :], iotaS[:, :], tile_[:, t:t + 1], None, ALU.is_equal)
                ins.then_inc(routed_sem, 1)

            step(v.tensor_copy(cur_next[:, :], route[:, 0, :]))
            for t in range(NT):
                ins = v.tensor_scalar(onehot[:, t, :], iotaS[:, :], cur_next[:, t:t + 1], None, ALU.is_equal)
            ins.then_inc(routed_sem, 1)

            def add_scattered(e):
                for t in range(NT):
                    key = ("scatter", t)
                    wait_full(eng, key, e)
                    v.tensor_tensor(x[:, t, :], area(key)[:, :], x[:, t, :], ALU.add).then_inc(x_added, 1)

            with v.Fori(0, turns) as e:
                done_m = [0]

                def upto(n):
                    for key in moe_loop[done_m[0]:n]:
                        lo_of(key, e)
                    done_m[0] = max(done_m[0], n)

                def moe_product(g):
                    eng.wait_ge(silu_done, tl.after("silu_done", ("moe", g), e))
                    if g:
                        wait_full(eng, ("moe", "T", g - 1), e)
                    v.tensor_tensor(act_m[:, :], ps[0][:, FF_GROUP:], silu_m[:, :], ALU.mult).then_inc(act_ready, 1)

                def moe_rest(g):
                    rest(("moe", "T", g), actm_lo[g % 2][:, :, :],
                         ps[1][:, 0:FF_GROUP].rearrange("p (a n) -> p a n", a=4), actm_hi[g % 2][:, :, :], e)

                upto(2)
                rest(("gather",), xg_lo[:, :, :].rearrange("p k n -> p (k n)"), ps[3][:, :],
                     xg_hi[:, :, :].rearrange("p k n -> p (k n)"), e)
                upto(before_silu(0))
                moe_product(0)
                upto(before_split(0))
                add_scattered(e)
                moe_rest(0)
                upto(before_split(0) + 2)
                slots_of(e, cur, e * 2 + 1, onehot_w, True)
                upto(before_split(0) + 4)
                slots_of(e + 1, cur_next, e * 2 + 2, onehot, False)
                for g in range(1, GROUPS):
                    upto(before_silu(g))
                    moe_product(g)
                    if g == 1:
                        wait_full(eng, ("T_back",), e)
                        v.tensor_copy(back[:, :], ps[1][:, 0:TOK]).then_inc(psum_free[1], 1)
                    upto(before_split(g))
                    moe_rest(g)
                upto(FFN_CHUNKS)
            add_scattered(turns)

            norm(5, x, normed)

        @block.tensor
        def _(pe):
            mm = nc.tensor.matmul

            def three(o, w_hi, w_lo, a_hi, a_lo, start, stop, stationary):
                for i, (w, a) in enumerate(((w_hi, a_hi), (w_hi, a_lo), (w_lo, a_hi))):
                    lhsT, rhs = (w, a) if stationary else (a, w)
                    ins = mm(o, lhsT, rhs, start=start and i == 0, stop=stop and i == 2, skip_group_check=True)
                return ins

            def wait_chunk(key, it=0):
                pe.wait_ge(chunk_split, chunk_no(key, it) + 1)
                n = slot(key) % SPLIT
                return whi[n], wlo[n]

            def stationary_chunk(key, a_hi, a_lo, out, first, last, it=0):
                hi, lo = wait_chunk(key, it)
                for kk in range(2):
                    for j in range(4):
                        w = slice(512 * kk + P * j, 512 * kk + P * (j + 1))
                        ins = three(out[:, TOK * j:TOK * (j + 1)], hi[:, w], lo[:, w], a_hi(kk), a_lo(kk),
                                    first and kk == 0 and j % 2 == 0, last and kk == 1, True)
                return ins

            def moving_chunk(key, a_hi, a_lo, outs, blocks, width, first, last, it=0):
                hi, lo = wait_chunk(key, it)
                for kk in range(blocks):
                    w = slice(width * kk, width * (kk + 1))
                    for t, o in enumerate(outs):
                        ins = three(o, hi[:, w], lo[:, w], a_hi(kk, t), a_lo(kk, t),
                                    first and kk == 0, last and kk == blocks - 1, False)
                return ins

            def used(ins):
                ins.then_inc(chunk_used, 1)

            def h_at(k):
                return lambda kk: hT_hi[:, k + kk, :], lambda kk: hT_lo[:, k + kk, :]

            def h_tile(k):
                return (lambda kk, t: hT_hi[:, k + kk, P * t:P * (t + 1)],
                        lambda kk, t: hT_lo[:, k + kk, P * t:P * (t + 1)])

            def banks(key, width):
                return [area(key)[:, 512 * t:512 * t + width] for t in range(NT)]

            def transposes(name, n):
                for a in range(2):
                    wait_free(pe, (*name, a, "area"))
                for t in range(NT):
                    pe.wait_ge(norm_done, NT * n + t + 1)
                    for a in range(2):
                        for k in range(4):
                            c = TOK * k + P * t
                            ins = nc.tensor.transpose(ps[a][:, c:c + P],
                                                      normed[:, t, P * (4 * a + k):P * (4 * a + k + 1)], ident[:, :])
                        if t == NT - 1:
                            ins.then_inc(psum_full[a], 1)

            def wait_piece(name, i):
                pe.wait_ge(hT_split, tl.after("hT_split", (*name, i)))

            def stationary_section(keys, full_key, act_of, name=None):
                wait_free(pe, full_key)
                for i, key in enumerate(keys):
                    if name is not None:
                        wait_piece(name, i)
                    used(stationary_chunk(key, *act_of(i), area(full_key), i == 0, i == len(keys) - 1))

            def moving_section(keys, full_key, width, blocks, act_of, name=None):
                wait_free(pe, full_key)
                for i, key in enumerate(keys):
                    if name is not None:
                        wait_piece(name, i)
                    used(moving_chunk(key, *act_of(i), banks(full_key, width), blocks, width, i == 0, i == len(keys) - 1))

            pe.wait_ge(constants, 6)
            transposes(("memT",), 0)
            for l in range(DEPTH):
                stationary_section([("memk", l, c) for c in range(4)], ("memk", l), lambda i: h_at(2 * i), ("memT",))
                moving_section([("memv", l, c) for c in range(4)], ("memv", l), 512, 2, lambda i: h_tile(2 * i))

            for l in range(DEPTH):
                transposes(("hT", 2 * l), 2 * l + 1)
                moving_section([("qa", l, c) for c in range(4)], ("qa", l), 512, 2, lambda i: h_tile(2 * i), ("hT", 2 * l))
                moving_section([("kvcq", l, c) for c in range(4)], ("kvcq", l), 512, 2, lambda i: h_tile(2 * i))
                moving_section([("ckvkr", l, c) for c in range(2)], ("ckvkr", l), KV_RANK + B_ROPE, 4, lambda i: h_tile(4 * i))
                stationary_section([("qm", l, c) for c in range(4)], ("qm", l), lambda i: h_at(2 * i))
                key = ("T_qa", l)
                wait_free(pe, key)
                for j in range(4):
                    for t in range(NT):
                        ins = nc.tensor.transpose(area(key)[:, TOK * j + P * t:TOK * j + P * (t + 1)],
                                                  qa_rot[:, t, P * j:P * (j + 1)], ident[:, :])
                ins.then_inc(psum_full[areas[key]], 1)
                wait_read(pe, ("kvcq", l))
                wait_read(pe, ("ckvkr", l))
                key = ("T_lat", l)
                wait_free(pe, key)
                for kv in range(A_KV):
                    for t in range(NT):
                        nc.tensor.transpose(area(key)[:, TOK * kv + P * t:TOK * kv + P * (t + 1)],
                                            k_dup[:, t, kv, :, :].rearrange("p a n -> p (a n)"), ident[:, :])
                for k in range(2):
                    for t in range(NT):
                        c = 512 + TOK * k + P * t
                        ins = nc.tensor.transpose(area(key)[:, c:c + P], cq_n[:, t, P * k:P * (k + 1)], ident[:, :])
                ins.then_inc(psum_full[areas[key]], 1)
                key = ("T_kv", l)
                wait_free(pe, key)
                pe.wait_ge(constants, 6 + l + 1)
                for t in range(NT):
                    nc.tensor.transpose(area(key)[:, P * t:P * (t + 1)], ckv_n[:, t, :], ident[:, :])
                for t in range(NT):
                    ins = nc.tensor.transpose(area(key)[0:B_QK, 512 + P * t:512 + P * (t + 1)], kr_pad[:, t, :], ident[:, :])
                ins.then_inc(psum_full[areas[key]], 1)
                wait_read(pe, ("T_lat", l))
                for t in range(NT):
                    wait_free(pe, ("uq", l, t))
                for k in range(2):
                    hi, lo = wait_chunk(("uq", l, k))
                    for t in range(NT):
                        for half in range(2):
                            w = slice(4 * B_QK * half, 4 * B_QK * (half + 1))
                            ins = three(area(("uq", l, t))[:, 512 * half:512 * half + 4 * B_QK], hi[:, w], lo[:, w],
                                        cqT_hi[:, k, P * t:P * (t + 1)], cqT_lo[:, k, P * t:P * (t + 1)], k == 0, k == 1, False)
                    used(ins)
                hi, lo = wait_chunk(("ukv", l, 0))
                wait_read(pe, ("T_kv", l))
                for a in range(2):
                    key = ("ukv_k", l, a)
                    wait_free(pe, key)
                    for j in range(4):
                        w = slice(P * (4 * a + j), P * (4 * a + j + 1))
                        ins = three(area(key)[:, TOK * j:TOK * (j + 1)], hi[:, w], lo[:, w], ckvT_hi[:, :], ckvT_lo[:, :],
                                    True, True, True)
                    ins.then_inc(psum_full[areas[key]], 1)
                key = ("ukv_v", l)
                wait_free(pe, key)
                values = [w[:, :].rearrange("p (h n) -> p h n", h=B_HEADS)[:, :, B_NOPE:] for w in (hi, lo)]
                for t in range(NT):
                    ins = three(area(key)[:, 512 * t:512 * (t + 1)].rearrange("p (h n) -> p h n", h=B_HEADS), *values,
                                ckvT_hi[:, P * t:P * (t + 1)], ckvT_lo[:, P * t:P * (t + 1)], True, True, False)
                used(ins)
                for a in range(2):
                    key = ("T_qb", l, a)
                    wait_free(pe, key)
                    pe.wait_ge(qb_ready, NT * (l + 1))
                    for j in range(4):
                        for t in range(NT):
                            c = TOK * j + P * t
                            ins = nc.tensor.transpose(area(key)[0:B_QK, c:c + P], qB[:, t, 4 * a + j, :], ident[:, :])
                    ins.then_inc(psum_full[areas[key]], 1)

                def scores(u):
                    kind, j = units[u]
                    key = ("S", l, u)
                    wait_free(pe, key)
                    if u == 0:
                        for k in (("T_qa", l), ("T_lat", l), ("T_qb", l, 0), ("T_qb", l, 1), ("ukv_k", l, 0),
                                  ("ukv_k", l, 1), ("ukv_v", l), ("qm", l)):
                            wait_read(pe, k)
                    for h in range(2):
                        head = 2 * j + h
                        for t in range(NT):
                            o = area(key)[:, TOK * (NT * h + t):TOK * (NT * h + t + 1)]
                            tt = slice(P * t, P * (t + 1))
                            if kind == "A":
                                r = slice(A_DIM * h, A_DIM * (h + 1))
                                ins = mm(o, qaT[r, j, tt], kaT[r, j // 2, :], start=True, stop=True)
                            elif kind == "B":
                                ins = mm(o, qBT[:, head, tt], kBT[:, head, :], start=True, stop=True)
                            else:
                                ins = mm(o, qMT[:, head, tt], kM[:, l, head, :], start=True, stop=True)
                    ins.then_inc(psum_full[0], 1)

                def turn(u):
                    key = ("pT", l, u)
                    pe.wait_ge(probs_ready, l * len(units) + u + 1)
                    wait_free(pe, key)
                    for h in range(2):
                        for kt in range(NT):
                            for t in range(NT):
                                c = TOK * (NT * h + kt) + P * t
                                ins = nc.tensor.transpose(area(key)[:, c:c + P], probs[:, u % 2, h, t, P * kt:P * (kt + 1)], ident[:, :])
                    ins.then_inc(psum_full[1], 1)

                def values_of(u):
                    kind, j = units[u]
                    key = ("oT", l, u)
                    wait_free(pe, key)
                    wait_read(pe, ("pT", l, u))
                    for h in range(2):
                        head = 2 * j + h
                        for kt in range(NT):
                            if kind == "M":
                                o, lhsT = area(key)[:, TOK * h:TOK * (h + 1)], vM[:, l, kt, M_DIM * head:M_DIM * (head + 1)]
                            else:
                                o = area(key)[64 * h:64 * (h + 1), 0:TOK]
                                c = A_DIM * (j // 2) if kind == "A" else B_V * head
                                lhsT = (vA if kind == "A" else vB)[:, kt, c:c + 64]
                            ins = mm(o, lhsT, pT[:, h, kt, :], start=kt == 0, stop=kt == NT - 1)
                    ins.then_inc(psum_full[2], 1)

                for step in attention_steps():
                    for kind, n in step:
                        if kind == "QK":
                            scores(n)
                        elif kind == "PV":
                            values_of(n)
                        elif kind == "T":
                            turn(n)
                        else:
                            g, c = n
                            key = ("gate", l, g)
                            if c == 0:
                                wait_free(pe, key)
                            used(stationary_chunk(("gate", l, g, c), *h_at(2 * c), area(key), c == 0, c == 3))

                for h in range(2):
                    for i in range(BRANCHES):
                        wait_read(pe, ("oT", l, len(units) - 1))
                        stationary_section([("branch", l, h, i, c) for c in range(2)], ("branch", l, h, i),
                                           lambda c: (lambda kk: y_hi[:, 4 * i + 2 * c + kk, :],
                                                      lambda kk: y_lo[:, 4 * i + 2 * c + kk, :]))
                for n in range(2):
                    wait_free(pe, ("out", l, n))
                for part in range(2):
                    pe.wait_ge(mixed_split, 2 * l + part + 1)
                    for n in range(2):
                        for c in (2 * part, 2 * part + 1):
                            used(moving_chunk(("out", l, n, c), lambda kk, t: mixT_hi[:, 2 * c + kk, P * t:P * (t + 1)],
                                              lambda kk, t: mixT_lo[:, 2 * c + kk, P * t:P * (t + 1)],
                                              banks(("out", l, n), 512), 2, 512, c == 0, c == 3))
                transposes(("hT", 2 * l + 1), 2 * l + 2)

                if l == 0:
                    pe.wait_ge(zeros_ready, 1)
                    for t in range(NT):
                        wait_free(pe, ("down", t))
                        for half in range(2):
                            mm(ps[2 + t][:, 512 * half:512 * (half + 1)], zeros[0:1, 0:P], zeros[0:1, :], start=True,
                               stop=False, skip_group_check=True)

                    def up(tag, g, it=0):
                        for which, a, freed, name in (("G", 0, silu_done, "silu_done"), ("U", 1, act_ready, "act_ready")):
                            if tag == "dense":
                                wait_free(pe, (tag, which, g))
                            else:
                                pe.wait_ge(freed, tl.before(name, (tag, g), it))
                            for c in range(4):
                                if tag == "dense":
                                    wait_piece(("hT", 1), c)
                                used(stationary_chunk((tag, which, g, c), *h_at(2 * c), ps[a], c == 0, c == 3, it))

                    def down(tag, g, pair, splits, it=0):
                        pe.wait_ge(act_split, splits)
                        for j in range(4):
                            hi, lo = wait_chunk((tag, "D", g, j), it)
                            for t in range(NT):
                                for half in range(2):
                                    w = slice(512 * half, 512 * (half + 1))
                                    ins = three(ps[2 + t][:, w], hi[:, w], lo[:, w],
                                                actT_hi[pair][:, j, P * t:P * (t + 1)], actT_lo[pair][:, j, P * t:P * (t + 1)],
                                                False, g == "last" and j == 3, False)
                            used(ins)

                    up("dense", 0)
                    with nc.tensor.Fori(0, DENSE_TURNS) as it:
                        for tag, kind, g in dense_pair():
                            if kind == "GU":
                                up(tag, g, it)
                            else:
                                down(tag, g, g % 2, it * 2 + (g + 1), it)
                    down("dense", "last", (GROUPS - 1) % 2, GROUPS)

            pe.wait_ge(wr_split, 1)
            wait_free(pe, ("router",))
            for k in range(KD):
                if k % 2 == 0:
                    wait_piece(("hT", 3), k // 2)
                ins = three(ps[2][0:EXPERTS, 0:TOK], wr_hi[:, k, :], wr_lo[:, k, :], hT_hi[:, k, :], hT_lo[:, k, :],
                            k == 0, k == KD - 1, True)
            ins.then_inc(psum_full[2], 1)
            wait_free(pe, ("router_T",))
            for t in range(NT):
                ins = nc.tensor.transpose(ps[2][:, EXPERTS * t:EXPERTS * (t + 1)], logitsT[:, P * t:P * (t + 1)],
                                          ident[0:EXPERTS, 0:EXPERTS])
            ins.then_inc(psum_full[2], 1)
            pe.wait_ge(masks_ready, 1)
            wait_free(pe, ("rank",))
            mm(ps[3][:, 0:8], earlier[:, :], routed[:, 0, :], start=True, stop=True)
            mm(ps[3][:, 8:16], ones[:, :], routed[:, 0, :], start=True, stop=False)
            mm(ps[3][:, 8:16], earlier[:, :], routed[:, 1, :], start=False, stop=True)
            mm(ps[3][:, 16:24], ones[:, :], routed[:, 0, :], start=True, stop=False)
            mm(ps[3][:, 16:24], ones[:, :], routed[:, 1, :], start=False, stop=True).then_inc(psum_full[3], 1)
            wait_free(pe, ("zero",))
            for half in range(2):
                ins = mm(ps[2][:, 512 * half:512 * (half + 1)], zeros_m[0:1, 0:P], zeros_m[0:1, :], start=True, stop=True)
            ins.then_inc(psum_full[2], 1)

            def gather():
                for k in range(KD):
                    for t in range(NT):
                        ins = mm(ps[3][:, SLOTS * k:SLOTS * (k + 1)], normed[:, t, P * k:P * (k + 1)], onehot[:, t, :],
                                 start=t == 0, stop=t == NT - 1)
                ins.then_inc(psum_full[3], 1)

            def scatter(e):
                pe.wait_ge(y_copied, e + 1)
                for t in range(NT):
                    for half in range(2):
                        w = slice(512 * half, 512 * (half + 1))
                        ins = mm(area(("scatter", t))[:, w], back[:, P * t:P * (t + 1)], y_sb[:, w], start=True, stop=True)
                    ins.then_inc(psum_full[areas["scatter", t]], 1)

            pe.wait_ge(turns_ready, 1)
            pe.wait_ge(routed_sem, 1)
            gather()
            turns = nc.tensor.value_load(turns_i[0:1, 0:1], min_val=EXPERTS, max_val=2 * EXPERTS)

            with nc.tensor.Fori(0, turns) as e:
                pe.wait_ge(psum_free[3], tl.after("psum_free3", ("gather",), e))

                def transposed_act(g):
                    key = ("moe", "T", g)
                    pe.wait_ge(act_ready, tl.after("act_ready", ("moe", g), e))
                    wait_free_in_loop(pe, key, e)
                    for j in range(4):
                        ins = nc.tensor.transpose(ps[1][:, P * j:P * (j + 1)], act_m[:, P * j:P * (j + 1)], ident[:, :])
                    ins.then_inc(psum_full[1], 1)

                for kind, g in group_order():
                    if kind == "GU":
                        if g:
                            pe.wait_ge(act_ready, tl.after("act_ready", ("moe", g - 1), e))
                        for which in "GU":
                            o = ps[0][:, 0:FF_GROUP] if which == "G" else ps[0][:, FF_GROUP:]
                            for c in range(4):
                                ins = moving_chunk(("moe", which, g, c), lambda kk, t: xg_hi[:, 2 * c + kk, :],
                                                   lambda kk, t: xg_lo[:, 2 * c + kk, :], [o], 2, 512, c == 0, c == 3, e)
                                used(ins)
                        if g == 0:
                            scatter(e)
                            transposed_act(0)
                        if g == 1:
                            pe.wait_ge(routed_sem, tl.after("routed", "onehot_w", e))
                            wait_free_in_loop(pe, ("T_back",), e)
                            for t in range(NT):
                                ins = nc.tensor.transpose(ps[1][:, P * t:P * (t + 1)], onehot_w[:, t, :], ident[:, :])
                            ins.then_inc(psum_full[1], 1)
                    else:
                        wait_read(pe, ("moe", "T", g), e)
                        if g == 0:
                            pe.wait_ge(x_added, tl.after("x_added", ("scatter", 1), e))
                        for j in range(4):
                            hi, lo = wait_chunk(("moe", "D", g, j), e)
                            for half in range(2):
                                w = slice(512 * half, 512 * (half + 1))
                                ins = three(ps[2][:, w], hi[:, w], lo[:, w], actm_hi[g % 2][:, j, :],
                                            actm_lo[g % 2][:, j, :], g == 0 and j == 0, g == GROUPS - 1 and j == 3, False)
                            used(ins)
                        if g + 1 < GROUPS:
                            transposed_act(g + 1)
                        if g + 2 == GROUPS:
                            pe.wait_ge(routed_sem, tl.after("routed", "onehot", e))
                            gather()
            scatter(turns)


INPUTS = ["x", "mem", "positions", "g_mix", "w_in", "g_q_lat", "w_uq", "g_kv_lat", "w_ukv", "sink", "w_mem_kv",
          "w_branch", "w_out", "g_ffn", "w_gate_dense", "w_up_dense", "w_down_dense", "w_router", "w_gate_exp",
          "w_up_exp", "w_down_exp", "g_mem", "g_final"]


def kernel(**inputs):
    import numpy as np
    import concourse.bacc as bacc
    from concourse.bass_utils import run_bass_kernel_spmd

    nc = bacc.Bacc("TRN2", target_bir_lowering=False, num_devices=1)
    arrays, args = {}, {}
    freqs = []
    for dim in (A_DIM, B_ROPE):
        exponent = -np.arange(dim // 2, dtype=np.float32) * np.float32(2.0 / dim)
        freqs.append(np.power(np.float64(THETA), exponent.astype(np.float64)).astype(np.float32))
    arrays["inv_freq"] = np.concatenate(freqs)
    for name in INPUTS:
        arrays["in_" + name] = np.ascontiguousarray(inputs[name])
    for name, a in arrays.items():
        args[name] = nc.dram_tensor(name, a.shape, mybir.dt.from_np(a.dtype), kind="ExternalInput").ap()
    out = nc.dram_tensor("out", (1, TOK, D), F32, kind="ExternalOutput").ap()
    trunk_kernel(nc, {n: args["in_" + n] for n in INPUTS}, args["inv_freq"], out)
    r = run_bass_kernel_spmd(nc, [arrays], core_ids=[0])
    return r.results[0]["out"]
```

```python
from contextlib import ExitStack

import concourse.bass as bass
from concourse import mybir

F32 = mybir.dt.float32
F32R = mybir.dt.float32r
I32 = mybir.dt.int32
U32 = mybir.dt.uint32
ALU = mybir.AluOpType
ACT = mybir.ActivationFunctionType
AX = mybir.AxisListType

P = 128
TOK = 256
NT = TOK // P
D = 1024
KD = D // P
DEPTH = 2
A_HEADS, A_KV, A_DIM = 8, 2, 64
B_HEADS, B_NOPE, B_ROPE, B_V = 8, 64, 32, 64
B_QK = B_NOPE + B_ROPE
Q_RANK, KV_RANK = 256, 128
M_HEADS, M_DIM = 4, 128
D_FF = 3584
FF_GROUP = 512
GROUPS = D_FF // FF_GROUP
EXPERTS = 8
SLOTS = 128
BRANCHES = 3
EPS = 1e-6
MASKED = -1e30
THETA = 10000.0

COL_QA = 0
COL_KVCQ = A_HEADS * A_DIM
COL_CKVKR = COL_KVCQ + 2 * A_KV * A_DIM + Q_RANK
COL_QM = COL_CKVKR + KV_RANK + B_ROPE
COL_GATES = COL_QM + M_HEADS * M_DIM

CHUNK = 1024
RAW = 6
DEEP = 21
LATE = 3
SPLIT = 4
FFN_CHUNKS = 3 * GROUPS * 4
PAIR_CHUNKS = 24
assert FFN_CHUNKS % DEEP == 0 and FFN_CHUNKS % SPLIT == 0
assert PAIR_CHUNKS % RAW == 0 and PAIR_CHUNKS % SPLIT == 0

TWO_PI_HI = 6.28125
TWO_PI_MID = 0.0019350051879882812
TWO_PI_LO = 3.01991598196e-07
ROUND = 12582912.0
PI_BELOW = 3.1415925


class Tally:

    def __init__(self):
        self.count = {}
        self.events = {}
        self.body = None

    def add(self, name, key, n=1):
        self.count[name] = self.count.get(name, 0) + n
        self.events[name, key] = [self.count[name], 0, 1]
        if self.body is not None:
            self.body.append((name, key))

    def enter_loop(self):
        self.body, self.start = [], dict(self.count)

    def leave_loop(self, times):
        per = {n: c - self.start.get(n, 0) for n, c in self.count.items()}
        for name, key in self.body:
            self.events[name, key][1:] = per[name], times
        for n, c in per.items():
            self.count[n] += c * (times - 1)
        self.body = None

    def after(self, name, key, it=0):
        base, per, _ = self.events[name, key]
        return base + it * per

    def last(self, name, key):
        base, per, times = self.events[name, key]
        return base + (times - 1) * per

    def before(self, name, key, it=0):
        return self.after(name, key, it) - 1



def mixer_chunks(l):
    return ([("qa", l, c) for c in range(4)] + [("kvcq", l, c) for c in range(4)]
            + [("ckvkr", l, c) for c in range(2)] + [("qm", l, c) for c in range(4)]
            + [("uq", l, c) for c in range(2)] + [("ukv", l, 0)]
            + [("gate", l, g, c) for g in range(6) for c in range(4)]
            + [("branch", l, h, i, c) for h in range(2) for i in range(BRANCHES) for c in range(2)]
            + [("out", l, n, c) for part in range(2) for n in range(2) for c in (2 * part, 2 * part + 1)])


def group_order():
    steps = [("GU", 0)]
    for g in range(1, GROUPS):
        steps += [("GU", g), ("D", g - 1)]
    return steps + [("D", GROUPS - 1)]


def group_chunks(tag, kind, g):
    if kind == "GU":
        return [(tag, "G", g, c) for c in range(4)] + [(tag, "U", g, c) for c in range(4)]
    return [(tag, "D", g, c) for c in range(4)]


def build_tally():
    tl = Tally()
    areas, full_by, free_by, prior, latest = {}, {}, {}, {}, {}

    def psum(key, area, full=None, free=None):
        areas[key] = area
        if full is None:
            full = (f"psum_full{area}", key)
            tl.add(*full)
        if free is None:
            free = (f"psum_free{area}", key)
            tl.add(*free)
        full_by[key], free_by[key] = full, free
        prior[key], latest[area] = latest.get(area), key

    def split(key, area, full=None):
        psum(key, area, full)
        tl.add("hi_copied", key)

    tiles, experts_from = {}, [0]

    def chunks(keys):
        for key in keys:
            n = tl.count.get("chunk", 0)
            if key[0] == "moe":
                n = (n - experts_from[0]) % DEEP
                own = DEEP - RAW - LATE
                if n < own:
                    tiles[key] = RAW + n
                elif n < own + RAW:
                    tiles[key] = (experts_from[0] + n - own) % RAW
                else:
                    tiles[key] = n
            else:
                tiles[key] = n % RAW
            tl.add("chunk", key)
            tl.add(f"loaded{tiles[key]}", key)
        return "chunk", keys[-1]

    def transposed(name):
        for a in range(2):
            for half in range(2):
                tl.add("hi_copied", (*name, 2 * a + half))
                tl.add("hT_split", (*name, 2 * a + half))
            psum((*name, a, "area"), a, free=("hT_split", (*name, 2 * a + 1)))

    transposed(("memT",))
    for l in range(DEPTH):
        psum(("memk", l), 2, full=chunks([("memk", l, c) for c in range(4)]))
        psum(("memv", l), 3, full=chunks([("memv", l, c) for c in range(4)]))
    for l in range(DEPTH):
        keys = mixer_chunks(l)
        chunks(keys)
        last = {key[0]: ("chunk", key) for key in keys}
        transposed(("hT", 2 * l))
        tl.add("qa_ready", l)
        tl.add("k_ready", l)
        psum(("qa", l), 2, last["qa"], ("qa_ready", l))
        psum(("kvcq", l), 3, last["kvcq"], ("k_ready", l))
        psum(("ckvkr", l), 0, last["ckvkr"], ("k_ready", l))
        psum(("qm", l), 1, last["qm"])
        psum(("T_qa", l), 2)
        split(("T_lat", l), 1)
        split(("T_kv", l), 2)
        for t in range(NT):
            tl.add("qb_copied", (l, t))
            psum(("uq", l, t), (3, 0)[t], last["uq"], ("qb_copied", (l, t)))
        psum(("ukv_k", l, 0), 1)
        psum(("ukv_k", l, 1), 2)
        psum(("ukv_v", l), 3, last["ukv"])
        psum(("T_qb", l, 0), 0)
        psum(("T_qb", l, 1), 1)
        for step in attention_steps():
            for kind, n in step:
                if kind == "QK":
                    a_unit = attention_units()[n][0] == "A"
                    tl.add("exp_done", (l, n), 5 if a_unit else 4)
                    psum(("S", l, n), 0, free=None if a_unit else ("exp_done", (l, n)))
                elif kind == "T":
                    psum(("pT", l, n), 1)
                elif kind == "PV":
                    split(("oT", l, n), 2)
                elif kind == "gate" and n[1] == 3:
                    psum(("gate", l, n[0]), 3, ("chunk", ("gate", l, *n)))
        for h in range(2):
            for i in range(BRANCHES):
                psum(("branch", l, h, i), (h * BRANCHES + i) % 2, ("chunk", ("branch", l, h, i, 1)))
            tl.add("hi_copied", ("mixed", l, h))
        for n in range(2):
            for t in range(NT):
                tl.add("x_added", ("out", l, n, t))
                full_by["out", l, n, t] = ("chunk", ("out", l, n, 3))
            psum(("out", l, n), 2 + n, ("chunk", ("out", l, n, 3)), ("x_added", ("out", l, n, NT - 1)))
        full_by["out", l, 1, 0] = ("psum_full3", ("out", l, 1, 0))
        tl.add("psum_full3", ("out", l, 1, 0))
        transposed(("hT", 2 * l + 1))
        if l == 0:
            def dense_step(kind, g, tag):
                last_chunk = chunks(group_chunks(tag, kind, g))
                if kind == "GU":
                    for name in ("silu_done", "act_ready", "hi_copied", "act_split"):
                        tl.add(name, (tag, g))
                    psum((tag, "G", g), 0, ("chunk", (tag, "G", g, 3)), ("silu_done", (tag, g)))
                    psum((tag, "U", g), 1, last_chunk, ("act_ready", (tag, g)))
                return last_chunk

            dense_step("GU", 0, "dense")
            tl.enter_loop()
            for tag, kind, g in dense_pair():
                dense_step(kind, g, tag)
            tl.leave_loop((GROUPS - 1) // 2)
            last_chunk = dense_step("D", "last", "dense")
            for t in range(NT):
                for half in range(2):
                    tl.add("x_added", ("down", t, half))
                    if t == NT - 1 and half == 1:
                        full_by["down", t, half] = last_chunk
                    else:
                        full_by["down", t, half] = (f"psum_full{2 + t}", ("down", t, half))
                        tl.add(*full_by["down", t, half])
                psum(("down", t), 2 + t, last_chunk, ("x_added", ("down", t, 1)))
        else:
            psum(("router",), 2)
            psum(("router_T",), 2)
            tl.add("turns_ready", "turns")
            psum(("rank",), 3, free=("turns_ready", "turns"))
            tl.add("routed", "first")
            for half in range(2):
                tl.add("psum_full3", ("gathered", "first", half))
            experts_from[0] = tl.count["chunk"]
            tl.enter_loop()
            for half in range(2):
                areas["gather", half] = 3
                tl.add("hi_copied", ("gather", half))
                tl.add("psum_free3", ("gather", half))
            tl.add("routed", "onehot")
            tl.add("routed", "onehot_next")
            for kind, g in group_order():
                last_chunk = chunks(group_chunks("moe", kind, g))
                if kind == "GU":
                    tl.add("silu_done", ("moe", g))
                    tl.add("act_ready", ("moe", g))
                    psum(("moe", "GU", g), 0, last_chunk, ("act_ready", ("moe", g)))
                    if g == 0:
                        for t in range(NT):
                            tl.add("x_added", ("scatter", t))
                            psum(("scatter", t), (3, 2)[t], free=("x_added", ("scatter", t)))
                        split(("moe", "T", 0), 1)
                    if g == 1:
                        psum(("T_back",), 1)
                elif g + 1 < GROUPS:
                    split(("moe", "T", g + 1), 1)
            for half in range(2):
                tl.add("psum_full3", ("gathered", "next", half))
            tl.leave_loop(EXPERTS)
    return tl, areas, full_by, free_by, prior, tiles


def dense_pair():
    return [("pair", "GU", 1), ("pair", "D", 0), ("pair", "GU", 2), ("pair", "D", 1)]


def before_silu(g):
    return order_index("GU", g) + 8 + SPLIT - 1


def before_split(g):
    return order_index("GU", 0) + 8 + SPLIT if g == 0 else order_index("D", g - 1) + 4 + SPLIT - 1


def order_index(kind, g):
    steps = group_order()
    return sum(8 if k == "GU" else 4 for k, _ in steps[:steps.index((kind, g))])


def attention_units():
    return [("A", j) for j in range(4)] + [("B", j) for j in range(4)] + [("M", j) for j in range(2)]


def y_place(u):
    kind, j = attention_units()[u]
    return {"A": (j, 1), "B": (4 + j, 1), "M": (8 + 2 * j, 2)}[kind]


def attention_steps():
    gates = [(g, c) for g in range(6) for c in range(4)]
    n = len(attention_units())
    steps = []
    for u in range(n + 2):
        step = []
        if u < n:
            step.append(("QK", u))
        if gates:
            step.append(("gate", gates.pop(0)))
        if u >= 2:
            step.append(("PV", u - 2))
        if 1 <= u <= n:
            step.append(("T", u - 1))
        if gates:
            step.append(("gate", gates.pop(0)))
        steps.append(step)
    assert not gates
    return steps


def trunk_kernel(nc, A, inv_freq, out):
    tl, areas, full_by, free_by, prior, tiles = build_tally()
    units = attention_units()

    with ExitStack() as ctx:
        def sem(name):
            return ctx.enter_context(nc.semaphore(name))

        def sb_in(scope):
            return lambda name, shape, dt=F32: scope.enter_context(nc.sbuf_tensor(name, shape, dt))

        sb = sb_in(ctx)

        raw = [sb(f"raw{i}", [P, CHUNK]) for i in range(RAW)]
        whi = [sb(f"whi{i}", [P, CHUNK], F32R) for i in range(SPLIT)]
        wlo = [sb(f"wlo{i}", [P, CHUNK], F32R) for i in range(SPLIT)]
        x = sb("x", [P, NT, D])
        gain = sb("gain", [P, D])
        kM = sb("kM", [P, DEPTH, M_HEADS, TOK])
        vM = sb("vM", [P, DEPTH, NT, M_HEADS * M_DIM])
        wr_hi = sb("wr_hi", [P, KD, EXPERTS], F32R)
        wr_lo = sb("wr_lo", [P, KD, EXPERTS], F32R)
        ident = sb("ident", [P, P])
        mask = sb("mask", [P, NT, TOK])
        freqs = sb("freqs", [P, 48])
        pos_i = sb("pos_i", [P, NT], I32)
        pos_f = sb("pos_f", [P, NT])
        cosA = sb("cosA", [P, NT, A_DIM])
        sinA = sb("sinA", [P, NT, A_DIM])
        cosB = sb("cosB", [P, NT, B_ROPE])
        sinB = sb("sinB", [P, NT, B_ROPE])
        ang = sb("ang", [P, 5, NT, 48])
        meansq = sb("meansq", [P, NT])
        rstd = sb("rstd", [P, NT])
        power = sb("power", [P, 4])
        g_lat = sb("g_lat", [P, DEPTH, Q_RANK + KV_RANK])
        sink = sb("sink", [P, DEPTH, A_HEADS])
        lat_sumsq = sb("lat_sumsq", [P, 2, NT])
        lat_meansq = sb("lat_meansq", [P, 2, NT])
        lat_rstd = sb("lat_rstd", [P, 2, NT])
        row_max = sb("row_max", [P, 4])
        neg_max = sb("neg_max", [P, 4])
        sink_arg = sb("sink_arg", [P, 4])
        sink_exp = sb("sink_exp", [P, 4])
        row_sum = sb("row_sum", [P, 4])
        inv_sum = sb("inv_sum", [P, 4])
        sumsq = sb("sumsq", [P, 2, NT])

        trunk = ExitStack()
        sb = sb_in(trunk)
        hT_hi = sb("hT_hi", [P, KD, TOK], F32R)
        hT_lo = sb("hT_lo", [P, KD, TOK], F32R)
        gates = sb("gates", [P, BRANCHES * KD, TOK])
        normed = gates[:, 0:8, :].rearrange("p (t a) n -> p t (a n)", t=NT)
        junk = gates[:, 8:16, :].rearrange("p (t a) n -> p t (a n)", t=NT)
        wr = gates[:, BRANCHES * KD - 1, 0:KD * EXPERTS].rearrange("p (k e) -> p k e", k=KD)
        mixer = ExitStack()
        sb = sb_in(mixer)
        y_hi = sb("y_hi", [P, 12, TOK], F32R)
        y_lo = sb("y_lo", [P, 12, TOK], F32R)

        attn = ExitStack()
        sb = sb_in(attn)
        qaT = sb("qaT", [P, 4, TOK])
        kaT = sb("kaT", [P, A_KV, TOK])
        vA = sb("vA", [P, NT, A_KV * A_DIM])
        cqT_hi = sb("cqT_hi", [P, 2, TOK], F32R)
        cqT_lo = sb("cqT_lo", [P, 2, TOK], F32R)
        ckvT_hi = sb("ckvT_hi", [P, TOK], F32R)
        ckvT_lo = sb("ckvT_lo", [P, TOK], F32R)
        qBT = sb("qBT", [B_QK, B_HEADS, TOK])
        kBT = sb("kBT", [B_QK, B_HEADS, TOK])
        vB = sb("vB", [P, NT, B_HEADS * B_V])
        qMT = sb("qMT", [P, M_HEADS, TOK])
        rows = ExitStack()
        sb = sb_in(rows)
        qa_rot = sb("qa_rot", [P, NT, A_HEADS * A_DIM])
        cq_n = sb("cq_n", [P, NT, Q_RANK])
        kr_pad = sb("kr_pad", [P, NT, B_QK])
        qB = sb("qB", [P, NT, B_HEADS, B_QK])
        rows.close()
        sb = sb_in(attn)
        probs = sb("probs", [P, 2, 2, NT, TOK])
        pT = sb("pT", [P, 2, NT, TOK])
        rot1 = gates[:, 16:18, :].rearrange("p a n -> p (a n)")
        rot2 = gates[:, 18:20, :].rearrange("p a n -> p (a n)")
        k_dup = gates[:, 20:22, :].rearrange("p t (k a n) -> p t k a n", k=A_KV, a=2)
        ckv_n = gates[:, 22, :].rearrange("p (t n) -> p t n", t=NT)
        attn.close()

        mixing = ExitStack()
        sb = sb_in(mixing)
        mixed = sb("mixed", [P, 4, TOK])
        gated = sb("gated", [P, 4, TOK])
        mixT_hi = sb("mixT_hi", [P, KD, TOK], F32R)
        mixT_lo = sb("mixT_lo", [P, KD, TOK], F32R)
        mixing.close()

        ffn = ExitStack()
        sb = sb_in(ffn)
        silu = sb("silu", [P, 4, TOK])
        act = sb("act", [P, 4, TOK])
        actT_hi = [sb(f"actT_hi{i}", [P, 4, TOK], F32R) for i in range(2)]
        actT_lo = [sb(f"actT_lo{i}", [P, 4, TOK], F32R) for i in range(2)]
        zeros = sb("zeros", [1, FF_GROUP])
        ffn.close()
        mixer.close()
        trunk.close()

        moe = ExitStack()
        sb = sb_in(moe)
        in_rows = [sb(f"raw{i}", [P, CHUNK]) for i in range(DEEP - LATE, DEEP)]
        y_out_hi = sb("y_out_hi", [P, D], F32R)
        normed_lo = sb("normed_lo", [P, NT, D], F32R)
        normed_hi = sb("normed_hi", [P, NT, D], F32R)
        in_gates = [sb(f"raw{i}", [P, CHUNK]) for i in range(DEEP - LATE - 2, DEEP - LATE)]
        raw += [sb(f"raw{i}", [P, CHUNK]) for i in range(RAW, RAW + 6)]
        raw += [kM[:, l, :, :].rearrange("p h n -> p (h n)") for l in range(DEPTH)]
        raw += [vM[:, l, :, :].rearrange("p t n -> p (t n)") for l in range(DEPTH)]
        raw += in_gates + in_rows
        assert len(raw) == DEEP
        logitsT = sb("logitsT", [EXPERTS, TOK])
        logits = sb("logits", [P, NT, EXPERTS])
        top8 = sb("top8", [P, NT, 8])
        top_i = sb("top_i", [P, NT, 8], U32)
        top_f = sb("top_f", [P, NT, 8])
        pair_e = sb("pair_e", [P, NT])
        pair_d = sb("pair_d", [P, NT])
        pair_w = sb("pair_w", [P, 2, NT])
        hot = sb("hot", [P, 2, NT, EXPERTS])
        routed = sb("routed", [P, NT, EXPERTS])
        route_w = sb("route_w", [P, NT, EXPERTS])
        earlier = sb("earlier", [P, P])
        ones = sb("ones", [P, P])
        iota8 = sb("iota8", [P, EXPERTS])
        iotaS = sb("iotaS", [P, SLOTS])
        route = sb("route", [P, 2 * EXPERTS + 1, 4])
        cur = sb("cur", [P, 4])
        cur_next = sb("cur_next", [P, 4])
        y_out_lo = sb("y_out_lo", [P, D], F32R)
        most = sb("most", [P, 1])
        turns_f = sb("turns_f", [P, 1])
        turns_i = sb("turns_i", [P, 1], I32)
        onehot = sb("onehot", [P, NT, SLOTS])
        onehot_next = sb("onehot_next", [P, NT, SLOTS], F32R)
        back = sb("back", [P, TOK], F32R)
        slot_w = sb("slot_w", [P, 1])
        xg_hi = sb("xg_hi", [P, KD, SLOTS], F32R)
        xg_lo = sb("xg_lo", [P, KD, SLOTS], F32R)
        silu_m = sb("silu_m", [P, FF_GROUP])
        act_m = sb("act_m", [P, FF_GROUP])
        actm_hi = [sb(f"actm_hi{i}", [P, 4, SLOTS], F32R) for i in range(2)]
        actm_lo = [sb(f"actm_lo{i}", [P, 4, SLOTS], F32R) for i in range(2)]
        moe.close()

        ps = [ctx.enter_context(nc.psum_tensor(f"ps{a}", [P, CHUNK], F32)) for a in range(4)]

        chunk_loaded = [sem(f"chunk_loaded{i}") for i in range(DEEP)]
        chunk_hi = sem("chunk_hi")
        chunk_split = sem("chunk_split")
        chunk_used = sem("chunk_used")
        hT_split = sem("hT_split")
        psum_full = [sem(f"psum_full{a}") for a in range(4)]
        psum_free = [sem(f"psum_free{a}") for a in range(4)]
        hi_copied = sem("hi_copied")
        mem_loaded = [sem(f"mem_loaded{t}") for t in range(NT)]
        x_loaded = sem("x_loaded")
        small_loaded = sem("small_loaded")
        router_loaded = sem("router_loaded")
        gain_loaded = sem("gain_loaded")
        constants = sem("constants")
        routing_constants = sem("routing_constants")
        sumsq_ready = sem("sumsq_ready")
        meansq_ready = sem("meansq_ready")
        rstd_ready = sem("rstd_ready")
        norm_done = sem("norm_done")
        lat_sumsq_ready = sem("lat_sumsq_ready")
        lat_meansq_ready = sem("lat_meansq_ready")
        lat_rstd_ready = sem("lat_rstd_ready")
        angles_ready = sem("angles_ready")
        trig_ready = sem("trig_ready")
        dve_step = sem("dve_step")
        v_copied = sem("v_copied")
        qa_ready = sem("qa_ready")
        k_ready = sem("k_ready")
        qb_copied = sem("qb_copied")
        qb_ready = sem("qb_ready")
        kr_copied = sem("kr_copied")
        max_ready = sem("max_ready")
        exp_done = sem("exp_done")
        probs_ready = sem("probs_ready")
        gates_ready = sem("gates_ready")
        mixed_ready = sem("mixed_ready")
        mixed_split = sem("mixed_split")
        x_added = sem("x_added")
        silu_done = sem("silu_done")
        act_ready = sem("act_ready")
        act_split = sem("act_split")
        y_copied = sem("y_copied")
        y_split = sem("y_split")
        normed_hi_ready = sem("normed_hi_ready")
        normed_split = sem("normed_split")
        zeros_ready = sem("zeros_ready")
        wr_hi_ready = sem("wr_hi_ready")
        wr_split = sem("wr_split")
        diff_ready = sem("diff_ready")
        ratio_ready = sem("ratio_ready")
        masks_ready = sem("masks_ready")
        turns_ready = sem("turns_ready")
        picked = sem("picked")
        routed_sem = sem("routed")
        stored = sem("stored")

        counters = {"chunk": chunk_used, "qa_ready": qa_ready, "k_ready": k_ready, "qb_copied": qb_copied,
                    "exp_done": exp_done, "silu_done": silu_done, "act_ready": act_ready,
                    "turns_ready": turns_ready, "x_added": x_added, "hT_split": hT_split}
        for a in range(4):
            counters[f"psum_full{a}"], counters[f"psum_free{a}"] = psum_full[a], psum_free[a]

        def wait_full(eng, key, it=0):
            name, event = full_by[key]
            eng.wait_ge(counters[name], tl.after(name, event, it))

        def wait_free(eng, key):
            if prior[key] is not None:
                name, event = free_by[prior[key]]
                eng.wait_ge(counters[name], tl.last(name, event))

        def wait_free_in_loop(eng, key, it):
            a = areas[key]
            eng.wait_ge(psum_free[a], tl.before(f"psum_free{a}", key, it))

        def wait_read(eng, key, it=0):
            name, event = free_by[key]
            eng.wait_ge(counters[name], tl.after(name, event, it))

        def gathered_by(turn, half):
            per_turn = tl.events["psum_full3", ("gathered", "next", half)][1]
            return turn * per_turn + tl.after("psum_full3", ("gathered", "first", half))

        def area(key):
            return ps[areas[key]]

        def chunk_no(key, it=0):
            return tl.before("chunk", key, it)

        def slot(key):
            return tl.before("chunk", key)

        def tile(key):
            return tiles[key]

        w_in = A["w_in"].rearrange("l (k p) n -> l p k n", p=P)
        w_mem = A["w_mem_kv"].rearrange("l (k p) n -> l p k n", p=P)
        w_uq = A["w_uq"].rearrange("l (k p) n -> l p k n", p=P)
        w_branch = A["w_branch"].rearrange("l b (k p) n -> l b p k n", p=P)
        w_out = A["w_out"].rearrange("l (k p) n -> l p k n", p=P)
        dense_w = {"G": A["w_gate_dense"].rearrange("l (k p) n -> l p k n", p=P),
                   "U": A["w_up_dense"].rearrange("l (k p) n -> l p k n", p=P),
                   "D": A["w_down_dense"].rearrange("l (k p) n -> l k p n", p=P)}
        expert_w = {"G": A["w_gate_exp"].rearrange("l e (k p) n -> (l e) p k n", p=P),
                    "U": A["w_up_exp"].rearrange("l e (k p) n -> (l e) p k n", p=P),
                    "D": A["w_down_exp"].rearrange("l e (k p) n -> (l e) k p n", p=P)}

        def chunk_source(key, it=0):
            kind = key[0]
            if kind in ("memk", "memv"):
                _, l, c = key
                n0 = 0 if kind == "memk" else M_HEADS * M_DIM
                return w_mem[l, :, 2 * c:2 * c + 2, n0:n0 + 512]
            if kind in ("qa", "kvcq", "qm"):
                _, l, c = key
                n0 = {"qa": COL_QA, "kvcq": COL_KVCQ, "qm": COL_QM}[kind]
                return w_in[l, :, 2 * c:2 * c + 2, n0:n0 + 512]
            if kind == "ckvkr":
                _, l, c = key
                return w_in[l, :, 4 * c:4 * c + 4, COL_CKVKR:COL_QM]
            if kind == "uq":
                _, l, c = key
                return w_uq[l, :, c, :]
            if kind == "ukv":
                return A["w_ukv"][key[1]]
            if kind == "gate":
                _, l, g, c = key
                n0 = COL_GATES + 512 * g
                return w_in[l, :, 2 * c:2 * c + 2, n0:n0 + 512]
            if kind == "branch":
                _, l, h, i, c = key
                return w_branch[l, i, :, 2 * c:2 * c + 2, 512 * h:512 * h + 512]
            if kind == "out":
                _, l, n, c = key
                return w_out[l, :, 2 * c:2 * c + 2, 512 * n:512 * n + 512]
            _, which, g, c = key
            if kind == "moe":
                w = expert_w[which][it]
                if which == "D":
                    return w[4 * g + c]
                return w[:, 2 * c:2 * c + 2, FF_GROUP * g:FF_GROUP * (g + 1)]
            w = dense_w[which][0]
            if kind == "dense":
                g = GROUPS - 1 if g == "last" else g
                if which == "D":
                    return w[4 * g + c]
                return w[:, 2 * c:2 * c + 2, FF_GROUP * g:FF_GROUP * (g + 1)]
            if which == "D":
                return w[it * 8 + (4 * g + c)]
            return w[:, 2 * c:2 * c + 2, bass.ds(it * (2 * FF_GROUP) + g * FF_GROUP, FF_GROUP)]

        def chunk_view(key, tile):
            kind = key[0]
            if kind == "ckvkr":
                return tile[:, 0:4 * (KV_RANK + B_ROPE)].rearrange("p (k n) -> p k n", k=4)
            if kind == "uq":
                return tile[:, 0:B_HEADS * B_QK]
            if kind == "ukv" or key[1] == "D":
                return tile[:, :]
            return tile[:, :].rearrange("p (k n) -> p k n", k=2)

        def chunk_width(key):
            return {"ckvkr": 4 * (KV_RANK + B_ROPE), "uq": B_HEADS * B_QK}.get(key[0], CHUNK)

        opening = [(k, l, c) for l in range(DEPTH) for k in ("memk", "memv") for c in range(4)]
        dense_first = group_chunks("dense", "GU", 0)
        dense_loop = [c for tag, kind, g in dense_pair() for c in group_chunks(tag, kind, g)]
        dense_last = group_chunks("dense", "D", "last")
        moe_loop = [c for kind, g in group_order() for c in group_chunks("moe", kind, g)]
        DENSE_TURNS = (GROUPS - 1) // 2
        assert len(dense_loop) == PAIR_CHUNKS and len(moe_loop) == FFN_CHUNKS

        block = ctx.enter_context(nc.Block())

        @block.sync
        def _(sp):
            def load(key, it=0, weights_of=None):
                depth = DEEP if key[0] == "moe" else RAW
                if not isinstance(it, int) or slot(key) >= RAW:
                    sp.wait_ge(chunk_split, chunk_no(key, it) - depth + 1)
                src = chunk_source(key, it if weights_of is None else weights_of)
                sp.dma_start(chunk_view(key, raw[tile(key)]), src).then_inc(chunk_loaded[tile(key)], 16)

            for t in range(NT):
                sp.dma_start(normed[:, t, :], A["mem"][0, P * t:P * (t + 1)]).then_inc(mem_loaded[t], 16)
            for key in opening[0:SPLIT]:
                load(key)
            sp.dma_start(x[:, :, :], A["x"][0].rearrange("(t p) d -> p t d", p=P)).then_inc(x_loaded, 16)
            for key in opening[SPLIT:] + mixer_chunks(0) + dense_first:
                load(key)
            with nc.sync.Fori(0, DENSE_TURNS) as it:
                for key in dense_loop:
                    load(key, it)
            for key in dense_last + mixer_chunks(1):
                load(key)
            sp.wait_ge(chunk_used, tl.after("chunk", ("branch", DEPTH - 1, 1, BRANCHES - 1, 1)))
            sp.wait_ge(mixed_ready, 2 * DEPTH)
            with nc.sync.Fori(0, EXPERTS) as e:
                for n, key in enumerate(moe_loop):
                    if 0 <= n - (DEEP - RAW - LATE) < RAW:
                        sp.wait_ge(chunk_split, chunk_no(moe_loop[0], 0) - RAW + n - (DEEP - RAW - LATE) + 1)
                    if n == DEEP - LATE:
                        wait_full(sp, ("router",))
                    load(key, e)
            sp.wait_ge(turns_ready, 1)
            turns = nc.sync.value_load(turns_i[0:1, 0:1], min_val=EXPERTS, max_val=2 * EXPERTS)
            with nc.sync.If(turns > EXPERTS):
                with nc.sync.Fori(EXPERTS, 2 * EXPERTS) as e:
                    for key in moe_loop:
                        load(key, e, weights_of=e - EXPERTS)
            for t in range(NT):
                sp.wait_ge(norm_done, NT * 5 + t + 1)
                sp.dma_start(out[0, P * t:P * (t + 1)], x[:, t, :]).then_inc(stored, 16)
            sp.wait_ge(stored, 16 * NT)

        @block.gpsimd
        def _(pool):
            def load_gain(n, row):
                if n:
                    pool.wait_ge(norm_done, 2 * n)
                pool.dma_start(gain[:, :], row.partition_broadcast(P)).then_inc(gain_loaded, 16)

            load_gain(0, A["g_mem"])
            nc.gpsimd.memset(ident[:, :], 0.0).then_inc(constants, 1)
            nc.gpsimd.memset(power[:, :], -0.5).then_inc(constants, 1)
            pool.wait_ge(constants, 2)
            nc.gpsimd.affine_select(out=ident[:, :], in_=ident[:, :], compare_op=ALU.not_equal, fill=1.0, base=0,
                                    pattern=[[-1, P]], channel_multiplier=1).then_inc(constants, 1)

            def rstd_of(n):
                for t in range(NT):
                    pool.wait_ge(meansq_ready, NT * n + t + 1)
                    nc.gpsimd.tensor_tensor(rstd[:, t:t + 1], meansq[:, t:t + 1], power[:, 0:1],
                                            ALU.pow).then_inc(rstd_ready, 1)

            rstd_of(0)
            for t in range(NT):
                pool.dma_start(pos_i[:, t:t + 1],
                               A["positions"][0, P * t:P * (t + 1)].unsqueeze(1)).then_inc(small_loaded, 16)
            pool.dma_start(freqs[:, :], inv_freq.partition_broadcast(P)).then_inc(small_loaded, 16)
            for l in range(DEPTH):
                pool.dma_start(g_lat[:, l, 0:Q_RANK], A["g_q_lat"][l].partition_broadcast(P)).then_inc(small_loaded, 16)
                pool.dma_start(g_lat[:, l, Q_RANK:], A["g_kv_lat"][l].partition_broadcast(P)).then_inc(small_loaded, 16)
                pool.dma_start(sink[:, l, :], A["sink"][l].partition_broadcast(P)).then_inc(small_loaded, 16)
            pool.dma_start(wr[:, :, :], A["w_router"][0].rearrange("(k p) e -> p k e", p=P)).then_inc(router_loaded, 16)
            nc.gpsimd.memset(mask[:, :, :], 0.0).then_inc(constants, 1)
            pool.wait_ge(constants, 4)
            nc.gpsimd.affine_select(out=mask[:, 0, P:], in_=mask[:, 0, P:], compare_op=ALU.is_ge, fill=MASKED,
                                    base=0, pattern=[[-1, P]], channel_multiplier=1).then_inc(constants, 1)
            nc.gpsimd.affine_select(out=mask[:, 1, 0:P], in_=mask[:, 1, 0:P], compare_op=ALU.is_ge, fill=MASKED,
                                    base=0, pattern=[[1, P]], channel_multiplier=-1).then_inc(constants, 1)
            load_gain(1, A["g_mix"][0])
            for l in range(DEPTH):
                rstd_of(2 * l + 1)
                load_gain(2 * l + 2, A["g_ffn"][l])
                pool.wait_ge(chunk_used, tl.after("chunk", ("qa", l, 3)))
                nc.gpsimd.memset(kr_pad[:, :, 0:B_NOPE], 0.0).then_inc(constants, 1)
                pool.wait_ge(lat_meansq_ready, l + 1)
                nc.gpsimd.tensor_tensor(lat_rstd[:, :, :], lat_meansq[:, :, :],
                                        power[:, :].rearrange("p (a t) -> p a t", a=2),
                                        ALU.pow).then_inc(lat_rstd_ready, 1)
                rstd_of(2 * l + 2)
                load_gain(2 * l + 3, A["g_mix"][1] if l == 0 else A["g_final"])
                if l == 0:
                    nc.gpsimd.memset(zeros[:, :], 0.0).then_inc(zeros_ready, 1)
                else:
                    nc.gpsimd.memset(ones[:, :], 1.0).then_inc(routing_constants, 1)
                    nc.gpsimd.memset(slot_w[:, :], 0.0).then_inc(routing_constants, 1)
                    nc.gpsimd.memset(route[:, 2 * EXPERTS, :], -1.0).then_inc(routing_constants, 1)
                    nc.gpsimd.iota(iota8[:, :], pattern=[[1, EXPERTS]], base=0, channel_multiplier=0,
                                   allow_small_or_imprecise_dtypes=True).then_inc(routing_constants, 1)
                    nc.gpsimd.iota(iotaS[:, :], pattern=[[1, SLOTS]], base=0, channel_multiplier=0,
                                   allow_small_or_imprecise_dtypes=True).then_inc(routing_constants, 1)
                    pool.wait_ge(routing_constants, 1)
                    nc.gpsimd.affine_select(out=earlier[:, :], in_=ones[:, :], compare_op=ALU.is_gt, fill=0.0, base=0,
                                            pattern=[[1, P]], channel_multiplier=-1).then_inc(routing_constants, 1)
            rstd_of(5)

        @block.scalar
        def _(eng):
            s = nc.scalar

            def hi_of(key, it=0):
                n = slot(key)
                w = chunk_width(key)
                loads, loads_per_turn, _ = tl.events[f"loaded{tile(key)}", key]
                eng.wait_ge(chunk_loaded[tile(key)], 16 * loads + it * (16 * loads_per_turn))
                if not isinstance(it, int) or n >= SPLIT:
                    eng.wait_ge(chunk_used, chunk_no(key, it) - SPLIT + 1)
                s.activation(whi[n % SPLIT][:, 0:w], raw[tile(key)][:, 0:w], ACT.Copy).then_inc(chunk_hi, 1)

            def copy_hi(key, dst, src, it=0):
                wait_full(eng, key, it)
                s.activation(dst, src, ACT.Copy).then_inc(hi_copied, 1)

            def copy_out(key, dst, src, it=0):
                wait_full(eng, key, it)
                a = areas[key]
                s.activation(dst, src, ACT.Copy).then_inc(psum_free[a], 1)

            def square(src, half, t, squared=None):
                cols = slice(512 * half, 512 * (half + 1))
                s.activation(junk[:, t, cols] if squared is None else squared[:, cols], src[:, t, cols], ACT.Square,
                             accum_out=sumsq[:, half, t:t + 1]).then_inc(sumsq_ready, 1)

            def transposed(name):
                for a in range(2):
                    wait_full(eng, (*name, a, "area"))
                    for half in range(2):
                        k = 4 * a + 2 * half
                        s.activation(hT_hi[:, k:k + 2, :].rearrange("p k n -> p (k n)"),
                                     ps[a][:, 512 * half:512 * (half + 1)], ACT.Copy).then_inc(hi_copied, 1)

            for t in range(NT):
                eng.wait_ge(mem_loaded[t], 16)
                for half in range(2):
                    square(normed, half, t)
            for key in opening[0:2]:
                hi_of(key)
            transposed(("memT",))
            for key in opening[2:SPLIT]:
                hi_of(key)
            pending = opening[SPLIT:] + mixer_chunks(0)[0:2]
            for l in range(DEPTH):
                for key in pending[0:2]:
                    hi_of(key)
                pending = pending[2:]
                copy_out(("memk", l), kM[:, l, :, :].rearrange("p h n -> p (h n)"), area(("memk", l))[:, :])
                for key in pending[0:3]:
                    hi_of(key)
                if l == 0:
                    eng.wait_ge(x_loaded, 16)
                    for t in range(NT):
                        for half in range(2):
                            square(x, half, t)
                else:
                    eng.wait_ge(angles_ready, 1)
                    s.activation(ang[:, 3:5, :, :], ang[:, 0:2, :, :], ACT.Sin).then_inc(trig_ready, 1)
                    eng.wait_ge(router_loaded, 16)
                    s.activation(wr_hi[:, :, :], wr[:, :, :], ACT.Copy).then_inc(wr_hi_ready, 1)
                for key in pending[3:6]:
                    hi_of(key)
                pending = pending[6:]
            for l in range(DEPTH):
                todo = mixer_chunks(l)
                done = [2 if l == 0 else 0]

                def ahead(key, more=3):
                    upto = min(len(todo), todo.index(key) + 1 + more)
                    for k in todo[done[0]:upto]:
                        hi_of(k)
                    done[0] = max(done[0], upto)

                if l == 0:
                    ahead(("qa", l, 0))
                else:
                    for t in range(NT):
                        for half in range(2):
                            if t and half:
                                ahead(("qa", l, 0), 1)
                            eng.wait_ge(x_added, tl.after("x_added", ("down", t, half)))
                            square(x, half, t)
                    ahead(("qa", l, 0), 2)
                transposed(("hT", 2 * l))
                ahead(("kvcq", l, 3))
                key = ("kvcq", l)
                wait_full(eng, key)
                kv = area(key)[:, :].rearrange("p (t n) -> p t n", t=NT)
                s.activation(vA[:, :, :], kv[:, :, 128:256], ACT.Copy).then_inc(v_copied, 1)
                for t in range(NT):
                    s.activation(junk[:, t, 0:Q_RANK], kv[:, t, 256:512], ACT.Square,
                                 accum_out=lat_sumsq[:, 0, t:t + 1]).then_inc(lat_sumsq_ready, 1)
                ahead(("ckvkr", l, 1))
                key = ("ckvkr", l)
                wait_full(eng, key)
                kv = area(key)[:, :].rearrange("p (t n) -> p t n", t=NT)
                for t in range(NT):
                    s.activation(junk[:, t, 512:512 + KV_RANK], kv[:, t, 0:KV_RANK], ACT.Square,
                                 accum_out=lat_sumsq[:, 1, t:t + 1]).then_inc(lat_sumsq_ready, 1)
                ahead(("qm", l, 3))
                copy_out(("qm", l), qMT[:, :, :].rearrange("p h n -> p (h n)"), area(("qm", l))[:, :])
                copy_out(("T_qa", l), qaT[:, :, :].rearrange("p h n -> p (h n)"), area(("T_qa", l))[:, :])
                key = ("T_lat", l)
                copy_hi(key, cqT_hi[:, :, :].rearrange("p k n -> p (k n)"), area(key)[:, 512:1024])
                key = ("T_kv", l)
                copy_hi(key, ckvT_hi[:, :], area(key)[:, 0:TOK])
                s.activation(kBT[B_NOPE:B_QK, :, :],
                             area(key)[B_NOPE:B_QK, 512:512 + TOK].unsqueeze(1).to_broadcast([B_ROPE, B_HEADS, TOK]),
                             ACT.Copy).then_inc(kr_copied, 1)
                ahead(("uq", l, 1))
                for t in range(NT):
                    key = ("uq", l, t)
                    wait_full(eng, key)
                    s.activation(qB[:, t, :, :].rearrange("p (a h) n -> p a (h n)", a=2),
                                 area(key)[:, :].rearrange("p (a n) -> p a n", a=2)[:, :, 0:4 * B_QK],
                                 ACT.Copy).then_inc(qb_copied, 1)
                ahead(("ukv", l, 0))
                for a in range(2):
                    key = ("ukv_k", l, a)
                    copy_out(key, kBT[0:B_NOPE, 4 * a:4 * a + 4, :].rearrange("p h n -> p (h n)"), area(key)[0:B_NOPE, :])
                copy_out(("T_qb", l, 0), qBT[:, 0:4, :].rearrange("p h n -> p (h n)"), area(("T_qb", l, 0))[0:B_QK, :])

                def exps(u):
                    kind, j = units[u]
                    eng.wait_ge(max_ready, l * len(units) + u + 1)
                    if kind == "A":
                        for q in range(4):
                            tile = probs[:, u % 2, q // 2, q % 2, :]
                            s.activation(tile, tile, ACT.Exp, bias=neg_max[:, q:q + 1],
                                         accum_out=row_sum[:, q:q + 1]).then_inc(exp_done, 1)
                        s.activation(sink_exp[:, :], sink_arg[:, :], ACT.Exp).then_inc(exp_done, 1)
                    else:
                        wait_full(eng, ("pT", l, u - 2))
                        scale = (B_QK if kind == "B" else M_DIM) ** -0.5
                        for q in range(4):
                            s.activation(probs[:, u % 2, q // 2, q % 2, :],
                                         area(("S", l, u))[:, TOK * q:TOK * (q + 1)], ACT.Exp,
                                         bias=neg_max[:, q:q + 1], scale=scale,
                                         accum_out=row_sum[:, q:q + 1]).then_inc(exp_done, 1)

                for step in attention_steps():
                    for kind, n in step:
                        if kind == "gate":
                            if n[1] != 3:
                                ahead(("gate", l, *n))
                            else:
                                g = n[0]
                                copy_out(("gate", l, g), gates[:, 4 * g:4 * g + 4, :].rearrange("p a n -> p (a n)"),
                                         area(("gate", l, g))[:, :])
                                ahead(("gate", l, *n))
                            if n == (0, 0):
                                exps(0)
                        elif kind == "T":
                            key = ("pT", l, n)
                            if n >= 1:
                                wait_full(eng, ("oT", l, n - 1))
                            copy_out(key, pT[:, :, :, :].rearrange("p h k n -> p (h k n)"), area(key)[:, :])
                            if step[0][0] == "QK":
                                exps(step[0][1])
                        elif kind == "PV":
                            key = ("oT", l, n)
                            blk, wide = y_place(n)
                            copy_hi(key, y_hi[:, blk:blk + wide, :].rearrange("p b n -> p (b n)"),
                                    area(key)[:, 0:wide * TOK])
                for g in range(6):
                    eng.wait_ge(psum_free[3], tl.after("psum_free3", ("gate", l, g)))
                    part = gates[:, 4 * g:4 * g + 4, :]
                    s.activation(part, part, ACT.Sigmoid).then_inc(gates_ready, 1)
                    ahead(("branch", l, 0, 0, 0), min(g, 3))
                for h in range(2):
                    ahead(("branch", l, h, 2, 1))
                    if l:
                        wait_full(eng, ("branch", l, h, 2))
                    eng.wait_ge(mixed_ready, 2 * l + h + 1)
                    s.activation(mixT_hi[:, 4 * h:4 * h + 4, :], mixed[:, :, :], ACT.Copy).then_inc(hi_copied, 1)
                ahead(("out", l, 1, 1))
                ahead(("out", l, 0, 3), 2)
                if l == 0:
                    for key in dense_first[0:2]:
                        hi_of(key)
                for half in range(2):
                    for t in range(NT):
                        eng.wait_ge(x_added, tl.after("x_added", ("out", l, half, t)))
                        square(x, half, t)
                if l == 0:
                    for key in dense_first[2:SPLIT]:
                        hi_of(key)
                transposed(("hT", 2 * l + 1))

                if l == 0:
                    def dense_silu(tag, g, it=0):
                        wait_full(eng, (tag, "G", g), it)
                        if tag == "pair":
                            eng.wait_ge(act_ready, tl.before("act_ready", (tag, g), it))
                        s.activation(silu[:, :, :], ps[0][:, :].rearrange("p (a n) -> p a n", a=4),
                                     ACT.Silu).then_inc(silu_done, 1)

                    def dense_hi(n, pair):
                        eng.wait_ge(act_ready, n + 1)
                        s.activation(actT_hi[pair][:, :, :], act[:, :, :], ACT.Copy).then_inc(hi_copied, 1)

                    for key in dense_first[SPLIT:7]:
                        hi_of(key)
                    dense_silu("dense", 0)
                    hi_of(dense_first[7])
                    with s.Fori(0, DENSE_TURNS) as it:
                        for tag, kind, g in dense_pair():
                            keys = group_chunks(tag, kind, g)
                            if kind == "GU":
                                for key in keys[0:3]:
                                    hi_of(key, it)
                                dense_hi(it * 2 + (g - 1), (g - 1) % 2)
                                for key in keys[3:7]:
                                    hi_of(key, it)
                                dense_silu(tag, g, it)
                                hi_of(keys[7], it)
                            else:
                                for key in keys:
                                    hi_of(key, it)
                    dense_hi(GROUPS - 1, (GROUPS - 1) % 2)
                    for key in dense_last:
                        hi_of(key)

            s.activation(normed_hi[:, :, :], normed, ACT.Copy).then_inc(normed_hi_ready, 1)
            copy_out(("router",), logitsT[:, :], ps[2][0:EXPERTS, 0:TOK])
            eng.wait_ge(diff_ready, 1)
            s.activation(pair_e[:, :], pair_d[:, :], ACT.Exp).then_inc(ratio_ready, 1)
            eng.wait_ge(turns_ready, 1)
            turns = s.value_load(turns_i[0:1, 0:1], min_val=EXPERTS, max_val=2 * EXPERTS)
            with s.Fori(0, turns) as e:
                done_m = [0]

                def upto(n):
                    for key in moe_loop[done_m[0]:n]:
                        hi_of(key, e)
                    done_m[0] = max(done_m[0], n)

                def moe_silu(g):
                    wait_full(eng, ("moe", "GU", g), e)
                    if g:
                        eng.wait_ge(act_ready, tl.after("act_ready", ("moe", g - 1), e))
                    s.activation(silu_m[:, :], ps[0][:, 0:FF_GROUP], ACT.Silu).then_inc(silu_done, 1)

                def moe_hi(g):
                    key = ("moe", "T", g)
                    wait_full(eng, key, e)
                    s.activation(actm_hi[g % 2][:, :, :], ps[1][:, 0:FF_GROUP].rearrange("p (a n) -> p a n", a=4),
                                 ACT.Copy).then_inc(hi_copied, 1)

                upto(2)
                for half in range(2):
                    eng.wait_ge(psum_full[3], gathered_by(e, half))
                    s.activation(xg_hi[:, 4 * half:4 * (half + 1), :].rearrange("p k n -> p (k n)"),
                                 ps[3][:, 512 * half:512 * (half + 1)], ACT.Copy).then_inc(hi_copied, 1)
                upto(4)
                eng.wait_ge(chunk_used, chunk_no(moe_loop[0], e))
                s.activation(y_out_hi[:, :], ps[2][:, :], ACT.Copy, scale=slot_w[:, 0:1]).then_inc(y_copied, 1)
                upto(before_silu(0))
                moe_silu(0)
                upto(before_split(0))
                moe_hi(0)
                for g in range(1, GROUPS):
                    upto(before_silu(g))
                    moe_silu(g)
                    upto(before_split(g))
                    moe_hi(g)
                upto(FFN_CHUNKS)
            eng.wait_ge(chunk_used, chunk_no(moe_loop[0], turns))
            for half in range(2):
                cols = slice(512 * half, 512 * (half + 1))
                s.activation(y_out_hi[:, cols], ps[2][:, cols], ACT.Copy, scale=slot_w[:, 0:1]).then_inc(y_copied, 1)
            for t in range(NT):
                eng.wait_ge(x_added, tl.after("x_added", ("scatter", t), turns))
                for half in range(2):
                    square(x, half, t, squared=raw[RAW + t])

        @block.vector
        def _(eng):
            v = nc.vector
            steps = [0]

            def step(ins):
                steps[0] += 1
                ins.then_inc(dve_step, 1)
                eng.wait_ge(dve_step, steps[0])

            def lo_of(key, it=0):
                n = slot(key)
                w = chunk_width(key)
                eng.wait_ge(chunk_hi, chunk_no(key, it) + 1)
                v.tensor_tensor(wlo[n % SPLIT][:, 0:w], raw[tile(key)][:, 0:w], whi[n % SPLIT][:, 0:w].bitcast(F32),
                                ALU.subtract).then_inc(chunk_split, 1)

            def rest(key, lo, src, hi, it=0):
                eng.wait_ge(hi_copied, tl.after("hi_copied", key, it))
                v.tensor_tensor(lo, src, hi.bitcast(F32), ALU.subtract).then_inc(psum_free[areas[key]], 1)

            def norm_tile(n, t, src, dst):
                sums = NT + t + 1 if n in (2, 4) else 2 * (t + 1)
                eng.wait_ge(sumsq_ready, 2 * NT * n + sums)
                step(v.tensor_tensor(meansq[:, t:t + 1], sumsq[:, 0, t:t + 1], sumsq[:, 1, t:t + 1], ALU.add))
                v.tensor_scalar(meansq[:, t:t + 1], meansq[:, t:t + 1], 1.0 / D, EPS, ALU.mult,
                                ALU.add).then_inc(meansq_ready, 1)
                eng.wait_ge(rstd_ready, NT * n + t + 1)
                eng.wait_ge(gain_loaded, 16 * (n + 1))
                v.scalar_tensor_tensor(dst[:, t, :], src[:, t, :], rstd[:, t:t + 1], gain[:, :],
                                       ALU.mult, ALU.mult).then_inc(norm_done, 1)

            def norm(n, src, dst):
                for t in range(NT):
                    norm_tile(n, t, src, dst)

            def transposed(name):
                for i in range(4):
                    eng.wait_ge(hi_copied, tl.after("hi_copied", (*name, i)))
                    flat = lambda w: w[:, 2 * i:2 * i + 2, :].rearrange("p k n -> p (k n)")
                    v.tensor_tensor(flat(hT_lo), ps[i // 2][:, 512 * (i % 2):512 * (i % 2 + 1)],
                                    flat(hT_hi).bitcast(F32), ALU.subtract).then_inc(hT_split, 1)

            def rotate(src, heads, half, cos, sin, dsts, done=None):
                n = heads * 2 * half
                r1 = rot1[:, 0:n].rearrange("p (h a d) -> p h a d", h=heads, a=2)
                r2 = rot2[:, 0:n].rearrange("p (h a d) -> p h a d", h=heads, a=2)
                c = cos.rearrange("p (a d) -> p a d", a=2)
                sn = sin.rearrange("p (a d) -> p a d", a=2)
                v.tensor_tensor(rot1[:, 0:n].rearrange("p (h n) -> p h n", h=heads),
                                src, cos.unsqueeze(1).to_broadcast([P, heads, 2 * half]), ALU.mult)
                v.tensor_tensor(r2[:, :, 0, :], src[:, :, half:2 * half],
                                sn[:, 0, :].unsqueeze(1).to_broadcast([P, heads, half]), ALU.mult)
                step(v.tensor_tensor(r2[:, :, 1, :], src[:, :, 0:half],
                                     sn[:, 1, :].unsqueeze(1).to_broadcast([P, heads, half]), ALU.mult))
                for dst in dsts:
                    ins = v.tensor_tensor(dst, rot1[:, 0:n].rearrange("p (h n) -> p h n", h=heads),
                                          rot2[:, 0:n].rearrange("p (h n) -> p h n", h=heads), ALU.add)
                    if done is None:
                        step(ins)
                    else:
                        ins.then_inc(*done[0:2])
                        eng.wait_ge(done[0], done[2])

            def reduced_angles():
                eng.wait_ge(small_loaded, 16 * (NT + 1 + 3 * DEPTH))
                step(v.tensor_copy(pos_f[:, :], pos_i[:, :]))
                for t in range(NT):
                    step(v.tensor_scalar(ang[:, 2, t, :], freqs[:, :], pos_f[:, t:t + 1], None, ALU.mult))
                for i, quarter in enumerate((0.0, 0.25)):
                    step(v.tensor_scalar(ang[:, 3 + i, :, :], ang[:, 2, :, :], 0.15915494309189535, quarter, ALU.mult, ALU.add))
                flat = lambda a: a.rearrange("p i t n -> p i (t n)")
                r, k = flat(ang[:, 0:2, :, :]), flat(ang[:, 3:5, :, :])
                angle = flat(ang[:, 2:3, :, :]).to_broadcast([P, 2, NT * 48])
                step(v.tensor_scalar(k, k, ROUND, None, ALU.add))
                step(v.tensor_scalar(k, k, ROUND, None, ALU.subtract))
                step(v.scalar_tensor_tensor(r, k, -TWO_PI_HI, angle, ALU.mult, ALU.add))
                step(v.scalar_tensor_tensor(r, k, -TWO_PI_MID, r, ALU.mult, ALU.add))
                step(v.scalar_tensor_tensor(r, k, -TWO_PI_LO, r, ALU.mult, ALU.add))
                step(v.tensor_scalar(r[:, 1, :], r[:, 1, :], 1.5707963267948966, None, ALU.add))
                step(v.tensor_scalar(k, r, PI_BELOW, -6.283185307179586, ALU.is_gt, ALU.mult))
                step(v.tensor_tensor(r, r, k, ALU.add))
                step(v.tensor_scalar(k, r, -PI_BELOW, 6.283185307179586, ALU.is_lt, ALU.mult))
                step(v.tensor_tensor(r, r, k, ALU.add))
                v.tensor_scalar(r, r, PI_BELOW, -PI_BELOW, ALU.min, ALU.max).then_inc(angles_ready, 1)

            norm(0, normed, normed)
            seq = opening + mixer_chunks(0)[0:2]
            for key in seq[0:2]:
                lo_of(key)
            transposed(("memT",))
            for key in seq[2:SPLIT]:
                lo_of(key)
            seq = seq[SPLIT:]
            for l in range(DEPTH):
                for key in seq[0:3]:
                    lo_of(key)
                if l:
                    reduced_angles()
                for key in seq[3:5]:
                    lo_of(key)
                if l == 0:
                    wait_full(eng, ("memT", 1, "area"))
                    norm(1, x, normed)
                lo_of(seq[5])
                seq = seq[6:]
                key = ("memv", l)
                wait_full(eng, key)
                v.tensor_copy(vM[:, l, :, :].rearrange("p t n -> p (t n)"), area(key)[:, :]).then_inc(psum_free[3], 1)
                for key in seq[0:2]:
                    lo_of(key)
                seq = seq[2:]
            for l in range(DEPTH):
                todo = mixer_chunks(l)
                done = [2 if l == 0 else 1]

                def ahead(key, more=3):
                    upto = min(len(todo), todo.index(key) + 1 + more)
                    for k in todo[done[0]:upto]:
                        lo_of(k)
                    done[0] = max(done[0], upto)

                if l:
                    ahead(("qa", l, 0), 1)
                    norm_tile(3, 1, x, normed)
                    ahead(("qa", l, 0), 2)
                transposed(("hT", 2 * l))
                ahead(("qa", l, 3))
                if l == 0:
                    eng.wait_ge(wr_hi_ready, 1)
                    v.tensor_tensor(wr_lo[:, :, :], wr[:, :, :], wr_hi[:, :, :].bitcast(F32), ALU.subtract).then_inc(wr_split, 1)
                    eng.wait_ge(trig_ready, 1)
                    for cos, sin, f0, half in ((cosA, sinA, 0, A_DIM // 2), (cosB, sinB, A_DIM // 2, B_ROPE // 2)):
                        v.tensor_copy(cos[:, :, 0:half], ang[:, 4, :, f0:f0 + half])
                        v.tensor_copy(cos[:, :, half:], ang[:, 4, :, f0:f0 + half])
                        v.tensor_scalar(sin[:, :, 0:half], ang[:, 3, :, f0:f0 + half], -1.0, None, ALU.mult)
                        step(v.tensor_copy(sin[:, :, half:], ang[:, 3, :, f0:f0 + half]))
                key = ("qa", l)
                wait_full(eng, key)
                for t in range(NT):
                    rotate(area(key)[:, 512 * t:512 * t + 512].rearrange("p (h n) -> p h n", h=A_HEADS), A_HEADS,
                           A_DIM // 2, cosA[:, t, :], sinA[:, t, :],
                           [qa_rot[:, t, :].rearrange("p (h n) -> p h n", h=A_HEADS)],
                           (qa_ready, 1, l + 1) if t == NT - 1 else None)
                ahead(("kvcq", l, 3))
                key = ("kvcq", l)
                eng.wait_ge(lat_sumsq_ready, 4 * l + 2)
                for t in range(NT):
                    rotate(area(key)[:, 512 * t:512 * t + 128].rearrange("p (h n) -> p h n", h=A_KV), A_KV,
                           A_DIM // 2, cosA[:, t, :], sinA[:, t, :],
                           [k_dup[:, t, :, i, :] for i in range(2)])
                ahead(("ckvkr", l, 1))
                wait_full(eng, ("ckvkr", l))
                eng.wait_ge(lat_sumsq_ready, 4 * (l + 1))
                step(v.tensor_scalar(lat_meansq[:, 0, :], lat_sumsq[:, 0, :], 1.0 / Q_RANK, EPS, ALU.mult, ALU.add))
                v.tensor_scalar(lat_meansq[:, 1, :], lat_sumsq[:, 1, :], 1.0 / KV_RANK, EPS, ALU.mult,
                                ALU.add).then_inc(lat_meansq_ready, 1)
                for t in range(NT):
                    rotate(area(("ckvkr", l))[:, 512 * t + KV_RANK:512 * t + KV_RANK + B_ROPE].unsqueeze(1), 1,
                           B_ROPE // 2, cosB[:, t, :], sinB[:, t, :], [kr_pad[:, t, B_NOPE:].unsqueeze(1)])
                eng.wait_ge(lat_rstd_ready, l + 1)
                eng.wait_ge(v_copied, l + 1)
                for t in range(NT):
                    v.scalar_tensor_tensor(cq_n[:, t, :], area(("kvcq", l))[:, 512 * t + 256:512 * t + 512],
                                           lat_rstd[:, 0, t:t + 1], g_lat[:, l, 0:Q_RANK], ALU.mult, ALU.mult)
                v.scalar_tensor_tensor(ckv_n[:, 0, :], area(("ckvkr", l))[:, 0:KV_RANK],
                                       lat_rstd[:, 1, 0:1], g_lat[:, l, Q_RANK:], ALU.mult, ALU.mult)
                v.scalar_tensor_tensor(ckv_n[:, 1, :], area(("ckvkr", l))[:, 512:512 + KV_RANK],
                                       lat_rstd[:, 1, 1:2], g_lat[:, l, Q_RANK:], ALU.mult, ALU.mult).then_inc(k_ready, 1)
                ahead(("qm", l, 3))
                key = ("T_lat", l)
                eng.wait_ge(hi_copied, tl.after("hi_copied", key))
                step(v.tensor_copy(kaT[:, :, :].rearrange("p h n -> p (h n)"), area(key)[:, 0:512]))
                rest(key, cqT_lo[:, :, :].rearrange("p k n -> p (k n)"), area(key)[:, 512:1024],
                     cqT_hi[:, :, :].rearrange("p k n -> p (k n)"))
                key = ("T_kv", l)
                eng.wait_ge(kr_copied, l + 1)
                rest(key, ckvT_lo[:, :], area(key)[:, 0:TOK], ckvT_hi[:, :])
                ahead(("uq", l, 1))
                for t in range(NT):
                    eng.wait_ge(qb_copied, NT * l + t + 1)
                    rotate(qB[:, t, :, B_NOPE:], B_HEADS, B_ROPE // 2, cosB[:, t, :], sinB[:, t, :],
                           [qB[:, t, :, B_NOPE:]], (qb_ready, 1, NT * l + t + 1))
                ahead(("ukv", l, 0))
                key = ("ukv_v", l)
                wait_full(eng, key)
                v.tensor_copy(vB[:, :, :].rearrange("p t n -> p (t n)"), area(key)[:, :]).then_inc(psum_free[3], 1)
                key = ("T_qb", l, 1)
                wait_full(eng, key)
                v.tensor_copy(qBT[:, 4:8, :].rearrange("p h n -> p (h n)"), area(key)[0:B_QK, :]).then_inc(psum_free[1], 1)

                def maxima(u):
                    kind, j = units[u]
                    key = ("S", l, u)
                    wait_full(eng, key)
                    if kind == "A":
                        if u >= 2:
                            wait_full(eng, ("pT", l, u - 2))
                        v.scalar_tensor_tensor(probs[:, u % 2, :, :, :].rearrange("p h t n -> p h (t n)"),
                                               area(key)[:, :].rearrange("p (h n) -> p h n", h=2), A_DIM ** -0.5,
                                               mask[:, :, :].rearrange("p t n -> p (t n)").unsqueeze(1).to_broadcast([P, 2, NT * TOK]),
                                               ALU.mult, ALU.add).then_inc(psum_free[0], 1)
                        wait_read(eng, key)
                        step(v.tensor_reduce(row_max[:, :], probs[:, u % 2, :, :, :].rearrange("p h t n -> p (h t) n"),
                                             AX.X, ALU.max))
                        both = sink[:, l, 2 * j:2 * j + 2].unsqueeze(2).to_broadcast([P, 2, NT])
                        m22 = row_max[:, :].rearrange("p (h t) -> p h t", h=2)
                        step(v.tensor_tensor(m22, m22, both, ALU.max))
                        step(v.tensor_scalar(neg_max[:, :], row_max[:, :], -1.0, None, ALU.mult))
                        v.tensor_tensor(sink_arg[:, :].rearrange("p (h t) -> p h t", h=2),
                                        neg_max[:, :].rearrange("p (h t) -> p h t", h=2), both,
                                        ALU.add).then_inc(max_ready, 1)
                    else:
                        scale = (B_QK if kind == "B" else M_DIM) ** -0.5
                        step(v.tensor_reduce(row_max[:, :], area(key)[:, :].rearrange("p (q n) -> p q n", q=4),
                                             AX.X, ALU.max))
                        v.tensor_scalar(neg_max[:, :], row_max[:, :], -scale, None, ALU.mult).then_inc(max_ready, 1)

                def normalise(u):
                    kind, j = units[u]
                    eng.wait_ge(exp_done, tl.after("exp_done", (l, u)))
                    if kind == "A":
                        step(v.tensor_tensor(row_sum[:, :], row_sum[:, :], sink_exp[:, :], ALU.add))
                    step(v.reciprocal(inv_sum[:, :], row_sum[:, :]))
                    tile = probs[:, u % 2, :, :, :].rearrange("p h t n -> p (h t) n")
                    v.tensor_tensor(tile, tile, inv_sum[:, :].unsqueeze(2).to_broadcast([P, 4, TOK]),
                                    ALU.mult).then_inc(probs_ready, 1)

                for n_step, st in enumerate(attention_steps()):
                    if 1 <= n_step <= len(units):
                        normalise(n_step - 1)
                    for kind, n in st:
                        if kind == "QK":
                            maxima(n)
                        elif kind == "gate":
                            ahead(("gate", l, *n))
                        elif kind == "PV":
                            key = ("oT", l, n)
                            blk, wide = y_place(n)
                            rest(key, y_lo[:, blk:blk + wide, :].rearrange("p b n -> p (b n)"),
                                 area(key)[:, 0:wide * TOK], y_hi[:, blk:blk + wide, :].rearrange("p b n -> p (b n)"))
                for h in range(2):
                    for i in range(BRANCHES):
                        ahead(("branch", l, h, i, 1))
                        key = ("branch", l, h, i)
                        g = 2 * i + h
                        wait_full(eng, key)
                        eng.wait_ge(gates_ready, 6 * l + g + 1)
                        if i == 0 and h:
                            eng.wait_ge(hi_copied, tl.after("hi_copied", ("mixed", l, 0)))
                        dst = mixed if i == 0 else gated
                        v.tensor_tensor(dst[:, :, :], area(key)[:, :].rearrange("p (a n) -> p a n", a=4),
                                        gates[:, 4 * g:4 * g + 4, :], ALU.mult).then_inc(psum_free[areas[key]], 1)
                        wait_read(eng, key)
                        if i == 1:
                            step(v.tensor_tensor(mixed[:, :, :], mixed[:, :, :], gated[:, :, :], ALU.add))
                        if i == 2:
                            v.tensor_tensor(mixed[:, :, :], mixed[:, :, :], gated[:, :, :], ALU.add).then_inc(mixed_ready, 1)
                    eng.wait_ge(hi_copied, tl.after("hi_copied", ("mixed", l, h)))
                    v.tensor_tensor(mixT_lo[:, 4 * h:4 * h + 4, :], mixed[:, :, :],
                                    mixT_hi[:, 4 * h:4 * h + 4, :].bitcast(F32), ALU.subtract).then_inc(mixed_split, 1)
                    if h == 0:
                        eng.wait_ge(mixed_split, 2 * l + 1)
                for n in range(2):
                    ahead(("out", l, n, 3), 2)
                    if n and l == 0:
                        for key in dense_first[0:2]:
                            lo_of(key)
                    for t in range(NT):
                        wait_full(eng, ("out", l, n, t))
                        cols = x[:, t, 512 * n:512 * n + 512]
                        v.tensor_tensor(cols, area(("out", l, n))[:, 512 * t:512 * (t + 1)], cols,
                                        ALU.add).then_inc(x_added, 1)
                norm(2 * l + 2, x, normed)
                if l == 0:
                    for key in dense_first[2:SPLIT]:
                        lo_of(key)
                transposed(("hT", 2 * l + 1))

                if l == 0:
                    def product(tag, g, it=0):
                        wait_full(eng, (tag, "U", g), it)
                        eng.wait_ge(silu_done, tl.after("silu_done", (tag, g), it))
                        v.tensor_tensor(act[:, :, :], ps[1][:, :].rearrange("p (a n) -> p a n", a=4), silu[:, :, :],
                                        ALU.mult).then_inc(act_ready, 1)

                    def act_rest(n, pair):
                        eng.wait_ge(hi_copied, n + tl.after("hi_copied", ("dense", 0)))
                        v.tensor_tensor(actT_lo[pair][:, :, :], act[:, :, :], actT_hi[pair][:, :, :].bitcast(F32),
                                        ALU.subtract).then_inc(act_split, 1)

                    for key in dense_first[SPLIT:]:
                        lo_of(key)
                    product("dense", 0)
                    with v.Fori(0, DENSE_TURNS) as it:
                        for tag, kind, g in dense_pair():
                            keys = group_chunks(tag, kind, g)
                            if kind == "GU":
                                for key in keys[0:3]:
                                    lo_of(key, it)
                                act_rest(it * 2 + (g - 1), (g - 1) % 2)
                                for key in keys[3:]:
                                    lo_of(key, it)
                            else:
                                for key in keys[0:3]:
                                    lo_of(key, it)
                                eng.wait_ge(act_split, tl.before("act_split", (tag, g + 1), it))
                                product(tag, g + 1, it)
                                lo_of(keys[3], it)
                    act_rest(GROUPS - 1, (GROUPS - 1) % 2)
                    for key in dense_last:
                        lo_of(key)
                    def add_down(t, half):
                        wait_full(eng, ("down", t, half))
                        cols = slice(512 * half, 512 * (half + 1))
                        v.tensor_tensor(x[:, t, cols], ps[2 + t][:, cols], x[:, t, cols], ALU.add).then_inc(x_added, 1)

                    for half in range(2):
                        add_down(0, half)
                    norm_tile(3, 0, x, normed)
                    add_down(1, 0)
                    key = mixer_chunks(1)[0]
                    lo_of(key)
                    add_down(1, 1)

            eng.wait_ge(normed_hi_ready, 1)
            v.tensor_tensor(normed_lo[:, :, :], normed, normed_hi[:, :, :].bitcast(F32), ALU.subtract).then_inc(normed_split, 1)
            wait_full(eng, ("router_T",))
            eng.wait_ge(routing_constants, 6)
            v.tensor_copy(logits[:, :, :], ps[2][:, 0:NT * EXPERTS].rearrange("p (t n) -> p t n", t=NT)).then_inc(psum_free[2], 1)
            wait_read(eng, ("router_T",))
            v.max(top8[:, 0, :], logits[:, 0, :])
            step(v.max(top8[:, 1, :], logits[:, 1, :]))
            v.max_index(top_i[:, 0, :], top8[:, 0, :], logits[:, 0, :])
            step(v.max_index(top_i[:, 1, :], top8[:, 1, :], logits[:, 1, :]))
            step(v.tensor_copy(top_f[:, :, :], top_i[:, :, :]))
            v.tensor_tensor(pair_d[:, :], top8[:, :, 1], top8[:, :, 0], ALU.subtract).then_inc(diff_ready, 1)
            for r in range(2):
                for t in range(NT):
                    ins = v.tensor_scalar(hot[:, r, t, :], iota8[:, :], top_f[:, t, r:r + 1], None, ALU.is_equal)
            step(ins)
            v.tensor_tensor(routed[:, :, :], hot[:, 0, :, :], hot[:, 1, :, :], ALU.add).then_inc(masks_ready, 1)
            eng.wait_ge(ratio_ready, 1)
            step(v.tensor_scalar(pair_d[:, :], pair_e[:, :], 1.0, None, ALU.add))
            step(v.reciprocal(pair_w[:, 0, :], pair_d[:, :]))
            step(v.tensor_tensor(pair_w[:, 1, :], pair_w[:, 0, :], pair_e[:, :], ALU.mult))
            for t in range(NT):
                step(v.tensor_scalar(route_w[:, t, :], hot[:, 0, t, :], pair_w[:, 0, t:t + 1], None, ALU.mult))
                step(v.scalar_tensor_tensor(route_w[:, t, :], hot[:, 1, t, :], pair_w[:, 1, t:t + 1], route_w[:, t, :],
                                            ALU.mult, ALU.add))
            wait_full(eng, ("rank",))
            both = logits[:, :, :].rearrange("p t e -> p (t e)")
            step(v.tensor_scalar(both, ps[3][:, 0:NT * EXPERTS], 1.0, None, ALU.add))
            step(v.tensor_tensor(both, both, routed[:, :, :].rearrange("p t e -> p (t e)"), ALU.mult))
            for turn in range(2):
                part = route[:, EXPERTS * turn:EXPERTS * (turn + 1), :]
                v.tensor_scalar(part[:, :, 0:NT], logits[:, :, :].rearrange("p t e -> p e t"), float(1 + SLOTS * turn),
                                None, ALU.subtract)
                step(v.tensor_copy(part[:, :, 2:2 + NT], route_w[:, :, :].rearrange("p t e -> p e t")))
            step(v.tensor_reduce(most[:, :], ps[3][:, NT * EXPERTS:(NT + 1) * EXPERTS], AX.X, ALU.max))
            step(v.tensor_copy(cur_next[:, :], route[:, 0, :]))
            for t in range(NT):
                ins = v.tensor_scalar(onehot_next[:, t, :], iotaS[:, :], cur_next[:, t:t + 1], None, ALU.is_equal)
            ins.then_inc(routed_sem, 1)
            step(v.tensor_scalar(turns_f[:, :], most[:, :], SLOTS + 0.5, float(EXPERTS), ALU.is_gt, ALU.mult))
            step(v.tensor_scalar(turns_f[:, :], turns_f[:, :], float(EXPERTS), None, ALU.add))
            v.tensor_copy(turns_i[:, :], turns_f[:, :]).then_inc(turns_ready, 1)
            for t in range(NT):
                v.tensor_copy(back[:, P * t:P * (t + 1)], ones[:, :])
            eng.wait_ge(turns_ready, 1)
            turns = v.value_load(turns_i[0:1, 0:1], min_val=EXPERTS, max_val=2 * EXPERTS)

            def slots_of(e, tile_, name, dst):
                v.tensor_copy(tile_[:, :], route[:, bass.ds(e, 1), :].rearrange("p a b -> p (a b)")).then_inc(picked, 1)
                eng.wait_ge(picked, name)
                for t in range(NT):
                    ins = v.tensor_scalar(dst[:, t, :], iotaS[:, :], tile_[:, t:t + 1], None, ALU.is_equal)
                ins.then_inc(routed_sem, 1)

            def y_rest(cols):
                v.scalar_tensor_tensor(y_out_lo[:, cols], ps[2][:, cols], slot_w[:, 0:1], y_out_hi[:, cols].bitcast(F32),
                                       ALU.mult, ALU.subtract).then_inc(y_split, 1)

            def add_scattered(e):
                for t in range(NT):
                    key = ("scatter", t)
                    wait_full(eng, key, e)
                    v.tensor_tensor(x[:, t, :], area(key)[:, :], x[:, t, :], ALU.add).then_inc(x_added, 1)

            with v.Fori(0, turns) as e:
                done_m = [0]

                def upto(n):
                    for key in moe_loop[done_m[0]:n]:
                        lo_of(key, e)
                    done_m[0] = max(done_m[0], n)

                def moe_product(g):
                    eng.wait_ge(silu_done, tl.after("silu_done", ("moe", g), e))
                    if g:
                        wait_full(eng, ("moe", "T", g - 1), e)
                    v.tensor_tensor(act_m[:, :], ps[0][:, FF_GROUP:], silu_m[:, :], ALU.mult).then_inc(act_ready, 1)

                def moe_rest(g):
                    rest(("moe", "T", g), actm_lo[g % 2][:, :, :],
                         ps[1][:, 0:FF_GROUP].rearrange("p (a n) -> p a n", a=4), actm_hi[g % 2][:, :, :], e)

                upto(2)
                for half in range(2):
                    part = slice(4 * half, 4 * (half + 1))
                    rest(("gather", half), xg_lo[:, part, :].rearrange("p k n -> p (k n)"),
                         ps[3][:, 512 * half:512 * (half + 1)], xg_hi[:, part, :].rearrange("p k n -> p (k n)"), e)
                upto(4)
                eng.wait_ge(y_copied, e + 1)
                y_rest(slice(0, D))
                upto(before_silu(0))
                moe_product(0)
                upto(before_split(0))
                add_scattered(e)
                moe_rest(0)
                upto(before_split(0) + 2)
                slots_of(e, cur, e * 2 + 1, onehot)
                upto(before_split(0) + 4)
                slots_of(e + 1, cur_next, e * 2 + 2, onehot_next)
                for g in range(1, GROUPS):
                    upto(before_silu(g))
                    moe_product(g)
                    if g == 1:
                        wait_full(eng, ("T_back",), e)
                        v.tensor_copy(slot_w[:, :], ps[1][:, TOK:TOK + 1])
                        v.tensor_copy(back[:, :], ps[1][:, 0:TOK]).then_inc(psum_free[1], 1)
                    upto(before_split(g))
                    moe_rest(g)
                upto(FFN_CHUNKS)
            for half in range(2):
                eng.wait_ge(y_copied, turns + (half + 1))
                y_rest(slice(512 * half, 512 * (half + 1)))
            add_scattered(turns)

            norm(5, x, x)

        @block.tensor
        def _(pe):
            mm = nc.tensor.matmul

            def three(o, w_hi, w_lo, a_hi, a_lo, start, stop, stationary):
                for i, (w, a) in enumerate(((w_hi, a_hi), (w_hi, a_lo), (w_lo, a_hi))):
                    lhsT, rhs = (w, a) if stationary else (a, w)
                    ins = mm(o, lhsT, rhs, start=start and i == 0, stop=stop and i == 2, skip_group_check=True)
                return ins

            def wait_chunk(key, it=0):
                pe.wait_ge(chunk_split, chunk_no(key, it) + 1)
                n = slot(key) % SPLIT
                return whi[n], wlo[n]

            def stationary_chunk(key, a_hi, a_lo, out, first, last, it=0):
                hi, lo = wait_chunk(key, it)
                for kk in range(2):
                    for j in range(4):
                        w = slice(512 * kk + P * j, 512 * kk + P * (j + 1))
                        ins = three(out[:, TOK * j:TOK * (j + 1)], hi[:, w], lo[:, w], a_hi(kk), a_lo(kk),
                                    first and kk == 0 and j % 2 == 0, last and kk == 1, True)
                return ins

            def moving_chunk(key, a_hi, a_lo, outs, blocks, width, first, last, it=0):
                hi, lo = wait_chunk(key, it)
                for kk in range(blocks):
                    w = slice(width * kk, width * (kk + 1))
                    for t, o in enumerate(outs):
                        ins = three(o, hi[:, w], lo[:, w], a_hi(kk, t), a_lo(kk, t),
                                    first and kk == 0, last and kk == blocks - 1, False)
                return ins

            def used(ins):
                ins.then_inc(chunk_used, 1)

            def h_at(k):
                return lambda kk: hT_hi[:, k + kk, :], lambda kk: hT_lo[:, k + kk, :]

            def h_tile(k):
                return (lambda kk, t: hT_hi[:, k + kk, P * t:P * (t + 1)],
                        lambda kk, t: hT_lo[:, k + kk, P * t:P * (t + 1)])

            def banks(key, width):
                return [area(key)[:, 512 * t:512 * t + width] for t in range(NT)]

            def transposes(name, n):
                for a in range(2):
                    wait_free(pe, (*name, a, "area"))
                for t in range(NT):
                    pe.wait_ge(norm_done, NT * n + t + 1)
                    for a in range(2):
                        for k in range(4):
                            c = TOK * k + P * t
                            ins = nc.tensor.transpose(ps[a][:, c:c + P],
                                                      normed[:, t, P * (4 * a + k):P * (4 * a + k + 1)], ident[:, :])
                        if t == NT - 1:
                            ins.then_inc(psum_full[a], 1)

            def wait_piece(name, i):
                pe.wait_ge(hT_split, tl.after("hT_split", (*name, i)))

            def stationary_section(keys, full_key, act_of, name=None):
                wait_free(pe, full_key)
                for i, key in enumerate(keys):
                    if name is not None:
                        wait_piece(name, i)
                    used(stationary_chunk(key, *act_of(i), area(full_key), i == 0, i == len(keys) - 1))

            def moving_section(keys, full_key, width, blocks, act_of, name=None):
                wait_free(pe, full_key)
                for i, key in enumerate(keys):
                    if name is not None:
                        wait_piece(name, i)
                    used(moving_chunk(key, *act_of(i), banks(full_key, width), blocks, width, i == 0, i == len(keys) - 1))

            pe.wait_ge(constants, 3)
            transposes(("memT",), 0)
            for l in range(DEPTH):
                stationary_section([("memk", l, c) for c in range(4)], ("memk", l), lambda i: h_at(2 * i), ("memT",))
                moving_section([("memv", l, c) for c in range(4)], ("memv", l), 512, 2, lambda i: h_tile(2 * i))

            for l in range(DEPTH):
                transposes(("hT", 2 * l), 2 * l + 1)
                moving_section([("qa", l, c) for c in range(4)], ("qa", l), 512, 2, lambda i: h_tile(2 * i), ("hT", 2 * l))
                moving_section([("kvcq", l, c) for c in range(4)], ("kvcq", l), 512, 2, lambda i: h_tile(2 * i))
                moving_section([("ckvkr", l, c) for c in range(2)], ("ckvkr", l), KV_RANK + B_ROPE, 4, lambda i: h_tile(4 * i))
                stationary_section([("qm", l, c) for c in range(4)], ("qm", l), lambda i: h_at(2 * i))
                key = ("T_qa", l)
                wait_free(pe, key)
                for j in range(4):
                    for t in range(NT):
                        ins = nc.tensor.transpose(area(key)[:, TOK * j + P * t:TOK * j + P * (t + 1)],
                                                  qa_rot[:, t, P * j:P * (j + 1)], ident[:, :])
                ins.then_inc(psum_full[areas[key]], 1)
                wait_read(pe, ("kvcq", l))
                wait_read(pe, ("ckvkr", l))
                key = ("T_lat", l)
                wait_free(pe, key)
                for kv in range(A_KV):
                    for t in range(NT):
                        nc.tensor.transpose(area(key)[:, TOK * kv + P * t:TOK * kv + P * (t + 1)],
                                            k_dup[:, t, kv, :, :].rearrange("p a n -> p (a n)"), ident[:, :])
                for k in range(2):
                    for t in range(NT):
                        c = 512 + TOK * k + P * t
                        ins = nc.tensor.transpose(area(key)[:, c:c + P], cq_n[:, t, P * k:P * (k + 1)], ident[:, :])
                ins.then_inc(psum_full[areas[key]], 1)
                key = ("T_kv", l)
                wait_free(pe, key)
                pe.wait_ge(constants, 6 + l + 1)
                for t in range(NT):
                    nc.tensor.transpose(area(key)[:, P * t:P * (t + 1)], ckv_n[:, t, :], ident[:, :])
                for t in range(NT):
                    ins = nc.tensor.transpose(area(key)[0:B_QK, 512 + P * t:512 + P * (t + 1)], kr_pad[:, t, :], ident[:, :])
                ins.then_inc(psum_full[areas[key]], 1)
                wait_read(pe, ("T_lat", l))
                for t in range(NT):
                    wait_free(pe, ("uq", l, t))
                for k in range(2):
                    hi, lo = wait_chunk(("uq", l, k))
                    for t in range(NT):
                        for half in range(2):
                            w = slice(4 * B_QK * half, 4 * B_QK * (half + 1))
                            ins = three(area(("uq", l, t))[:, 512 * half:512 * half + 4 * B_QK], hi[:, w], lo[:, w],
                                        cqT_hi[:, k, P * t:P * (t + 1)], cqT_lo[:, k, P * t:P * (t + 1)], k == 0, k == 1, False)
                    used(ins)
                hi, lo = wait_chunk(("ukv", l, 0))
                wait_read(pe, ("T_kv", l))
                for a in range(2):
                    key = ("ukv_k", l, a)
                    wait_free(pe, key)
                    for j in range(4):
                        w = slice(P * (4 * a + j), P * (4 * a + j + 1))
                        ins = three(area(key)[:, TOK * j:TOK * (j + 1)], hi[:, w], lo[:, w], ckvT_hi[:, :], ckvT_lo[:, :],
                                    True, True, True)
                    ins.then_inc(psum_full[areas[key]], 1)
                key = ("ukv_v", l)
                wait_free(pe, key)
                values = [w[:, :].rearrange("p (h n) -> p h n", h=B_HEADS)[:, :, B_NOPE:] for w in (hi, lo)]
                for t in range(NT):
                    ins = three(area(key)[:, 512 * t:512 * (t + 1)].rearrange("p (h n) -> p h n", h=B_HEADS), *values,
                                ckvT_hi[:, P * t:P * (t + 1)], ckvT_lo[:, P * t:P * (t + 1)], True, True, False)
                used(ins)
                for a in range(2):
                    key = ("T_qb", l, a)
                    wait_free(pe, key)
                    pe.wait_ge(qb_ready, NT * (l + 1))
                    for j in range(4):
                        for t in range(NT):
                            c = TOK * j + P * t
                            ins = nc.tensor.transpose(area(key)[0:B_QK, c:c + P], qB[:, t, 4 * a + j, :], ident[:, :])
                    ins.then_inc(psum_full[areas[key]], 1)

                def scores(u):
                    kind, j = units[u]
                    key = ("S", l, u)
                    wait_free(pe, key)
                    for k in {0: (("T_qa", l), ("T_lat", l)),
                              1: (("T_qb", l, 0), ("T_qb", l, 1), ("ukv_k", l, 0), ("ukv_k", l, 1), ("ukv_v", l),
                                  ("qm", l))}.get(u, ()):
                        wait_read(pe, k)
                    for h in range(2):
                        head = 2 * j + h
                        for t in range(NT):
                            o = area(key)[:, TOK * (NT * h + t):TOK * (NT * h + t + 1)]
                            tt = slice(P * t, P * (t + 1))
                            if kind == "A":
                                r = slice(A_DIM * h, A_DIM * (h + 1))
                                ins = mm(o, qaT[r, j, tt], kaT[r, j // 2, :], start=True, stop=True)
                            elif kind == "B":
                                ins = mm(o, qBT[:, head, tt], kBT[:, head, :], start=True, stop=True)
                            else:
                                ins = mm(o, qMT[:, head, tt], kM[:, l, head, :], start=True, stop=True)
                    ins.then_inc(psum_full[0], 1)

                def turn(u):
                    key = ("pT", l, u)
                    pe.wait_ge(probs_ready, l * len(units) + u + 1)
                    wait_free(pe, key)
                    for h in range(2):
                        for kt in range(NT):
                            for t in range(NT):
                                c = TOK * (NT * h + kt) + P * t
                                ins = nc.tensor.transpose(area(key)[:, c:c + P], probs[:, u % 2, h, t, P * kt:P * (kt + 1)], ident[:, :])
                    ins.then_inc(psum_full[1], 1)

                def values_of(u):
                    kind, j = units[u]
                    key = ("oT", l, u)
                    wait_free(pe, key)
                    wait_read(pe, ("pT", l, u))
                    for h in range(2):
                        head = 2 * j + h
                        for kt in range(NT):
                            if kind == "M":
                                o, lhsT = area(key)[:, TOK * h:TOK * (h + 1)], vM[:, l, kt, M_DIM * head:M_DIM * (head + 1)]
                            else:
                                o = area(key)[64 * h:64 * (h + 1), 0:TOK]
                                c = A_DIM * (j // 2) if kind == "A" else B_V * head
                                lhsT = (vA if kind == "A" else vB)[:, kt, c:c + 64]
                            ins = mm(o, lhsT, pT[:, h, kt, :], start=kt == 0, stop=kt == NT - 1)
                    ins.then_inc(psum_full[2], 1)

                for step in attention_steps():
                    for kind, n in step:
                        if kind == "QK":
                            scores(n)
                        elif kind == "PV":
                            values_of(n)
                        elif kind == "T":
                            turn(n)
                        else:
                            g, c = n
                            key = ("gate", l, g)
                            if c == 0:
                                wait_free(pe, key)
                            used(stationary_chunk(("gate", l, g, c), *h_at(2 * c), area(key), c == 0, c == 3))

                for h in range(2):
                    for i in range(BRANCHES):
                        wait_read(pe, ("oT", l, len(units) - 1))
                        stationary_section([("branch", l, h, i, c) for c in range(2)], ("branch", l, h, i),
                                           lambda c: (lambda kk: y_hi[:, 4 * i + 2 * c + kk, :],
                                                      lambda kk: y_lo[:, 4 * i + 2 * c + kk, :]))
                for n in range(2):
                    wait_free(pe, ("out", l, n))
                for part in range(2):
                    pe.wait_ge(mixed_split, 2 * l + part + 1)
                    for n in range(2 - part):
                        for c in (2 * part, 2 * part + 1):
                            used(moving_chunk(("out", l, n, c), lambda kk, t: mixT_hi[:, 2 * c + kk, P * t:P * (t + 1)],
                                              lambda kk, t: mixT_lo[:, 2 * c + kk, P * t:P * (t + 1)],
                                              banks(("out", l, n), 512), 2, 512, c == 0, c == 3))
                for t, o in enumerate(banks(("out", l, 1), 512)):
                    for c in (2, 3):
                        ins = moving_chunk(("out", l, 1, c), lambda kk, _: mixT_hi[:, 2 * c + kk, P * t:P * (t + 1)],
                                           lambda kk, _: mixT_lo[:, 2 * c + kk, P * t:P * (t + 1)],
                                           [o], 2, 512, False, c == 3)
                        if t == NT - 1:
                            used(ins)
                    if t == 0:
                        ins.then_inc(psum_full[3], 1)
                transposes(("hT", 2 * l + 1), 2 * l + 2)

                if l == 0:
                    pe.wait_ge(zeros_ready, 1)
                    for t in range(NT):
                        wait_free(pe, ("down", t))
                        for half in range(2):
                            mm(ps[2 + t][:, 512 * half:512 * (half + 1)], zeros[0:1, 0:P], zeros[0:1, :], start=True,
                               stop=False, skip_group_check=True)

                    def up(tag, g, it=0):
                        for which, a, freed, name in (("G", 0, silu_done, "silu_done"), ("U", 1, act_ready, "act_ready")):
                            if tag == "dense":
                                wait_free(pe, (tag, which, g))
                            else:
                                pe.wait_ge(freed, tl.before(name, (tag, g), it))
                            for c in range(4):
                                if tag == "dense":
                                    wait_piece(("hT", 1), c)
                                used(stationary_chunk((tag, which, g, c), *h_at(2 * c), ps[a], c == 0, c == 3, it))

                    def down(tag, g, pair, splits, it=0):
                        pe.wait_ge(act_split, splits)
                        for j in range(4):
                            hi, lo = wait_chunk((tag, "D", g, j), it)
                            for t in range(NT):
                                for half in range(2):
                                    w = slice(512 * half, 512 * (half + 1))
                                    ins = three(ps[2 + t][:, w], hi[:, w], lo[:, w],
                                                actT_hi[pair][:, j, P * t:P * (t + 1)], actT_lo[pair][:, j, P * t:P * (t + 1)],
                                                False, False, False)
                            used(ins)

                    up("dense", 0)
                    with nc.tensor.Fori(0, DENSE_TURNS) as it:
                        for tag, kind, g in dense_pair():
                            if kind == "GU":
                                up(tag, g, it)
                            else:
                                down(tag, g, g % 2, it * 2 + (g + 1), it)
                    pe.wait_ge(act_split, GROUPS)
                    pair = (GROUPS - 1) % 2
                    for t in range(NT):
                        for half in range(2):
                            w = slice(512 * half, 512 * (half + 1))
                            last_part = t == NT - 1 and half == 1
                            for j in range(4):
                                hi, lo = wait_chunk(("dense", "D", "last", j))
                                ins = three(ps[2 + t][:, w], hi[:, w], lo[:, w], actT_hi[pair][:, j, P * t:P * (t + 1)],
                                            actT_lo[pair][:, j, P * t:P * (t + 1)], False, j == 3, False)
                                if last_part:
                                    used(ins)
                            if not last_part:
                                ins.then_inc(psum_full[2 + t], 1)

            pe.wait_ge(wr_split, 1)
            wait_free(pe, ("router",))
            for k in range(KD):
                if k % 2 == 0:
                    wait_piece(("hT", 3), k // 2)
                ins = three(ps[2][0:EXPERTS, 0:TOK], wr_hi[:, k, :], wr_lo[:, k, :], hT_hi[:, k, :], hT_lo[:, k, :],
                            k == 0, k == KD - 1, True)
            ins.then_inc(psum_full[2], 1)
            wait_free(pe, ("router_T",))
            for t in range(NT):
                ins = nc.tensor.transpose(ps[2][:, EXPERTS * t:EXPERTS * (t + 1)], logitsT[:, P * t:P * (t + 1)],
                                          ident[0:EXPERTS, 0:EXPERTS])
            ins.then_inc(psum_full[2], 1)
            pe.wait_ge(masks_ready, 1)
            wait_free(pe, ("rank",))
            mm(ps[3][:, 0:8], earlier[:, :], routed[:, 0, :], start=True, stop=True)
            mm(ps[3][:, 8:16], ones[:, :], routed[:, 0, :], start=True, stop=False)
            mm(ps[3][:, 8:16], earlier[:, :], routed[:, 1, :], start=False, stop=True)
            mm(ps[3][:, 16:24], ones[:, :], routed[:, 0, :], start=True, stop=False)
            mm(ps[3][:, 16:24], ones[:, :], routed[:, 1, :], start=False, stop=True).then_inc(psum_full[3], 1)
            def gather():
                for k in range(KD):
                    for t in range(NT):
                        for i, part in enumerate((normed_hi, normed_lo)):
                            ins = mm(ps[3][:, SLOTS * k:SLOTS * (k + 1)], part[:, t, P * k:P * (k + 1)],
                                     onehot_next[:, t, :], start=t == 0 and i == 0, stop=t == NT - 1 and i == 1)
                    if k % (KD // 2) == KD // 2 - 1:
                        ins.then_inc(psum_full[3], 1)

            def scatter(e, in_halves=False):
                pe.wait_ge(y_split, e + 1)
                for t in range(NT):
                    for half in range(2):
                        if in_halves and t == 0 and half == 1:
                            pe.wait_ge(y_split, e + 2)
                        w = slice(512 * half, 512 * (half + 1))
                        for i, part in enumerate((y_out_hi, y_out_lo)):
                            ins = mm(area(("scatter", t))[:, w], back[:, P * t:P * (t + 1)], part[:, w], start=i == 0, stop=i == 1)
                    ins.then_inc(psum_full[areas["scatter", t]], 1)

            pe.wait_ge(normed_split, 1)
            pe.wait_ge(routed_sem, 1)
            gather()
            pe.wait_ge(turns_ready, 1)
            turns = nc.tensor.value_load(turns_i[0:1, 0:1], min_val=EXPERTS, max_val=2 * EXPERTS)

            with nc.tensor.Fori(0, turns) as e:
                pe.wait_ge(psum_free[3], tl.after("psum_free3", ("gather", 0), e))

                def transposed_act(g):
                    key = ("moe", "T", g)
                    pe.wait_ge(act_ready, tl.after("act_ready", ("moe", g), e))
                    wait_free_in_loop(pe, key, e)
                    for j in range(4):
                        ins = nc.tensor.transpose(ps[1][:, P * j:P * (j + 1)], act_m[:, P * j:P * (j + 1)], ident[:, :])
                    ins.then_inc(psum_full[1], 1)

                for kind, g in group_order():
                    if kind == "GU":
                        if g:
                            pe.wait_ge(act_ready, tl.after("act_ready", ("moe", g - 1), e))
                        for which in "GU":
                            o = ps[0][:, 0:FF_GROUP] if which == "G" else ps[0][:, FF_GROUP:]
                            for c in range(4):
                                if which == "G" and g == 0 and c == 2:
                                    pe.wait_ge(psum_free[3], tl.after("psum_free3", ("gather", 1), e))
                                ins = moving_chunk(("moe", which, g, c), lambda kk, t: xg_hi[:, 2 * c + kk, :],
                                                   lambda kk, t: xg_lo[:, 2 * c + kk, :], [o], 2, 512, c == 0, c == 3, e)
                                used(ins)
                        if g == 0:
                            scatter(e)
                            transposed_act(0)
                        if g == 1:
                            pe.wait_ge(routed_sem, tl.after("routed", "onehot", e))
                            wait_free_in_loop(pe, ("T_back",), e)
                            for t in range(NT):
                                mm(ps[1][:, TOK:TOK + 1], onehot[:, t, :], cur[:, 2 + t:3 + t], start=t == 0, stop=t == NT - 1)
                            for t in range(NT):
                                ins = nc.tensor.transpose(ps[1][:, P * t:P * (t + 1)], onehot[:, t, :], ident[:, :])
                            ins.then_inc(psum_full[1], 1)
                    else:
                        wait_read(pe, ("moe", "T", g), e)
                        if g == 0:
                            pe.wait_ge(x_added, tl.after("x_added", ("scatter", 1), e))
                        for j in range(4):
                            hi, lo = wait_chunk(("moe", "D", g, j), e)
                            for half in range(2):
                                w = slice(512 * half, 512 * (half + 1))
                                ins = three(ps[2][:, w], hi[:, w], lo[:, w], actm_hi[g % 2][:, j, :],
                                            actm_lo[g % 2][:, j, :], g == 0 and j == 0, g == GROUPS - 1 and j == 3, False)
                            used(ins)
                        if g + 1 < GROUPS:
                            transposed_act(g + 1)
                        if g + 2 == GROUPS:
                            pe.wait_ge(routed_sem, tl.after("routed", "onehot_next", e))
                            gather()
            scatter(turns, in_halves=True)


INPUTS = ["x", "mem", "positions", "g_mix", "w_in", "g_q_lat", "w_uq", "g_kv_lat", "w_ukv", "sink", "w_mem_kv",
          "w_branch", "w_out", "g_ffn", "w_gate_dense", "w_up_dense", "w_down_dense", "w_router", "w_gate_exp",
          "w_up_exp", "w_down_exp", "g_mem", "g_final"]


def kernel(**inputs):
    import numpy as np
    import concourse.bacc as bacc
    from concourse.bass_utils import run_bass_kernel_spmd

    nc = bacc.Bacc("TRN2", target_bir_lowering=False, num_devices=1)
    arrays, args = {}, {}
    freqs = []
    for dim in (A_DIM, B_ROPE):
        exponent = -np.arange(dim // 2, dtype=np.float32) * np.float32(2.0 / dim)
        freqs.append(np.power(np.float64(THETA), exponent.astype(np.float64)).astype(np.float32))
    arrays["inv_freq"] = np.concatenate(freqs)
    for name in INPUTS:
        arrays["in_" + name] = np.ascontiguousarray(inputs[name])
    for name, a in arrays.items():
        args[name] = nc.dram_tensor(name, a.shape, mybir.dt.from_np(a.dtype), kind="ExternalInput").ap()
    out = nc.dram_tensor("out", (1, TOK, D), F32, kind="ExternalOutput").ap()
    trunk_kernel(nc, {n: args["in_" + n] for n in INPUTS}, args["inv_freq"], out)
    r = run_bass_kernel_spmd(nc, [arrays], core_ids=[0])
    return r.results[0]["out"]
```
